# Optimizing a Trainium2 kernel written in Bass

```python
import jax, jax.numpy as jnp
from jax import lax
import numpy as np

D_MODEL = 2048
BATCH = 1
SEQ = 256
DEPTH = 2

CHUNK = 64
N_EVEN = (DEPTH + 1) // 2
N_ODD = DEPTH // 2

POOL_WIDTH = D_MODEL // 2
POOL_WINDOWS = (2, 4, 8, 16)
POOL_GROUP = POOL_WIDTH // len(POOL_WINDOWS)
GLA_HEADS = 4
GLA_DV = (D_MODEL // 2) // GLA_HEADS
GLA_DK = GLA_DV // 2
GLA_GATE_RANK = 16
GLA_TAU = 16.0
OFF_Q = POOL_WIDTH
OFF_K = OFF_Q + GLA_HEADS * GLA_DK
OFF_V = OFF_K + GLA_HEADS * GLA_DK
OFF_R = OFF_V + GLA_HEADS * GLA_DV
OFF_LR = OFF_R + GLA_HEADS * GLA_DV
P_AB = OFF_LR + GLA_GATE_RANK
MIX_AB = POOL_WIDTH + GLA_HEADS * GLA_DV
ATT_HEADS = 16
ATT_HEAD_DIM = D_MODEL // ATT_HEADS
ATT_PAST_CHUNKS = 8
REL_CLIP = 256
FFN_DIM = 5504
CONV_WIDTH = 3
ALPHA = (2.0 * DEPTH) ** 0.25
BETA = (8.0 * DEPTH) ** -0.25
LN_EPS = 1e-5

kernel_name = "hybrid_pool_gla_chunkattn_deepnorm_adaln"

def layer_norm(x, g, b):
    xf = x.astype(jnp.float32)
    mu = jnp.mean(xf, axis=-1, keepdims=True)
    var = jnp.mean(jnp.square(xf - mu), axis=-1, keepdims=True)
    return ((xf - mu) * lax.rsqrt(var + LN_EPS)).astype(x.dtype) * g + b

def multiscale_pool(u, w_pool, pool_scale):
    S_ = u.shape[1]
    uf = u.astype(jnp.float32)
    cs = jnp.cumsum(uf, axis=1)
    t = jnp.arange(1, S_ + 1, dtype=jnp.float32)
    outs = []
    for gi, w in enumerate(POOL_WINDOWS):
        sl = slice(gi * POOL_GROUP, (gi + 1) * POOL_GROUP)
        cs_g = cs[:, :, sl]
        lagged = jnp.pad(cs_g[:, :S_ - w, :], ((0, 0), (w, 0), (0, 0)))
        count = jnp.minimum(t, float(w))[None, :, None]
        d = (cs_g - lagged) / count - uf[:, :, sl]
        outs.append(jnp.einsum('bsc,cd->bsd', d.astype(u.dtype), w_pool[gi]))
    return jnp.concatenate(outs, axis=-1) * pool_scale

def gla_chunked(q, k, v, log_a):
    B_, S_, H, DK = q.shape
    DV = v.shape[-1]
    nc = S_ // CHUNK

    def blocks(t):
        return t.astype(jnp.float32).reshape(B_, nc, CHUNK, H, t.shape[-1]).transpose(1, 0, 3, 2, 4)

    qb = blocks(q) * (DK ** -0.5)
    kb, vb, gb = blocks(k), blocks(v), blocks(log_a)
    b = jnp.cumsum(gb, axis=3)
    b_last = b[:, :, :, -1:, :]
    q_dec = qb * jnp.exp(b)
    k_inv = kb * jnp.exp(-b)
    k_dec = kb * jnp.exp(b_last - b)
    causal = jnp.tril(jnp.ones((CHUNK, CHUNK), dtype=bool))
    scores = jnp.where(causal, jnp.einsum('nbhid,nbhjd->nbhij', q_dec, k_inv), 0.0)
    o_intra = jnp.einsum('nbhij,nbhjv->nbhiv', scores, vb)
    decay = jnp.exp(b_last)

    def step(state, inp):
        q_n, k_n, v_n, decay_n = inp
        o_inter = jnp.einsum('bhid,bhdv->bhiv', q_n, state)
        state = decay_n[:, :, 0, :, None] * state + jnp.einsum('bhjd,bhjv->bhdv', k_n, v_n)
        return state, o_inter

    state0 = jnp.zeros((B_, H, DK, DV), jnp.float32)
    _, o_inter = lax.scan(step, state0, (q_dec, k_dec, vb, decay))
    o = o_intra + o_inter
    return o.transpose(1, 0, 3, 2, 4).reshape(B_, S_, H, DV)

def even_mixer(u, w_in, w_gate_lr, b_gate, gla_norm_g, w_pool, pool_scale, w_out):
    B_, S_, _ = u.shape
    z = u @ w_in
    q = z[..., OFF_Q:OFF_K].reshape(B_, S_, GLA_HEADS, GLA_DK)
    k = z[..., OFF_K:OFF_V].reshape(B_, S_, GLA_HEADS, GLA_DK)
    v = z[..., OFF_V:OFF_R].reshape(B_, S_, GLA_HEADS, GLA_DV)
    r = z[..., OFF_R:OFF_LR]
    gate_pre = z[..., OFF_LR:] @ w_gate_lr + b_gate
    log_a = (jax.nn.log_sigmoid(gate_pre.astype(jnp.float32)) / GLA_TAU).reshape(B_, S_, GLA_HEADS, GLA_DK)
    o = gla_chunked(q, k, v, log_a)
    mu = jnp.mean(o, axis=-1, keepdims=True)
    var = jnp.mean(jnp.square(o - mu), axis=-1, keepdims=True)
    o = ((o - mu) * lax.rsqrt(var + LN_EPS)).reshape(B_, S_, GLA_HEADS * GLA_DV).astype(u.dtype)
    y_b = jax.nn.silu(r) * (o * gla_norm_g)
    y_a = multiscale_pool(z[..., :POOL_WIDTH], w_pool, pool_scale)
    return jnp.concatenate([y_a, y_b], axis=-1) @ w_out

def chunk_band_attention(q, k, v, rel_bias):
    B_, S_, H, dh = q.shape
    nc = S_ // CHUNK
    pad = ATT_PAST_CHUNKS * CHUNK
    band = pad + CHUNK
    kp = jnp.pad(k, ((0, 0), (pad, 0), (0, 0), (0, 0)))
    vp = jnp.pad(v, ((0, 0), (pad, 0), (0, 0), (0, 0)))
    qi = jnp.arange(CHUNK)[:, None]
    kj = jnp.arange(band)[None, :]
    rel = jnp.clip(pad + qi - kj, -REL_CLIP, REL_CLIP) + REL_CLIP
    bias = rel_bias[:, rel].astype(jnp.float32)
    scale = dh ** -0.5

    def one_chunk(n):
        start = n * CHUNK
        q_n = lax.dynamic_slice_in_dim(q, start, CHUNK, axis=1)
        k_n = lax.dynamic_slice_in_dim(kp, start, band, axis=1)
        v_n = lax.dynamic_slice_in_dim(vp, start, band, axis=1)
        s = jnp.einsum('blhd,bjhd->bhlj', q_n, k_n).astype(jnp.float32) * scale + bias
        s = jnp.where(kj >= pad - start, s, -1e30)
        p = jax.nn.softmax(s, axis=-1).astype(v.dtype)
        return jnp.einsum('bhlj,bjhd->blhd', p, v_n)

    out = lax.map(one_chunk, jnp.arange(nc))
    return out.transpose(1, 0, 2, 3, 4).reshape(B_, S_, H * dh)

def odd_mixer(u, w_qkv, rel_bias, w_o):
    B_, S_, _ = u.shape
    qkv = (u @ w_qkv).reshape(B_, S_, 3, ATT_HEADS, ATT_HEAD_DIM)
    attn = chunk_band_attention(qkv[:, :, 0], qkv[:, :, 1], qkv[:, :, 2], rel_bias)
    return attn @ w_o

def conv_ffn(u, w_up, conv_w, conv_b, w_down):
    S_ = u.shape[1]
    h = u @ w_up
    a, g = h[..., :FFN_DIM], h[..., FFN_DIM:]
    gp = jnp.pad(g, ((0, 0), (CONV_WIDTH - 1, 0), (0, 0)))
    gc = conv_b
    for i in range(CONV_WIDTH):
        gc = gc + gp[:, i:i + S_, :] * conv_w[i]
    return (jax.nn.gelu(gc) * a) @ w_down

def setup_inputs(seed: int = 0) -> dict:
    key = jax.random.key(seed)
    ks = jax.random.split(key, 20)
    D = D_MODEL

    def nrm(k, shape, scale):
        return jax.random.normal(k, shape, jnp.float32) * scale

    return {
        "x": nrm(ks[0], (BATCH, SEQ, D), 1.0),
        "c": nrm(ks[1], (BATCH, D), 1.0),
        "w_ada": nrm(ks[2], (DEPTH, D, 6 * D), 0.2 * D ** -0.5),
        "b_ada": nrm(ks[3], (DEPTH, 6 * D), 0.01),
        "ln_g": 1.0 + nrm(ks[4], (DEPTH, 2, D), 0.02),
        "ln_b": nrm(ks[5], (DEPTH, 2, D), 0.02),
        "w_in_ab": nrm(ks[6], (N_EVEN, D, P_AB), D ** -0.5),
        "w_gate_lr": nrm(ks[7], (N_EVEN, GLA_GATE_RANK, GLA_HEADS * GLA_DK), GLA_GATE_RANK ** -0.5),
        "b_gate": nrm(ks[8], (N_EVEN, GLA_HEADS * GLA_DK), 0.1),
        "gla_norm_g": 1.0 + nrm(ks[9], (N_EVEN, GLA_HEADS * GLA_DV), 0.02),
        "w_pool": nrm(ks[10], (N_EVEN, len(POOL_WINDOWS), POOL_GROUP, POOL_GROUP), POOL_GROUP ** -0.5),
        "pool_scale": 1.0 + nrm(ks[11], (N_EVEN, POOL_WIDTH), 0.02),
        "w_out_ab": nrm(ks[12], (N_EVEN, MIX_AB, D), BETA * MIX_AB ** -0.5),
        "w_qkv": nrm(ks[13], (N_ODD, D, 3 * D), D ** -0.5),
        "rel_bias": nrm(ks[14], (N_ODD, ATT_HEADS, 2 * REL_CLIP + 1), 0.5),
        "w_o": nrm(ks[15], (N_ODD, D, D), BETA * D ** -0.5),
        "w_up": nrm(ks[16], (DEPTH, D, 2 * FFN_DIM), D ** -0.5),
        "conv_w": nrm(ks[17], (DEPTH, CONV_WIDTH, FFN_DIM), CONV_WIDTH ** -0.5),
        "conv_b": nrm(ks[18], (DEPTH, FFN_DIM), 0.02),
        "w_down": nrm(ks[19], (DEPTH, FFN_DIM, D), BETA * FFN_DIM ** -0.5),
    }

def reference(x, c, w_ada, b_ada, ln_g, ln_b, w_in_ab, w_gate_lr, b_gate, gla_norm_g, w_pool,
              pool_scale, w_out_ab, w_qkv, rel_bias, w_o, w_up, conv_w, conv_b, w_down):
    cond = jax.nn.silu(c)
    for l in range(DEPTH):
        mod = (cond @ w_ada[l] + b_ada[l])[:, None, :]
        sh1, sc1, g1, sh2, sc2, g2 = jnp.split(mod, 6, axis=-1)
        u = x * (1.0 + sc1) + sh1
        if l % 2 == 0:
            e = l // 2
            y = even_mixer(u, w_in_ab[e], w_gate_lr[e], b_gate[e], gla_norm_g[e],
                           w_pool[e], pool_scale[e], w_out_ab[e])
        else:
            o = l // 2
            y = odd_mixer(u, w_qkv[o], rel_bias[o], w_o[o])
        x = layer_norm(ALPHA * x + (1.0 + g1) * y, ln_g[l, 0], ln_b[l, 0])
        u = x * (1.0 + sc2) + sh2
        y = conv_ffn(u, w_up[l], conv_w[l], conv_b[l], w_down[l])
        x = layer_norm(ALPHA * x + (1.0 + g2) * y, ln_g[l, 1], ln_b[l, 1])
    return x


_drawn_inputs = setup_inputs


def setup_inputs(seed=0):
    import zlib

    import numpy as np

    out = dict(_drawn_inputs(seed))
    spreads = {}
    factors = {'b_ada': 5.477,
     'w_gate_lr': 3.425,
     'b_gate': 8.0,
     'gla_norm_g': 8.0,
     'pool_scale': 8.0,
     'conv_b': 8.0}
    for name, (base, spread) in spreads.items():
        noise = np.random.default_rng([zlib.crc32(name.encode()), seed]).standard_normal(out[name].shape)
        drawn = base * np.exp(spread * noise) if base else spread * noise
        out[name] = __import__('jax').numpy.asarray(drawn.astype(out[name].dtype))
    for name, factor in factors.items():
        out[name] = (out[name] * factor).astype(out[name].dtype)
    return out
```

```python
import concourse.bass as bass
from concourse import mybir
from contextlib import ExitStack

D = 2048
S = 256
P = 128
F = 5504
KT = D // P
NT = S // P
NCOL = 512
UNIT = 2048
CH = 64
POOL_W = D // 2
WINDOWS = (2, 4, 8, 16)
PG = POOL_W // len(WINDOWS)
GH, GDV, GDK, GRANK, GTAU = 4, 256, 128, 16, 16.0
OFF_Q = POOL_W
OFF_K = OFF_Q + GH * GDK
OFF_V = OFF_K + GH * GDK
OFF_R = OFF_V + GH * GDV
OFF_LR = OFF_R + GH * GDV
AH, AD = 16, 128
REL = 256
DEPTH = 2
ALPHA = (2.0 * DEPTH) ** 0.25
EPS = 1e-5
FT = F // P
FT_A = 20
FT_B = FT - FT_A
NEG = -1e30
RAW_SLOTS, HL_SLOTS, ADA_SLOTS = 4, 2, 4
ADA_HALVES = KT // 2
CONST_COLS = 7 * P
BAND = 3 * P


def plan():
    four = (4, 4, 4, 4)
    phases = []
    for layer in range(DEPTH):
        if layer % 2 == 0:
            phases += [(layer, "in", 8, four, 8), (layer, "out", 4, four, 4)]
        else:
            phases += [(layer, "qkv", 12, four, 12), (layer, "o", 4, four, 0)]
        last = layer == DEPTH - 1
        phases += [(layer, "up_a", FT_A // 2, four, 4),
                   (layer, "down_a", 4, (4, 4, 4, 4, 2, 2), 0 if last else 4),
                   (layer, "up_b", FT_B // 2 + 1, four, 0),
                   (layer, "down_b", 4, (4, 4, 4, 4, 4, 3), 0 if last else 4)]
    out, unit, chunk, block = {}, 0, 0, 8
    for layer, name, chunks, kts, blocks in phases:
        out[layer, name] = dict(chunks=chunks, kts=kts, n=len(kts), unit=unit, chunk=chunk, block=block,
                                blocks=blocks)
        unit += chunks * len(kts) - (2 if name == "up_b" else 0)
        chunk += chunks
        block += blocks
    return out


def build(nc, A, out):
    f32, f32r, i32 = mybir.dt.float32, mybir.dt.float32r, mybir.dt.int32
    ALU = mybir.AluOpType
    ACT = mybir.ActivationFunctionType
    AX = mybir.AxisListType
    PH = plan()

    ctx = ExitStack()
    with ctx:
        used = [2048]

        def region(size):
            at = used[0]
            used[0] += (size + 31) // 32 * 32
            return at

        def place(name, shape, at, dt=f32):
            return nc.alloc_sbuf_tensor_at(name, shape, dt, offset=at)

        raw = place("w_raw", [P, RAW_SLOTS, UNIT], region(RAW_SLOTS * UNIT * 4))
        whi = place("w_hi", [P, HL_SLOTS, UNIT], region(HL_SLOTS * UNIT * 4), f32r)
        wlo = place("w_lo", [P, HL_SLOTS, UNIT], region(HL_SLOTS * UNIT * 4), f32r)
        ada_w = place("ada_w", [P, ADA_SLOTS, 2, NCOL], region(ADA_SLOTS * 2 * NCOL * 4))
        ada_acc = place("ada_acc", [P, NCOL], region(NCOL * 4))
        gate = place("gate", [P, D], region(D * 4))
        r_u = region(2 * KT * S * 4)
        uhi = place("u_hi", [P, KT, S], r_u, f32r)
        ulo = place("u_lo", [P, KT, S], r_u + KT * S * 4, f32r)
        x = place("x_tok", [P, NT, D], region(NT * D * 4))
        r_w = region(48 * 1024)
        r_aux = region(16 * 1024)
        r_s = region(12 * 1024)
        consts = place("consts", [P, CONST_COLS], region(CONST_COLS * 4))
        n_cols = 2 * 96 + DEPTH * 4 * FT + 8 + 8 + KT
        cols = place("cols", [P, n_cols], region(n_cols * 4))
        mod = place("mod", [P, DEPTH * 96], region(DEPTH * 96 * 4))
        silu_c = place("silu_c", [P, KT], region(KT * 4))
        small = place("small", [P, 192], region(192 * 4))
        assert used[0] <= 229368, used[0]

        xT = place("x_T", [P, KT, S], r_w)
        rows = place("rows", [P, 13, P], r_w + 32 * 1024)
        z = place("z", [P, NT, OFF_LR], r_w)
        kdec = place("k_dec", [P, NT, GH * GDK], r_w + 32768)
        loga = place("log_a", [P, NT, GH * GDK], r_w + 32768 + 4096)
        qdT = place("q_dec_T", [P, GH, S], r_w + 32768 + 8192)
        kiT = place("k_inv_T", [P, GH, S], r_w + 32768 + 12288)
        hhi = place("hid_hi", [P, FT_B, S], r_w, f32r)
        hlo = place("hid_lo", [P, FT_B, S], r_w + FT_B * S * 4, f32r)
        qkv = place("qkv", [P, NT, 3 * D], r_w)
        state = place("gla_state", [P, 2, GH, GDV], r_u + 8 * S * 4)
        state3 = place("gla_state3", [P, GH, GDV], r_u + KT * S * 4 + 8 * S * 4)
        scT = place("scores_T", [P, NT, GH, P], r_u + KT * S * 4 + 8 * S * 4 + 4096)
        band = place("band", [P, 4, BAND], r_aux)
        w_pool = place("w_pool_sb", [P, 4, 2, PG], r_aux + 4 * BAND * 4)
        toep = place("toeplitz", [P, AH, S], r_aux)
        lnp = place("ln_params", [P, 2, D], r_aux)
        g_tok = place("h_tok", [P, NT, NCOL], r_s)
        gc = place("conv", [P, 2, S], r_s + 4096)
        h32 = place("h_f32", [P, 2, S], r_s + 6144)
        y_tmp = place("y_gated", [P, NT, NCOL], r_s + 8192)
        u32 = place("u_f32", [P, 2, 2 * S], r_s)
        w_lr = place("w_lr", [P, KT, GRANK], r_w + 40960)
        w_lrh = place("w_lr_hi", [P, KT, GRANK], r_w + 40960 + 1024, f32r)
        w_lrl = place("w_lr_lo", [P, KT, GRANK], r_w + 40960 + 2048, f32r)
        lr = place("lr", [P, NT, GRANK], r_aux + 14336)
        lrT = place("lr_T", [GRANK, S], r_aux + 14336 + 128)
        w_g = place("w_gate", [GRANK, GH * GDK], r_s + 8192)
        b_g = place("b_gate", [P, GH * GDK], r_s + 10240)
        dT = place("pool_T", [P, 2, 2, S], r_s + 4096)
        qkT = place("qk_T", [P, 2, 2 * S], r_s)
        prob = place("prob", [P, 2, 3 * P], r_s + 4096)
        probT = place("prob_T", [P, 2, 3 * P], r_s + 7168)

        def cst(i):
            return consts[:, i * P:(i + 1) * P]

        ident, rev, sum_inc, sum_suf, ones = (cst(i) for i in range(5))
        mask_q, mask_k = consts[0:1, 5 * P:6 * P], consts[0:1, 6 * P:7 * P]
        C_CONV = 2 * 96
        C_POOL = C_CONV + DEPTH * 4 * FT
        C_NORM = C_POOL + 8
        C_C = C_NORM + 8
        bn = small[:, 0:48].rearrange("p (t c s) -> p t c s", t=2, c=4)
        mv = small[:, 48:52].rearrange("p (t s) -> p t s", t=2)
        var, sd, rs, t1 = (small[:, 52 + 2 * i:54 + 2 * i] for i in range(4))
        gbn = small[:, 64:112].rearrange("p (h s) -> p h s", h=8)
        gmv = small[:, 112:128].rearrange("p (h s) -> p h s", h=8)
        gvar, gsd, grs, gt = (small[:, 128 + 8 * i:136 + 8 * i] for i in range(4))
        decay = small[:, 160:176].rearrange("p (h c) -> p h c", h=4)
        nmax = small[:, 176:180].rearrange("p (b t) -> p b t", b=2)
        rsum = small[:, 180:184].rearrange("p (b t) -> p b t", b=2)
        rinv = small[:, 184:188].rearrange("p (b t) -> p b t", b=2)

        bank = [ctx.enter_context(nc.psum_tensor(f"bank{i}", [P, NCOL], f32)) for i in range(8)]
        T = bank[4:6]
        ada_p = bank[6]

        sems = {}

        def sem(name):
            if name not in sems:
                sems[name] = ctx.enter_context(nc.semaphore(name))
            return sems[name]

        w_loaded = [sem(f"w_loaded{i}") for i in range(RAW_SLOTS)]
        w_hi = sem("w_hi_done")
        w_lo = sem("w_lo_done")
        w_used = sem("w_used")
        acc_free = sem("acc_free")
        a_loaded = [sem(f"ada_loaded{i}") for i in range(ADA_SLOTS)]
        a_step = sem("ada_step")
        a_sum = sem("ada_summed")
        a_out = sem("ada_out")
        A0 = 2 * ADA_SLOTS

        t_full = sem("t_full")
        t_free = sem("t_free")
        u32_done = sem("u32_done")
        u_hi_done = sem("u_hi_done")
        u_ready = sem("u_ready")
        U_FIRST, U_MIX, U_LN, U_ATT = 0, 8, {0: 16, 1: 24, 2: 48}, 32
        T_X, T_MIX, T_LN = 0, 8, {0: 16, 1: 24, 2: 32}
        h_T = sem("hid_T")
        h_bias = sem("hid_bias")
        h_tap = sem("hid_tap")
        h_conv = sem("hid_conv")
        h_gelu = sem("hid_gelu")
        h_mul = sem("hid_mul")
        h_hi = sem("hid_hi_done")
        h_lo = sem("hid_lo_done")
        y_gated = sem("y_gated")
        y_sum = sem("y_sum")
        y_done = sem("y_done")

        H0 = {"up_a": 0, "up_b": FT_A // 2}
        H_LAYER = FT_A // 2 + FT_B // 2 + 1
        Y0 = {(0, "out"): 0, (0, "down_a"): 4, (0, "down_b"): 8, (1, "o"): 12, (1, "down_a"): 16,
              (1, "down_b"): 20}
        ADA = {(0, "in", 0): (0, 2), (0, "in", 4): (0, 3), (0, "out", 0): (0, 4), (0, "up_a", 1): (0, 5),
               (0, "down_a", 0): (1, 0), (0, "down_b", 0): (1, 1), (1, "qkv", 0): (1, 3),
               (1, "qkv", 4): (1, 4), (1, "qkv", 8): (1, 2), (1, "up_a", 1): (1, 5)}
        GATE_NO = {(0, 2): 1, (0, 5): 2, (1, 2): 3, (1, 5): 4}
        ROW_SRC = 13

        block = ctx.enter_context(nc.Block())

        def pairs(e, lo, hi, body):
            n = (hi - lo) // 2
            assert 2 * n == hi - lo
            if n == 1:
                body(lo, 0)
                body(lo + 1, 0)
            elif n:
                with e.Fori(0, n) as i:
                    body(lo, i)
                    body(lo + 1, i)

        def ada_of(key, lo, c0, i):
            src = ADA.get((*key, lo))
            if src is None or (key[1] == "up_a" and (c0 - lo) % 2):
                return None
            if key[1] == "up_a":
                return (*src, i, PH[key]["block"] + i)
            return (*src, 2 * i + (c0 - lo), PH[key]["block"] + c0 + 2 * i)

        def unit_no(ph, c0, i, j):
            u = ph["unit"] + c0 * ph["n"] + j
            return u, u + 2 * ph["n"] * i

        @block.sync
        def _(sp):
            def load_unit(ph, c0, i, j, halves):
                u, un = unit_no(ph, c0, i, j)
                sp.wait_ge(w_lo, un + 1)
                for dst, src in halves(raw[:, u % RAW_SLOTS, :]):
                    sp.dma_start(dst, src).then_inc(w_loaded[u % RAW_SLOTS], 16)

            def load_half(blk, half):
                layer, part, n, m = blk
                sp.wait_ge(a_step, m * KT + 2 * half + 2)
                w = A["w_ada"][layer].rearrange("(k p) (s n c) -> p k s n c", p=P, s=6, n=4)
                sp.dma_start(ada_w[:, half % ADA_SLOTS], w[:, 2 * half:2 * half + 2, part, n, :]
                             ).then_inc(a_loaded[half % ADA_SLOTS], 16)

            def phase(key, lo, hi):
                layer, name = key
                ph = PH[key]
                first = [sum(ph["kts"][:j]) for j in range(ph["n"])]
                base = {"down_b": FT_A}.get(name, 0)
                if name in ("up_a", "up_b"):
                    f0 = 0 if name == "up_a" else FT_A * P
                    f1 = f0 + (FT_A if name == "up_a" else FT_B - 1) * P
                    w = A["w_up"][layer].rearrange("(k p) (s f) -> p k s f", p=P, s=2)
                    w = w[:, :, :, f0:f1].rearrange("p k s (c f) -> p k s c f", f=2 * P)
                else:
                    w = {"in": lambda: A["w_in_ab"][0][:, 0:OFF_LR], "out": lambda: A["w_out_ab"][0],
                         "qkv": lambda: A["w_qkv"][0], "o": lambda: A["w_o"][0],
                         "down_a": lambda: A["w_down"][layer], "down_b": lambda: A["w_down"][layer]}[name]()
                    w = w.rearrange("(k p) (c n) -> p k c n", p=P, n=NCOL)
                after = {4: (0, 2, 4, 8), 6: (0, 2, 3, 5, 6, 8)}[ph["n"]]

                def body(c0, i):
                    blk, c = ada_of(key, lo, c0, i), 2 * i + c0
                    for j in range(ph["n"]):
                        k = ph["kts"][j]
                        if name in ("up_a", "up_b"):
                            load_unit(ph, c0, i, j, lambda r: [
                                (r.rearrange("p (k s f) -> p k s f", k=k, s=2)[:, :, s, :],
                                 w[:, 4 * j:4 * j + 4, s, c, :]) for s in range(2)])
                        else:
                            k0, cut = base + first[j], (k + 1) // 2
                            load_unit(ph, c0, i, j, lambda r: [
                                (r[:, a * NCOL:b * NCOL].rearrange("p (k n) -> p k n", n=NCOL),
                                 w[:, k0 + a:k0 + b, c, :]) for a, b in ((0, cut), (cut, k))])
                        if blk and j:
                            for half in range(after[j - 1], after[j]):
                                load_half(blk, half)
                if hi - lo == 1:
                    body(lo, 0)
                else:
                    pairs(sp, lo, hi, body)

            def gate_load(layer, part, uses):
                if uses:
                    sp.wait_ge(y_done, uses)
                sp.dma_start(gate[:, :], A["b_ada"][layer:layer + 1, part * D:(part + 1) * D].broadcast_to((P, D))
                             ).then_inc(sem("gate_in"), 16)

            def ln_load(s):
                layer, which = divmod(s, 2)
                if s:
                    sp.wait_ge(sem("ln_done"), s)
                for k, name in enumerate(("ln_g", "ln_b")):
                    sp.dma_start(lnp[:, k, :], A[name][layer, which:which + 1, :].broadcast_to((P, D))
                                 ).then_inc(sem("ln_in"), 16)

            def mlp(layer, uses):
                phase((layer, "up_a"), 0, 1)
                gate_load(layer, 5, uses)
                phase((layer, "up_a"), 1, 9)
                phase((layer, "up_a"), 9, 10)
                phase((layer, "down_a"), 0, 4)
                phase((layer, "up_b"), 0, 1)
                phase((layer, "up_b"), 1, 11)
                w = A["w_up"][layer].rearrange("(k p) (s f) -> p k s f", p=P, s=2)[:, :, :, F - P:F]
                for j in range(2):
                    load_unit(PH[layer, "up_b"], 11, 0, j, lambda r: [
                        (r.rearrange("p (k s f) -> p k s f", k=8, s=2)[:, :, s, :], w[:, 8 * j:8 * j + 8, s, :])
                        for s in range(2)])
                phase((layer, "down_b"), 0, 4)

            sp.dma_start(consts[:, :], A["consts"]).then_inc(sem("const_in"), 16)
            row_list = [A["b_ada"][l] for l in range(DEPTH)]
            for l in range(DEPTH):
                row_list += [A["conv_w"][l, i] for i in range(3)] + [A["conv_b"][l]]
            row_list += [A["pool_scale"][0], A["gla_norm_g"][0], A["c"][0]]
            for i, src in enumerate(row_list):
                sp.dma_start(rows[0:src.shape[0] // P, i, :], src.rearrange("(r c) -> r c", c=P)
                             ).then_inc(sem("rows_in"), 16)
            sp.dma_start(x[:, :, :], A["x"][0].rearrange("(t p) n -> p t n", p=P)).then_inc(sem("x_in"), 16)
            for part in (0, 1):
                with sp.Fori(0, 4) as n:
                    for half in range(ADA_HALVES):
                        load_half((0, part, n, n + 4 * part), half)
            phase((0, "in"), 0, 4) if False else None
            gate_load(0, 2, 0)
            phase((0, "in"), 0, 4)
            sp.dma_start(w_lr[:, :, :], A["w_in_ab"][0][:, OFF_LR:OFF_LR + GRANK].rearrange("(k p) n -> p k n", p=P)
                         ).then_inc(sem("lr_in"), 16)
            sp.dma_start(w_g[:, :], A["w_gate_lr"][0]).then_inc(sem("gla_in"), 16)
            sp.dma_start(b_g[:, :], A["b_gate"][0:1, :].broadcast_to((P, GH * GDK))).then_inc(sem("gla_in"), 16)
            sp.dma_start(band[:, :, :], A["band"]).then_inc(sem("pool_in"), 16)
            for g in range(4):
                sp.dma_start(w_pool[:, g], A["w_pool"][0, g].rearrange("(k p) n -> p k n", p=P)
                             ).then_inc(sem("pool_in"), 16)
            phase((0, "in"), 4, 8)
            phase((0, "out"), 0, 4)
            ln_load(0)
            mlp(0, 4)
            ln_load(1)
            phase((1, "qkv"), 0, 4)
            sp.wait_ge(sem("ln_done"), 2)
            rb = A["rel_bias"]
            sp.dma_start(toep[:, :, :], bass.AP(rb.tensor, REL - 127, [[1, P], [2 * REL + 1, AH], [1, S]])
                         ).then_inc(sem("toep_in"), 16)
            phase((1, "qkv"), 4, 8)
            gate_load(1, 2, 12)
            phase((1, "qkv"), 8, 12)
            phase((1, "o"), 0, 4)
            sp.wait_ge(sem("att_s"), AH)
            ln_load(2)
            mlp(1, 16)
            ln_load(3)
            out_v = out[0].rearrange("(t p) n -> p t n", p=P)
            for n in range(4):
                sp.wait_ge(sem("ln_chunk"), 13 + n)
                sp.dma_start(out_v[:, :, n * NCOL:(n + 1) * NCOL], x[:, :, n * NCOL:(n + 1) * NCOL]
                             ).then_inc(sem("out_done"), 16)
            sp.wait_ge(sem("out_done"), 4 * 16)

        @block.scalar
        def _(act):
            def hi_unit(ph, c0, i, j, width):
                u, un = unit_no(ph, c0, i, j)
                act.wait_ge(w_loaded[u % RAW_SLOTS], 32 * (u // RAW_SLOTS + 1) + 16 * ph["n"] * i)
                if u >= HL_SLOTS:
                    act.wait_ge(w_used, un - 1)
                nc.scalar.activation(whi[:, u % HL_SLOTS, 0:width], raw[:, u % RAW_SLOTS, 0:width], ACT.Copy
                                     ).then_inc(w_hi, 1)

            def steps(key, lo, hi, mid=None, tail=None, more=True):
                ph = PH[key]

                def body(c0, i):
                    own = 2 if key[1] == "up_b" and c0 == 11 else ph["n"]
                    for j in range(2, own + 2):
                        if j >= own and not more and c0 == hi - 1:
                            continue
                        width = ph["kts"][j] * NCOL if j < own else UNIT
                        hi_unit(ph, c0, i, j, width)
                        if j == 2 and mid:
                            mid(c0, i)
                    if tail:
                        tail(c0, i)
                if hi - lo == 1 or not more:
                    for c in range(lo, hi):
                        body(c, 0)
                else:
                    pairs(act, lo, hi, body)

            def chunk_end(key, c0, i):
                ph = PH[key]
                own = 2 if key[1] == "up_b" and c0 == 11 else ph["n"]
                act.wait_ge(w_used, unit_no(ph, c0, i, own)[1])

            def copy_out(dst, key):
                def tail(c0, i):
                    chunk_end(key, c0, i)
                    for t in range(NT):
                        ins = nc.scalar.activation(dst(t, c0, i), bank[2 * (c0 % 2) + t][:, :], ACT.Copy)
                    ins.then_inc(acc_free, 1)
                return tail

            def piece(g, t, src, kt, scale=None, bias=None, src_sbuf=False):
                act.wait_ge(u_ready, g + 1)
                slot = t % 2 if isinstance(t, int) else 0
                for k in range(2):
                    ins = nc.scalar.activation(u32[:, slot, k * S:(k + 1) * S], src(k), ACT.Identity,
                                               scale=scale(k), bias=bias(k) if bias else 0.0)
                ins.then_inc(u32_done, 1)
                act.wait_ge(u32_done, g + 1)
                if not src_sbuf:
                    pass
                nc.scalar.activation(uhi[:, kt:kt + 2, :], u32[:, slot, :].rearrange("p (k s) -> p k s", k=2),
                                     ACT.Copy).then_inc(u_hi_done, 1)

            act.wait_ge(sem("cols_in"), 2)
            nc.scalar.activation(silu_c[:, :], cols[:, C_C:C_C + KT], ACT.Silu).then_inc(sem("silu_c"), 1)
            for v in range(8):
                act.wait_ge(t_full, T_X + v + 1)
                nc.scalar.activation(xT[:, 2 * v:2 * v + 2, :], T[v % 2].rearrange("p (k s) -> p k s", k=2), ACT.Copy
                                     ).then_inc(t_free, 1)
            act.wait_ge(t_free, 2 + T_X + 8)
            with act.Fori(0, 4) as n:
                act.wait_ge(a_out, n + 6)
                for b in range(2):
                    g = 2 * n + b
                    act.wait_ge(u_ready, g + 1)
                    for k in range(2):
                        kt = 4 * n + (2 * b + k)
                        ins = nc.scalar.activation(u32[:, b, k * S:(k + 1) * S], xT[:, kt, :], ACT.Identity,
                                                   scale=mod[:, bass.ds(kt + KT, 1)], bias=mod[:, bass.ds(kt, 1)])
                    ins.then_inc(u32_done, 1)
                    act.wait_ge(u32_done, g + 1)
                    nc.scalar.activation(uhi[:, bass.ds(4 * n + 2 * b, 2), :],
                                         u32[:, b, :].rearrange("p (k s) -> p k s", k=2), ACT.Copy
                                         ).then_inc(u_hi_done, 1)
            hi_unit(PH[0, "in"], 0, 0, 0, UNIT)
            hi_unit(PH[0, "in"], 0, 0, 1, UNIT)

            def z_at(t, c0, i):
                return z[:, t, bass.ds(2 * NCOL * i + c0 * NCOL, NCOL)]
            steps((0, "in"), 0, 4, tail=copy_out(z_at, (0, "in")))
            steps((0, "in"), 4, 8, tail=copy_out(z_at, (0, "in")))

            act.wait_ge(sem("lr_in"), 16)
            nc.scalar.activation(w_lrh[:, :, :], w_lr[:, :, :], ACT.Copy).then_inc(sem("lr_hi"), 1)
            act.wait_ge(acc_free, 2 + 8)
            for t in range(NT):
                nc.scalar.activation(z[:, t, OFF_R:OFF_LR], z[:, t, OFF_R:OFF_LR], ACT.Silu).then_inc(sem("silu_r"), 1)

            def pool_T(g):
                if g >= 2:
                    act.wait_ge(t_full, T_MIX + g - 1)
                act.wait_ge(sem("pool_T"), g + 1)
                nc.scalar.activation(dT[:, g % 2], bank[g].rearrange("p (k s) -> p k s", k=2), ACT.Copy
                                     ).then_inc(sem("pool_T_out"), 1)

            def mix_piece(v, col):
                act.wait_ge(t_full, T_MIX + v + 1)
                act.wait_ge(u_ready, U_MIX + v + 1)
                for k in range(2):
                    ins = nc.scalar.activation(u32[:, v % 2, k * S:(k + 1) * S], T[v % 2][:, k * S:(k + 1) * S],
                                               ACT.Identity, scale=cols[:, col + k:col + k + 1])
                ins.then_inc(t_free, 1)
                act.wait_ge(t_free, 2 + T_MIX + v + 1)
                nc.scalar.activation(uhi[:, 2 * v:2 * v + 2, :], u32[:, v % 2, :].rearrange("p (k s) -> p k s", k=2),
                                     ACT.Copy).then_inc(u_hi_done, 1)
            pool_T(0)
            pool_T(1)
            mix_piece(0, C_POOL)
            mix_piece(1, C_POOL + 2)
            pool_T(2)
            pool_T(3)
            mix_piece(2, C_POOL + 4)
            mix_piece(3, C_POOL + 6)
            act.wait_ge(sem("gate_pre_out"), 1)
            nc.scalar.activation(kdec[:, :, :], loga[:, :, :], ACT.Abs).then_inc(sem("ls"), 1)
            act.wait_ge(sem("ls"), 1)
            nc.scalar.activation(kdec[:, :, :], kdec[:, :, :], ACT.Exp, scale=-1.0).then_inc(sem("ls"), 1)
            act.wait_ge(sem("ls"), 2)
            nc.scalar.activation(kdec[:, :, :], kdec[:, :, :], ACT.Ln, bias=1.0).then_inc(sem("ls"), 1)
            act.wait_ge(sem("qk_T"), 1)
            for j in range(2):
                nc.scalar.activation(qdT[:, 2 * j:2 * j + 2, :], bank[j].rearrange("p (h s) -> p h s", h=2), ACT.Copy,
                                     scale=float(GDK) ** -0.5)
                ins = nc.scalar.activation(kiT[:, 2 * j:2 * j + 2, :], bank[2 + j].rearrange("p (h s) -> p h s", h=2),
                                           ACT.Copy)
            ins.then_inc(sem("qk_T_out"), 1)
            act.wait_ge(sem("cum"), 1)
            for t in range(NT):
                nc.scalar.activation(kdec[:, t, :], bank[t][:, :], ACT.Exp).then_inc(sem("exp_suf"), 1)
            act.wait_ge(sem("exp_suf"), 2)
            for j in range(2):
                nc.scalar.activation(bank[j][:, :], bank[2 + j][:, :], ACT.Exp, scale=-1.0).then_inc(sem("exp_b"), 1)
            act.wait_ge(sem("exp_b"), 2)
            for j in range(2):
                nc.scalar.activation(bank[2 + j][:, :], bank[2 + j][:, :], ACT.Exp).then_inc(sem("exp_b"), 1)
            act.wait_ge(sem("gla_var"), 1)
            nc.scalar.activation(gsd, gvar, ACT.Sqrt).then_inc(sem("gla_sd"), 1)
            for v in range(4, 8):
                mix_piece(v, C_NORM + 2 * (v - 4))
            steps((0, "out"), 0, 4)

            def ln_and_u(s, shift):
                act.wait_ge(sem("ln_var"), s + 1)
                nc.scalar.activation(sd, var, ACT.Sqrt).then_inc(sem("ln_sd"), 1)
                if shift is None:
                    return
                for v in range(8):
                    act.wait_ge(t_full, T_LN[s] + v + 1)
                    act.wait_ge(u_ready, U_LN[s] + v + 1)
                    for k in range(2):
                        m = shift + 2 * v + k
                        ins = nc.scalar.activation(u32[:, v % 2, k * S:(k + 1) * S], T[v % 2][:, k * S:(k + 1) * S],
                                                   ACT.Identity, scale=mod[:, m + KT:m + KT + 1], bias=mod[:, m:m + 1])
                    ins.then_inc(t_free, 1)
                    act.wait_ge(t_free, 2 + T_LN[s] + v + 1)
                    nc.scalar.activation(uhi[:, 2 * v:2 * v + 2, :],
                                         u32[:, v % 2, :].rearrange("p (k s) -> p k s", k=2), ACT.Copy
                                         ).then_inc(u_hi_done, 1)

            def hidden(layer, name, c0, i, nf=2):
                q = H_LAYER * layer + H0[name] + c0 + 2 * i
                f = (0 if name == "up_a" else FT_A) + 2 * c0 + 4 * i
                col = C_CONV + layer * 4 * FT + f
                act.wait_ge(h_T, q + 1)
                for k in range(nf):
                    ins = nc.scalar.activation(gc[:, k, :], T[1][:, k * S:(k + 1) * S], ACT.Identity,
                                               scale=cols[:, bass.ds(col + 2 * FT + k, 1)],
                                               bias=cols[:, bass.ds(col + 3 * FT + k, 1)])
                ins.then_inc(h_bias, 1)
                act.wait_ge(h_conv, q + 1)
                nc.scalar.activation(gc[:, 0:nf, :], gc[:, 0:nf, :], ACT.Gelu_apprx_tanh).then_inc(h_gelu, 1)
                act.wait_ge(h_mul, q + 2)
                nc.scalar.activation(hhi[:, bass.ds(2 * c0 + 4 * i, nf), :], h32[:, 0:nf, :], ACT.Copy
                                     ).then_inc(h_hi, 1)

            def mlp(layer):
                for name in ("up_a", "up_b"):
                    key = (layer, name)
                    last = PH[key]["chunks"] - 1
                    out_h = copy_out(lambda t, c0, i: g_tok[:, t, :], key)
                    prev = lambda c0, i: hidden(layer, name, c0 - 1, i)
                    steps(key, 0, 1, tail=out_h)
                    steps(key, 1, 1 + (last - 1) // 2 * 2, mid=prev, tail=out_h)
                    for c in range(1 + (last - 1) // 2 * 2, last + 1):
                        if name == "up_b" and c == last:
                            hidden(layer, name, c - 1, 0)
                            hi_unit(PH[key], c, 0, 2, UNIT)
                            hi_unit(PH[key], c, 0, 3, UNIT)
                            chunk_end(key, c, 0)
                            for t in range(NT):
                                ins = nc.scalar.activation(g_tok[:, t, 0:2 * P], bank[2 * (c % 2) + t][:, 0:2 * P],
                                                           ACT.Copy)
                            ins.then_inc(acc_free, 1)
                        else:
                            steps(key, c, c + 1, mid=prev, tail=out_h)
                    hidden(layer, name, last, 0, 1 if name == "up_b" else 2)
                    steps((layer, "down" + name[2:]), 0, 4, more=not (layer == DEPTH - 1 and name == "up_b"))

            ln_and_u(0, 3 * KT)
            mlp(0)
            ln_and_u(1, 96)
            steps((1, "qkv"), 0, 12, tail=copy_out(
                lambda t, c0, i: qkv[:, t, bass.ds(2 * NCOL * i + c0 * NCOL, NCOL)], (1, "qkv")))
            for s in range(AH + 3):
                if s < AH:
                    act.wait_ge(sem("att_T"), s + 1)
                    nc.scalar.activation(qkT[:, s % 2, 0:S], T[s % 2][:, 0:S], ACT.Copy, scale=float(AD) ** -0.5)
                    nc.scalar.activation(qkT[:, s % 2, S:2 * S], T[s % 2][:, S:2 * S], ACT.Copy
                                         ).then_inc(sem("att_qk"), 1)
                if 1 <= s <= AH:
                    h = s - 1
                    act.wait_ge(sem("att_max"), h + 1)
                    if h >= 2:
                        act.wait_ge(sem("att_pT"), h - 1)
                    sb = bank[6 + h % 2]
                    nc.scalar.activation(prob[:, h % 2, 0:P], sb[:, 0:P], ACT.Exp, bias=nmax[:, h % 2, 0:1],
                                         accum_out=rsum[:, h % 2, 0:1])
                    nc.scalar.activation(prob[:, h % 2, P:3 * P], sb[:, P:3 * P], ACT.Exp, bias=nmax[:, h % 2, 1:2],
                                         accum_out=rsum[:, h % 2, 1:2]).then_inc(sem("att_exp"), 1)
                if s >= 3:
                    h = s - 3
                    act.wait_ge(sem("att_o"), h + 1)
                    nc.scalar.activation(uhi[:, h, :], bank[2 + h % 2][:, 0:S], ACT.Copy).then_inc(u_hi_done, 1)
            steps((1, "o"), 0, 4)
            ln_and_u(2, 96 + 3 * KT)
            mlp(1)
            ln_and_u(3, None)

        @block.vector
        def _(dve):
            chained = [0]

            def link(ins):
                chained[0] += 1
                ins.then_inc(sem("dve_chain"), 1)
                dve.wait_ge(sem("dve_chain"), chained[0])

            def lo_unit(ph, c0, i, j, width):
                u, un = unit_no(ph, c0, i, j)
                dve.wait_ge(w_hi, un + 1)
                if u >= HL_SLOTS:
                    dve.wait_ge(w_used, un - 1)
                nc.vector.tensor_tensor(wlo[:, u % HL_SLOTS, 0:width], raw[:, u % RAW_SLOTS, 0:width],
                                        whi[:, u % HL_SLOTS, 0:width].bitcast(f32), ALU.subtract).then_inc(w_lo, 1)

            def ada_rows(m, lo, hi):
                for r in range(lo, hi):
                    half = r // 2
                    if r % 2 == 0:
                        dve.wait_ge(a_loaded[half % ADA_SLOTS], 32 * m + 16 * (half // ADA_SLOTS + 1))
                    w = ada_w[:, half % ADA_SLOTS, r % 2, :]
                    if r == 0:
                        nc.vector.tensor_scalar(ada_acc[:, :], w, silu_c[:, 0:1], None, ALU.mult).then_inc(a_step, 1)
                    else:
                        dve.wait_ge(a_step, m * KT + (A0 + r))
                        nc.vector.scalar_tensor_tensor(ada_acc[:, :], w, silu_c[:, r:r + 1], ada_acc[:, :],
                                                       ALU.mult, ALU.add).then_inc(a_step, 1)

            def ada_evac(blk):
                layer, part, n, m = blk
                dve.wait_ge(a_sum, m + 1)
                if part in (2, 5):
                    dve.wait_ge(sem("gate_in"), 16 * GATE_NO[layer, part])
                    to = gate[:, bass.ds(n * NCOL, NCOL)]
                    nc.vector.scalar_tensor_tensor(to, ada_p[:, :], 1.0, to, ALU.add, ALU.add).then_inc(a_out, 1)
                else:
                    at = bass.ds(n * 4 + (96 * layer + KT * part), 4)
                    nc.vector.scalar_tensor_tensor(mod[:, at], ada_p[:, 0:4], 1.0 if part in (1, 4) else 0.0,
                                                   cols[:, at], ALU.add, ALU.add).then_inc(a_out, 1)

            def steps(key, lo, hi, mid=None, tail=None, more=True):
                ph = PH[key]
                split = {4: (4, 4, 4, 4), 6: (3, 3, 3, 3, 2, 2)}[ph["n"]]

                def body(c0, i):
                    blk = ada_of(key, lo, c0, i)
                    own = 2 if key[1] == "up_b" and c0 == 11 else ph["n"]
                    row = 0
                    for j in range(2, own + 2):
                        if blk:
                            ada_rows(blk[3], row, row + split[j - 2])
                            row += split[j - 2]
                        if j >= own and not more and c0 == hi - 1:
                            continue
                        lo_unit(ph, c0, i, j, ph["kts"][j] * NCOL if j < own else UNIT)
                        if j == 2 and mid:
                            mid(c0, i)
                    if tail:
                        tail(c0, i)
                    if blk:
                        ada_evac(blk)
                if hi - lo == 1 or not more:
                    for c in range(lo, hi):
                        body(c, 0)
                else:
                    pairs(dve, lo, hi, body)

            def u_lo(g, dst_kt, slot):
                dve.wait_ge(u_hi_done, g + 1)
                nc.vector.tensor_tensor(ulo[:, dst_kt, :], u32[:, slot, :].rearrange("p (k s) -> p k s", k=2),
                                        uhi[:, dst_kt, :].bitcast(f32), ALU.subtract).then_inc(u_ready, 1)

            def y_out(key, first, stats):
                ph = PH[key]

                def tail(c0, i):
                    y = Y0[key] + c0 + 2 * i
                    cs = bass.ds(2 * NCOL * i + c0 * NCOL, NCOL)
                    dve.wait_ge(w_used, unit_no(ph, c0, i, ph["n"])[1])
                    for t in range(NT):
                        ins = nc.vector.tensor_tensor(y_tmp[:, t, :], bank[2 * (c0 % 2) + t][:, :], gate[:, cs],
                                                      ALU.mult)
                    ins.then_inc(acc_free, 1)
                    dve.wait_ge(acc_free, ph["chunk"] + c0 + 2 * i + 3)
                    for t in range(NT):
                        ins = nc.vector.scalar_tensor_tensor(x[:, t, cs], x[:, t, cs], ALPHA if first else 1.0,
                                                             y_tmp[:, t, :], ALU.mult, ALU.add)
                    ins.then_inc(y_sum, 1)
                    dve.wait_ge(y_sum, y + 1)
                    if stats:
                        for t in range(NT):
                            ins = nc.vector.bn_stats(bn[:, t, bass.ds(c0 + 2 * i, 1), :].rearrange("p a s -> p (a s)"),
                                                     x[:, t, cs])
                        ins.then_inc(y_done, 1)
                    else:
                        nc.vector.tensor_copy(t1[:, 0:1], mod[:, 0:1]).then_inc(y_done, 1)
                return tail

            def rstd(v, sdv, r, t, var_sem, sd_sem, n):
                dve.wait_ge(sem(sd_sem), n)
                link(nc.vector.reciprocal(r, sdv))
                link(nc.vector.tensor_tensor(t, r, r, ALU.mult))
                link(nc.vector.tensor_tensor(t, t, v, ALU.mult))
                link(nc.vector.tensor_scalar(t, t, -0.5, 1.5, ALU.mult, ALU.add))
                link(nc.vector.tensor_tensor(r, r, t, ALU.mult))

            def layer_norm(s, last):
                dve.wait_ge(y_done, {0: 4, 1: 12, 2: 16, 3: 24}[s])
                for t in range(NT):
                    ins = nc.vector.bn_aggr(mv[:, t, :], bn[:, t].rearrange("p c s -> p (c s)"))
                link(ins)
                nc.vector.tensor_scalar(var, mv[:, :, 1], EPS, None, ALU.add).then_inc(sem("ln_var"), 1)
                dve.wait_ge(sem("ln_var"), s + 1)
                rstd(var, sd, rs, t1, "ln_var", "ln_sd", s + 1)
                dve.wait_ge(sem("ln_in"), 32 * (s + 1))
                done = 0
                for n in range(4):
                    cs = slice(n * NCOL, (n + 1) * NCOL)
                    for t in range(NT):
                        ins = nc.vector.scalar_tensor_tensor(x[:, t, cs], x[:, t, cs], mv[:, t, 0:1], lnp[:, 0, cs],
                                                             ALU.subtract, ALU.mult)
                    link(ins)
                    for t in range(NT):
                        ins = nc.vector.scalar_tensor_tensor(x[:, t, cs], x[:, t, cs], rs[:, t:t + 1], lnp[:, 1, cs],
                                                             ALU.mult, ALU.add)
                    ins.then_inc(sem("ln_chunk"), 1)
                    if n and not last:
                        for v in (2 * n - 2, 2 * n - 1):
                            u_lo(U_LN[s] + v, slice(2 * v, 2 * v + 2), v % 2)
                if not last:
                    dve.wait_ge(sem("ln_chunk"), 4 * s + 4)
                    for v in (6, 7):
                        u_lo(U_LN[s] + v, slice(2 * v, 2 * v + 2), v % 2)
                    nc.vector.tensor_copy(t1[:, 0:1], mod[:, 0:1]).then_inc(sem("ln_done"), 1)

            def hidden(layer, name, c0, i, nf=2):
                q = H_LAYER * layer + H0[name] + c0 + 2 * i
                f = (0 if name == "up_a" else FT_A) + 2 * c0 + 4 * i
                col = C_CONV + layer * 4 * FT + f
                dve.wait_ge(h_bias, q + 1)
                for tap, lag, s in ((1, 1, h_tap), (0, 2, h_conv)):
                    for k in range(nf):
                        ins = nc.vector.scalar_tensor_tensor(
                            gc[:, k, lag:S], T[1][:, k * S:(k + 1) * S - lag],
                            cols[:, bass.ds(col + tap * FT + k, 1)], gc[:, k, lag:S], ALU.mult, ALU.add)
                    ins.then_inc(s, 1)
                    if tap:
                        dve.wait_ge(h_tap, q + 1)
                dve.wait_ge(h_gelu, q + 1)
                nc.vector.tensor_tensor(h32[:, 0:nf, :], T[0][:, 0:nf * S].rearrange("p (k s) -> p k s", k=nf),
                                        gc[:, 0:nf, :], ALU.mult).then_inc(h_mul, 1)
                dve.wait_ge(h_hi, q + 1)
                at = bass.ds(2 * c0 + 4 * i, nf)
                nc.vector.tensor_tensor(hlo[:, at, :], h32[:, 0:nf, :], hhi[:, at, :].bitcast(f32), ALU.subtract
                                        ).then_inc(h_lo, 1)

            def mlp(layer):
                for name in ("up_a", "up_b"):
                    key = (layer, name)
                    last = PH[key]["chunks"] - 1
                    prev = lambda c0, i: hidden(layer, name, c0 - 1, i)
                    steps(key, 0, 1)
                    steps(key, 1, 1 + (last - 1) // 2 * 2, mid=prev)
                    for c in range(1 + (last - 1) // 2 * 2, last + 1):
                        if name == "up_b" and c == last:
                            hidden(layer, name, c - 1, 0)
                            lo_unit(PH[key], c, 0, 2, UNIT)
                            lo_unit(PH[key], c, 0, 3, UNIT)
                        else:
                            steps(key, c, c + 1, mid=prev)
                    hidden(layer, name, last, 0, 1 if name == "up_b" else 2)
                    down = (layer, "down" + name[2:])
                    steps(down, 0, 4, tail=y_out(down, name == "up_a", name == "up_b"),
                          more=not (layer == DEPTH - 1 and name == "up_b"))

            nc.vector.memset(t1[:, 0:1], 0.0).then_inc(w_lo, RAW_SLOTS)
            nc.vector.memset(t1[:, 1:2], 0.0).then_inc(a_step, A0)
            nc.vector.memset(var[:, 0:1], 0.0).then_inc(a_out, 1)
            nc.vector.memset(var[:, 1:2], 0.0).then_inc(u_ready, 2)
            nc.vector.memset(sd[:, 0:1], 0.0).then_inc(t_free, 2)
            nc.vector.memset(sd[:, 1:2], 0.0).then_inc(acc_free, 2)
            nc.vector.memset(rs[:, 0:1], 0.0).then_inc(h_mul, 1)
            dve.wait_ge(sem("rows_T"), 1)
            nc.vector.tensor_copy(cols[:, 0:2 * 96 + 4 * FT], bank[0][:, 0:2 * 96 + 4 * FT]).then_inc(sem("cols_in"), 1)
            nc.vector.tensor_copy(cols[:, 2 * 96 + 4 * FT:n_cols], bank[1][:, 0:n_cols - 2 * 96 - 4 * FT]
                                  ).then_inc(sem("cols_in"), 1)
            dve.wait_ge(sem("cols_in"), 2)
            dve.wait_ge(sem("silu_c"), 1)
            with dve.Fori(0, 4) as n:
                ada_rows(n, 0, KT)
                ada_evac((0, 0, n, n))
            with dve.Fori(0, 4) as n:
                ada_rows(n + 4, 0, KT)
                ada_evac((0, 1, n, n + 4))
                for b in range(2):
                    u_lo(2 * n + b, bass.ds(4 * n + 2 * b, 2), b)
            lo_unit(PH[0, "in"], 0, 0, 0, UNIT)
            lo_unit(PH[0, "in"], 0, 0, 1, UNIT)
            steps((0, "in"), 0, 4)
            steps((0, "in"), 4, 8)

            dve.wait_ge(sem("lr_hi"), 1)
            nc.vector.tensor_tensor(w_lrl[:, :, :], w_lr[:, :, :], w_lrh[:, :, :].bitcast(f32), ALU.subtract
                                    ).then_inc(sem("lr_lo"), 1)
            dve.wait_ge(sem("lr"), 1)
            nc.vector.tensor_copy(lr[:, :, :], bank[7][:, 0:NT * GRANK].rearrange("p (t r) -> p t r", t=NT)
                                  ).then_inc(sem("lr_out"), 1)
            dve.wait_ge(sem("lr_T"), 1)
            nc.vector.tensor_copy(lrT[:, :], bank[7][0:GRANK, 0:S]).then_inc(sem("lr_T_out"), 1)

            def mix_lo(v):
                u_lo(U_MIX + v, slice(2 * v, 2 * v + 2), v % 2)
            mix_lo(0)
            mix_lo(1)
            dve.wait_ge(sem("gate_pre"), 1)
            dve.wait_ge(sem("gla_in"), 32)
            for t in range(NT):
                ins = nc.vector.tensor_tensor(loga[:, t, :], bank[6 + t][:, :], b_g[:, :], ALU.add)
            ins.then_inc(sem("gate_pre_out"), 1)
            mix_lo(2)
            mix_lo(3)
            dve.wait_ge(sem("gate_pre_out"), 1)
            dve.wait_ge(sem("ls"), 3)
            nc.vector.scalar_tensor_tensor(loga[:, :, :].rearrange("p t c -> p (t c)"),
                                           loga[:, :, :].rearrange("p t c -> p (t c)"), 0.0,
                                           kdec[:, :, :].rearrange("p t c -> p (t c)"), ALU.min, ALU.subtract
                                           ).then_inc(sem("log_a"), 1)
            nc.vector.memset(scT[:, :, :, :], 0.0).then_inc(sem("sc_zero"), 1)
            dve.wait_ge(sem("exp_suf"), 2)
            nc.vector.tensor_tensor(kdec[:, :, :], kdec[:, :, :], z[:, :, OFF_K:OFF_V], ALU.mult).then_inc(sem("kdec"), 1)
            dve.wait_ge(sem("qk_T_out"), 1)
            dve.wait_ge(sem("exp_b"), 4)
            for j in range(2):
                hs = slice(2 * j, 2 * j + 2)
                e_b = bank[2 + j].rearrange("p (h s) -> p h s", h=2)
                nc.vector.tensor_copy(decay[:, hs, :], e_b[:, :, CH - 1::CH])
                nc.vector.tensor_tensor(qdT[:, hs, :], qdT[:, hs, :], e_b, ALU.mult)
                ins = nc.vector.tensor_tensor(kiT[:, hs, :], kiT[:, hs, :], bank[j].rearrange("p (h s) -> p h s", h=2),
                                              ALU.mult)
            ins.then_inc(sem("qk_dec"), 1)
            dve.wait_ge(sem("qk_dec"), 1)
            dve.wait_ge(sem("scores"), 1)
            dve.wait_ge(sem("sc_zero"), 1)
            for t in range(NT):
                for h in range(GH):
                    ins = nc.vector.copy_predicated(scT[:, t, h, :], sum_inc.bitcast(i32),
                                                    bank[6 + t][:, h * P:(h + 1) * P])
            ins.then_inc(sem("scores_out"), 1)
            dve.wait_ge(sem("outer"), 1)
            for j in range(2):
                ins = nc.vector.tensor_copy(state[:, 0, 2 * j:2 * j + 2, :],
                                            bank[j].rearrange("p (h v) -> p h v", h=2))
            link(ins)
            for c in (1, 2):
                for h in range(GH):
                    to = state[:, 1, h, :] if c == 1 else state3[:, h, :]
                    ins = nc.vector.scalar_tensor_tensor(to, state[:, c - 1, h, :], decay[:, h, c:c + 1],
                                                         bank[2 * c + h // 2][:, (h % 2) * GDV:(h % 2 + 1) * GDV],
                                                         ALU.mult, ALU.add)
                if c == 1:
                    link(ins)
            ins.then_inc(sem("states"), 1)
            dve.wait_ge(sem("gla_o"), 1)
            for q in range(8):
                t, h = divmod(q, GH)
                ins = nc.vector.bn_stats(gbn[:, q, :], bank[2 * t + h // 2][:, (h % 2) * GDV:(h % 2 + 1) * GDV])
            link(ins)
            for q in range(8):
                ins = nc.vector.bn_aggr(gmv[:, q, :], gbn[:, q, :])
            link(ins)
            nc.vector.tensor_scalar(gvar, gmv[:, :, 1], EPS, None, ALU.add).then_inc(sem("gla_var"), 1)
            dve.wait_ge(sem("gla_var"), 1)
            rstd(gvar, gsd, grs, gt, "gla_var", "gla_sd", 1)
            dve.wait_ge(sem("silu_r"), 2)
            for q in range(8):
                t, h = divmod(q, GH)
                ins = nc.vector.scalar_tensor_tensor(
                    z[:, t, OFF_Q + h * GDV:OFF_Q + (h + 1) * GDV], bank[2 * t + h // 2][:, (h % 2) * GDV:(h % 2 + 1) * GDV],
                    gmv[:, q, 0:1], z[:, t, OFF_R + h * GDV:OFF_R + (h + 1) * GDV], ALU.subtract, ALU.mult)
            link(ins)
            for h in range(GH):
                for t in range(NT):
                    o = z[:, t, OFF_Q + h * GDV:OFF_Q + (h + 1) * GDV]
                    ins = nc.vector.tensor_scalar(o, o, grs[:, t * GH + h:t * GH + h + 1], None, ALU.mult)
                ins.then_inc(sem("y_b"), 1)
            dve.wait_ge(sem("y_b"), 4)
            for v in range(4, 8):
                mix_lo(v)
            steps((0, "out"), 0, 4, tail=y_out((0, "out"), True, True))
            layer_norm(0, False)
            mlp(0)
            layer_norm(1, False)
            steps((1, "qkv"), 0, 4)
            steps((1, "qkv"), 4, 8)
            steps((1, "qkv"), 8, 12)
            for s in range(1, AH + 3):
                if s <= AH:
                    h = s - 1
                    dve.wait_ge(sem("att_s"), h + 1)
                    sb = bank[6 + h % 2]
                    nc.vector.reduce_max(nmax[:, h % 2, 0:1], sb[:, 0:P], AX.X, negate=True)
                    nc.vector.reduce_max(nmax[:, h % 2, 1:2], sb[:, P:3 * P], AX.X, negate=True
                                         ).then_inc(sem("att_max"), 1)
                if 2 <= s <= AH + 1:
                    h = s - 2
                    dve.wait_ge(sem("att_pT"), h + 1)
                    nc.vector.tensor_copy(probT[:, h % 2, :], bank[h % 2][:, 0:3 * P]).then_inc(sem("att_pT_out"), 1)
                if s <= AH:
                    h = s - 1
                    dve.wait_ge(sem("att_exp"), h + 1)
                    link(nc.vector.reciprocal(rinv[:, h % 2, :], rsum[:, h % 2, :]))
                    for a, b, t in ((0, P, 0), (P, 3 * P, 1)):
                        ins = nc.vector.tensor_scalar(prob[:, h % 2, a:b], prob[:, h % 2, a:b], rinv[:, h % 2, t:t + 1],
                                                      None, ALU.mult)
                    ins.then_inc(sem("att_p"), 1)
                if s >= 3:
                    h = s - 3
                    dve.wait_ge(u_hi_done, U_ATT + h + 1)
                    nc.vector.tensor_tensor(ulo[:, h, :], bank[2 + h % 2][:, 0:S], uhi[:, h, :].bitcast(f32),
                                            ALU.subtract).then_inc(u_ready, 1)
            steps((1, "o"), 0, 4, tail=y_out((1, "o"), True, True))
            layer_norm(2, False)
            mlp(1)
            layer_norm(3, True)

        @block.tensor
        def _(pe):
            def unit(ph, c0, i, j, parts, u_of, first, last, banks, after=None, late=None):
                u, un = unit_no(ph, c0, i, j)
                pe.wait_ge(w_lo, un + (RAW_SLOTS + 1))
                if after is not None:
                    pe.wait_ge(u_ready, after)
                h, l = u_of
                width = UNIT // (8 if len(parts) == 8 else 4)
                slot = u % HL_SLOTS
                for n, (k, kt) in enumerate(parts):
                    if late is not None and kt == late[0]:
                        pe.wait_ge(h_lo, late[1])
                    w_h = whi[:, slot, k * width:(k + 1) * width]
                    w_l = wlo[:, slot, k * width:(k + 1) * width]
                    for t in range(NT):
                        acc = banks[t][:, 0:width]
                        uh, ul = h[:, kt, t * P:(t + 1) * P], l[:, kt, t * P:(t + 1) * P]
                        end = last and n == len(parts) - 1
                        nc.tensor.matmul(acc, uh, w_h, start=first and n == 0, stop=False)
                        nc.tensor.matmul(acc, uh, w_l, start=False, stop=False)
                        ins = nc.tensor.matmul(acc, ul, w_h, start=False, stop=end)
                ins.then_inc(w_used, 1)

            def ada_sum(blk):
                layer, part, n, m = blk
                pe.wait_ge(a_step, m * KT + (A0 + KT))
                pe.wait_ge(a_out, m + 1)
                if part in (2, 5):
                    ins = nc.tensor.matmul(ada_p[:, :], ones, ada_acc[:, :], start=True, stop=True)
                else:
                    for q in range(4):
                        ins = nc.tensor.matmul(ada_p[:, q:q + 1], ada_acc[:, q * P:(q + 1) * P], ones[:, 0:1],
                                               start=True, stop=True)
                ins.then_inc(a_sum, 1)

            def chunks(key, lo, hi, u_of=(uhi, ulo), u_from=None, mid=None, late=None):
                ph = PH[key]
                start = [sum(ph["kts"][:j]) for j in range(ph["n"])]

                def body(c0, i):
                    small = key[1] == "up_b" and c0 == 11
                    n = 2 if small else ph["n"]
                    pe.wait_ge(acc_free, ph["chunk"] + c0 + 2 * i + 1)
                    banks = bank[2 * (c0 % 2):2 * (c0 % 2) + 2]
                    for j in range(n):
                        k0, kn = (8 * j, 8) if small else (start[j], ph["kts"][j])
                        unit(ph, c0, i, j, [(k, k0 + k) for k in range(kn)], u_of, j == 0, j == n - 1, banks,
                             None if u_from is None else u_from + (k0 + kn) // 2, late)
                        if j == 0 and mid:
                            mid(c0, i)
                    blk = ada_of(key, lo, c0, i)
                    if blk:
                        ada_sum(blk)
                if hi - lo == 1:
                    body(lo, 0)
                else:
                    pairs(pe, lo, hi, body)

            def hidden_T(layer, name, c0, i, nf=2):
                q = H_LAYER * layer + H0[name] + c0 + 2 * i
                pe.wait_ge(acc_free, PH[layer, name]["chunk"] + c0 + 2 * i + 3)
                pe.wait_ge(h_mul, q + 1)
                for s in range(2):
                    for k in range(nf):
                        for t in range(NT):
                            ins = nc.tensor.transpose(T[s][:, k * S + t * P:k * S + (t + 1) * P],
                                                      g_tok[:, t, (s * nf + k) * P:(s * nf + k + 1) * P], ident)
                ins.then_inc(h_T, 1)

            def mlp(layer, u_from):
                for name in ("up_a", "up_b"):
                    key = (layer, name)
                    last = PH[key]["chunks"] - 1
                    prev = lambda c0, i: hidden_T(layer, name, c0 - 1, i)
                    chunks(key, 0, 1, u_from=u_from)
                    chunks(key, 1, 1 + (last - 1) // 2 * 2, mid=prev)
                    for c in range(1 + (last - 1) // 2 * 2, last + 1):
                        chunks(key, c, c + 1, mid=prev)
                    hidden_T(layer, name, last, 0, 1 if name == "up_b" else 2)
                    done = H_LAYER * layer + H0[name] + last + 1
                    pe.wait_ge(h_lo, done - 1)
                    kt = 2 * last
                    chunks((layer, "down" + name[2:]), 0, 4, u_of=(hhi, hlo), late=(kt, done))
                    u_from = None

            def channels_T(src, base, v):
                pe.wait_ge(t_free, base + v + 1)
                for k in range(2):
                    for t in range(NT):
                        ins = nc.tensor.transpose(T[v % 2][:, k * S + t * P:k * S + (t + 1) * P], src(t, 2 * v + k), ident)
                ins.then_inc(t_full, 1)

            pe.wait_ge(sem("const_in"), 16)
            pe.wait_ge(sem("rows_in"), 16 * ROW_SRC)
            sizes = [96] * 2 + [FT] * 8 + [8, 8, KT]
            at = 0
            for i, size in enumerate(sizes):
                if i == 6:
                    at = 0
                to = bank[0 if i < 6 else 1]
                ins = nc.tensor.transpose(to[:, at:at + size], rows[0:size, i, :], ident[0:size, 0:size])
                at += size
            ins.then_inc(sem("rows_T"), 1)
            pe.wait_ge(sem("x_in"), 16)
            for v in range(8):
                channels_T(lambda t, k: x[:, t, k * P:(k + 1) * P], T_X, v)
            with pe.Fori(0, 4) as n:
                ada_sum((0, 0, n, n))
            with pe.Fori(0, 4) as n:
                ada_sum((0, 1, n, n + 4))
            pe.wait_ge(sem("cols_in"), 2)
            chunks((0, "in"), 0, 4, u_from=2 + U_FIRST)
            chunks((0, "in"), 4, 8)

            pe.wait_ge(sem("lr_lo"), 1)
            for t in range(NT):
                for kt in range(KT):
                    uh, ul = uhi[:, kt, t * P:(t + 1) * P], ulo[:, kt, t * P:(t + 1) * P]
                    to = bank[7][:, t * GRANK:(t + 1) * GRANK]
                    nc.tensor.matmul(to, uh, w_lrh[:, kt, :], start=kt == 0, stop=False)
                    nc.tensor.matmul(to, uh, w_lrl[:, kt, :], start=False, stop=False)
                    ins = nc.tensor.matmul(to, ul, w_lrh[:, kt, :], start=False, stop=kt == KT - 1)
            ins.then_inc(sem("lr"), 1)
            pe.wait_ge(acc_free, 2 + 8)
            pe.wait_ge(sem("pool_in"), 16 * 5)

            def pool_mean(g):
                for k in range(2):
                    col = (2 * g + k) * P
                    nc.tensor.matmul(bank[g][:, k * S:(k + 1) * S], z[:, 0, col:col + P], band[:, g, 0:S],
                                     start=True, stop=False)
                    ins = nc.tensor.matmul(bank[g][:, k * S + P:(k + 1) * S], z[:, 1, col:col + P], band[:, g, S:S + P],
                                           start=False, stop=True)
                ins.then_inc(sem("pool_T"), 1)

            def pool_map(g):
                pe.wait_ge(t_free, T_MIX + g + 1)
                pe.wait_ge(sem("pool_T_out"), g + 1)
                for d in range(2):
                    for k in range(2):
                        ins = nc.tensor.matmul(T[g % 2][:, d * S:(d + 1) * S], w_pool[:, g, k, d * P:(d + 1) * P],
                                               dT[:, g % 2, k, :], start=k == 0, stop=k == 1)
                ins.then_inc(t_full, 1)
            pool_mean(0)
            pool_mean(1)
            pool_mean(2)
            pool_mean(3)
            pe.wait_ge(sem("lr_out"), 1)
            for t in range(NT):
                ins = nc.tensor.transpose(bank[7][0:GRANK, t * P:(t + 1) * P], lr[:, t, :], ident)
            ins.then_inc(sem("lr_T"), 1)
            pool_map(0)
            pe.wait_ge(sem("lr_T_out"), 1)
            pe.wait_ge(sem("gla_in"), 32)
            pe.wait_ge(a_out, 16 + 1)
            for t in range(NT):
                ins = nc.tensor.matmul(bank[6 + t][:, :], lrT[:, t * P:(t + 1) * P], w_g[:, :], start=True, stop=True)
            ins.then_inc(sem("gate_pre"), 1)
            for g in range(1, 4):
                pool_map(g)
            for j, off in ((0, OFF_Q), (2, OFF_K)):
                for h in range(GH):
                    for t in range(NT):
                        ins = nc.tensor.transpose(bank[j + h // 2][:, (h % 2) * S + t * P:(h % 2) * S + (t + 1) * P],
                                                  z[:, t, off + h * GDK:off + (h + 1) * GDK], ident)
            ins.then_inc(sem("qk_T"), 1)
            pe.wait_ge(sem("log_a"), 1)
            pe.wait_ge(sem("qk_T_out"), 1)
            for t in range(NT):
                nc.tensor.matmul(bank[t][:, :], sum_suf, loga[:, t, :], start=True, stop=True)
            for h in range(GH):
                for t in range(NT):
                    ins = nc.tensor.matmul(bank[2 + h // 2][:, (h % 2) * S + t * P:(h % 2) * S + (t + 1) * P],
                                           loga[:, t, h * GDK:(h + 1) * GDK], sum_inc, start=True, stop=True)
            ins.then_inc(sem("cum"), 1)
            pe.wait_ge(sem("qk_dec"), 1)
            for t in range(NT):
                for h in range(GH):
                    ins = nc.tensor.matmul(bank[6 + t][:, h * P:(h + 1) * P], kiT[:, h, t * P:(t + 1) * P],
                                           qdT[:, h, t * P:(t + 1) * P], start=True, stop=True)
            ins.then_inc(sem("scores"), 1)
            pe.wait_ge(sem("kdec"), 1)
            pe.wait_ge(t_free, 2 + T_MIX + 4)
            for c in range(3):
                t, r = c // 2, slice(c % 2 * CH, (c % 2 + 1) * CH)
                for h in range(GH):
                    ins = nc.tensor.matmul(bank[2 * c + h // 2][:, (h % 2) * GDV:(h % 2 + 1) * GDV],
                                           kdec[r, t, h * GDK:(h + 1) * GDK],
                                           z[r, t, OFF_V + h * GDV:OFF_V + (h + 1) * GDV], start=True, stop=True)
            ins.then_inc(sem("outer"), 1)
            pe.wait_ge(sem("scores_out"), 1)
            pe.wait_ge(sem("states"), 1)
            for t in range(NT):
                for h in range(GH):
                    to = bank[2 * t + h // 2][:, (h % 2) * GDV:(h % 2 + 1) * GDV]
                    ins = nc.tensor.matmul(to, scT[:, t, h, :], z[:, t, OFF_V + h * GDV:OFF_V + (h + 1) * GDV],
                                           start=True, stop=False, skip_group_check=True)
                    for c in (2 * t, 2 * t + 1):
                        if c:
                            st = state[:, c - 1, h, :] if c < 3 else state3[:, h, :]
                            r = slice(c % 2 * CH, (c % 2 + 1) * CH)
                            ins = nc.tensor.matmul(to[r, :], qdT[:, h, c * CH:(c + 1) * CH], st, start=False,
                                                   stop=True, skip_group_check=True)
            ins.then_inc(sem("gla_o"), 1)
            for v in range(4, 8):
                pe.wait_ge(sem("y_b"), v - 3)
                channels_T(lambda t, k: z[:, t, OFF_Q + (k - 8) * P:OFF_Q + (k - 7) * P], T_MIX, v)
            chunks((0, "out"), 0, 4, u_from=2 + U_MIX)

            def ln_T(s):
                for v in range(8):
                    pe.wait_ge(sem("ln_chunk"), 4 * s + v // 2 + 1)
                    channels_T(lambda t, k: x[:, t, k * P:(k + 1) * P], T_LN[s], v)
            ln_T(0)
            mlp(0, 2 + U_LN[0])
            ln_T(1)
            chunks((1, "qkv"), 0, 4, u_from=2 + U_LN[1])
            chunks((1, "qkv"), 4, 8)
            chunks((1, "qkv"), 8, 12)

            C_QKV = PH[1, "qkv"]["chunk"] + 12
            pe.wait_ge(acc_free, 2 + C_QKV)
            pe.wait_ge(t_free, 2 + T_LN[1] + 8)
            pe.wait_ge(a_out, PH[1, "up_a"]["block"] + 1)
            pe.wait_ge(sem("toep_in"), 16)
            for s in range(AH + 3):
                if s < AH:
                    if s >= 2:
                        pe.wait_ge(sem("att_qk"), s - 1)
                    for j in range(2):
                        for t in range(NT):
                            ins = nc.tensor.transpose(T[s % 2][:, j * S + t * P:j * S + (t + 1) * P],
                                                      qkv[:, t, j * D + s * AD:j * D + (s + 1) * AD], ident)
                    ins.then_inc(sem("att_T"), 1)
                if 1 <= s <= AH:
                    h = s - 1
                    pe.wait_ge(sem("att_qk"), h + 1)
                    if h >= 2:
                        pe.wait_ge(sem("att_exp"), h - 1)
                    sb, q, k = bank[6 + h % 2], qkT[:, h % 2, 0:S], qkT[:, h % 2, S:2 * S]
                    nc.tensor.matmul(sb[:, 0:P], q[:, 0:P], k[:, 0:P], start=True, stop=False)
                    nc.tensor.matmul(sb[:, 0:P], toep[:, h, 0:P], rev, start=False, stop=False)
                    nc.tensor.matmul(sb[:, 0:P], mask_q, mask_k, start=False, stop=True)
                    nc.tensor.matmul(sb[:, P:3 * P], q[:, P:S], k[:, 0:S], start=True, stop=False)
                    nc.tensor.matmul(sb[:, P:2 * P], toep[:, h, P:S], rev, start=False, stop=False)
                    nc.tensor.matmul(sb[:, 2 * P:3 * P], toep[:, h, 0:P], rev, start=False, stop=False)
                    nc.tensor.matmul(sb[:, 2 * P:3 * P], mask_q, mask_k, start=False, stop=True
                                     ).then_inc(sem("att_s"), 1)
                if 2 <= s <= AH + 1:
                    h = s - 2
                    pe.wait_ge(sem("att_p"), h + 1)
                    if h >= 2:
                        pe.wait_ge(sem("att_pT_out"), h - 1)
                    for j in range(3):
                        to = (0, P, 2 * P)[(0, 1, 2)[j]]
                        ins = nc.tensor.transpose(bank[h % 2][:, to:to + P], prob[:, h % 2, j * P:(j + 1) * P], ident)
                    ins.then_inc(sem("att_pT"), 1)
                if s >= 3:
                    h = s - 3
                    pe.wait_ge(sem("att_pT_out"), h + 1)
                    if h >= 2:
                        pe.wait_ge(u_ready, 2 + U_ATT + h - 1)
                    v0 = 2 * D + h * AD
                    nc.tensor.matmul(bank[2 + h % 2][:, 0:S], qkv[:, 0, v0:v0 + AD], probT[:, h % 2, 0:S],
                                     start=True, stop=False)
                    nc.tensor.matmul(bank[2 + h % 2][:, P:S], qkv[:, 1, v0:v0 + AD], probT[:, h % 2, 2 * P:3 * P],
                                     start=False, stop=True).then_inc(sem("att_o"), 1)
            pe.wait_ge(u_ready, 2 + U_ATT + AH)
            chunks((1, "o"), 0, 4)
            ln_T(2)
            mlp(1, 2 + U_LN[2])


_INS = ["x", "c", "w_ada", "b_ada", "ln_g", "ln_b", "w_in_ab", "w_gate_lr", "b_gate", "gla_norm_g", "w_pool",
        "pool_scale", "w_out_ab", "w_qkv", "rel_bias", "w_o", "w_up", "conv_w", "conv_b", "w_down"]


def constant_tables():
    import numpy as np
    j, i = np.arange(P)[:, None], np.arange(P)[None, :]
    same = j // CH == i // CH
    consts = np.zeros((P, CONST_COLS), np.float32)
    consts[:, 0:P] = j == i
    consts[:, P:2 * P] = j == P - 1 - i
    consts[:, 2 * P:3 * P] = (same & (j <= i)) / GTAU
    consts[:, 3 * P:4 * P] = (same & (j > i)) / GTAU
    consts[:, 4 * P:5 * P] = 1.0
    consts[0, 5 * P:5 * P + CH] = 1.0
    consts[0, 6 * P + CH:7 * P] = NEG
    band = np.zeros((P, 4, BAND), np.float32)
    src, dst = np.arange(S)[:, None], np.arange(S)[None, :]
    for g, w in enumerate(WINDOWS):
        m = ((src <= dst) & (src > dst - w)) / np.minimum(dst + 1, w) - (src == dst)
        band[:, g, 0:S] = m[0:P]
        band[:, g, S:] = m[P:, P:]
    return {"consts": consts, "band": band}


def kernel(**inputs):
    import numpy as np
    import concourse.bacc as bacc
    from concourse.bass_utils import run_bass_kernel_spmd as run

    nc = bacc.Bacc("TRN2", target_bir_lowering=False, num_devices=1, dynamic_dma_scratch_size=1024)
    arrays, args = {}, {}
    for name, a in [(n, inputs[n]) for n in _INS] + list(constant_tables().items()):
        a = np.ascontiguousarray(a)
        arrays[f"in_{name}"] = a
        args[name] = nc.dram_tensor(f"in_{name}", a.shape, mybir.dt.from_np(a.dtype), kind="ExternalInput").ap()
    out = nc.dram_tensor("out_x", (1, S, D), mybir.dt.float32, kind="ExternalOutput").ap()
    build(nc, args, out)
    r = run(nc, [arrays], core_ids=[0])
    return r.results[0]["out_x"]
```

```python
import concourse.bass as bass
from concourse import mybir
from contextlib import ExitStack

D = 2048
S = 256
P = 128
F = 5504
KT = D // P
NT = S // P
NCOL = 512
UNIT = 2048
CH = 64
POOL_W = D // 2
WINDOWS = (2, 4, 8, 16)
PG = POOL_W // len(WINDOWS)
GH, GDV, GDK, GRANK, GTAU = 4, 256, 128, 16, 16.0
OFF_Q = POOL_W
OFF_K = OFF_Q + GH * GDK
OFF_V = OFF_K + GH * GDK
OFF_R = OFF_V + GH * GDV
OFF_LR = OFF_R + GH * GDV
AH, AD = 16, 128
REL = 256
DEPTH = 2
ALPHA = (2.0 * DEPTH) ** 0.25
EPS = 1e-5
FT = F // P
FT_A = 20
FT_B = FT - FT_A
NEG = -1e30
RAW_SLOTS, HL_SLOTS, ADA_SLOTS = 4, 2, 4
ADA_HALVES = KT // 2
CONST_COLS = 7 * P
BAND = 3 * P


def plan():
    four = (4, 4, 4, 4)
    phases = []
    for layer in range(DEPTH):
        if layer % 2 == 0:
            phases += [(layer, "in", 8, four, 4), (layer, "mix", 0, four, 6), (layer, "out", 4, four, 2)]
        else:
            phases += [(layer, "qkv", 12, four, 6), (layer, "mix", 0, four, 3), (layer, "o", 4, four, 2)]
        last = layer == DEPTH - 1
        phases += [(layer, "up_a", FT_A // 2, four, 4),
                   (layer, "down_a", 4, (4, 4, 4, 4, 2, 2), 0 if last else 2),
                   (layer, "up_b", FT_B // 2 + 1, four, 0 if last else 5),
                   (layer, "down_b", 4, (4, 4, 4, 4, 4, 3), 0 if last else 2)]
    out, unit, chunk, block = {}, 0, 0, 8
    for layer, name, chunks, kts, blocks in phases:
        out[layer, name] = dict(chunks=chunks, kts=kts, n=len(kts), unit=unit, chunk=chunk, block=block,
                                blocks=blocks)
        unit += chunks * len(kts) - (2 if name == "up_b" else 0)
        chunk += chunks
        block += blocks
    return out


def build(nc, A, out):
    f32, f32r, i32 = mybir.dt.float32, mybir.dt.float32r, mybir.dt.int32
    ALU = mybir.AluOpType
    ACT = mybir.ActivationFunctionType
    AX = mybir.AxisListType
    PH = plan()

    ctx = ExitStack()
    with ctx:
        used = [2048]

        def region(size):
            at = used[0]
            used[0] += (size + 31) // 32 * 32
            return at

        def place(name, shape, at, dt=f32):
            return nc.alloc_sbuf_tensor_at(name, shape, dt, offset=at)

        raw = place("w_raw", [P, RAW_SLOTS, UNIT], region(RAW_SLOTS * UNIT * 4))
        whi = place("w_hi", [P, HL_SLOTS, UNIT], region(HL_SLOTS * UNIT * 4), f32r)
        wlo = place("w_lo", [P, HL_SLOTS, UNIT], region(HL_SLOTS * UNIT * 4), f32r)
        ada_w = place("ada_w", [P, ADA_SLOTS, 2, NCOL], region(ADA_SLOTS * 2 * NCOL * 4))
        ada_acc = place("ada_acc", [P, NCOL], region(NCOL * 4))
        gate = place("gate", [P, D], region(D * 4))
        r_u = region(2 * KT * S * 4)
        uhi = place("u_hi", [P, KT, S], r_u, f32r)
        ulo = place("u_lo", [P, KT, S], r_u + KT * S * 4, f32r)
        x = place("x_tok", [P, NT, D], region(NT * D * 4))
        r_w = region(48 * 1024)
        r_aux = region(16 * 1024)
        r_s = region(12 * 1024)
        consts = place("consts", [P, CONST_COLS], region(CONST_COLS * 4))
        n_cols = 2 * 96 + DEPTH * 4 * FT + 8 + 8
        cols = place("cols", [P, n_cols], region(n_cols * 4))
        mod = place("mod", [P, DEPTH * 96], region(DEPTH * 96 * 4))
        silu_c = place("silu_c", [P, KT], region(KT * 4))
        small = place("small", [P, 192], region(192 * 4))
        assert used[0] <= 229368, used[0]

        xT = place("x_T", [P, KT, S], r_w)
        rows = place("rows", [P, 13, P], r_w + 32 * 1024)
        z = place("z", [P, NT, OFF_LR], r_w)
        kdec = place("k_dec", [P, NT, GH * GDK], r_w + 32768)
        loga = place("log_a", [P, NT, GH * GDK], r_w + 32768 + 4096)
        qdT = place("q_dec_T", [P, GH, S], r_w + 32768 + 8192)
        kiT = place("k_inv_T", [P, GH, S], r_w + 32768 + 12288)
        hhi = place("hid_hi", [P, FT_B, S], r_w, f32r)
        hlo = place("hid_lo", [P, FT_B, S], r_w + FT_B * S * 4, f32r)
        qkv = place("qkv", [P, NT, 3 * D], r_w)
        state = place("gla_state", [P, 2, GH, GDV], r_u + 8 * S * 4)
        state3 = place("gla_state3", [P, GH, GDV], r_u + KT * S * 4 + 8 * S * 4)
        scT = place("scores_T", [P, NT, GH, P], r_u + KT * S * 4 + 8 * S * 4 + 4096)
        band = place("band", [P, 4, BAND], r_aux)
        w_pool = place("w_pool_sb", [P, 4, 2, PG], r_aux + 4 * BAND * 4)
        toep = place("toeplitz", [P, AH, S], r_aux)
        lnp = place("ln_params", [P, 2, D], r_aux)
        g_tok = place("h_tok", [P, NT, NCOL], r_s)
        gc = place("conv", [P, 2, S], r_s + 4096)
        h32 = place("h_f32", [P, 2, S], r_s + 6144)
        y_tmp = place("y_gated", [P, NT, NCOL], r_s + 8192)
        u32 = place("u_f32", [P, 2, 2 * S], r_s)
        w_lr = place("w_lr", [P, KT, GRANK], r_w + 40960)
        w_lrh = place("w_lr_hi", [P, KT, GRANK], r_w + 40960 + 1024, f32r)
        w_lrl = place("w_lr_lo", [P, KT, GRANK], r_w + 40960 + 2048, f32r)
        lr = place("lr", [P, NT, GRANK], r_u + KT * S * 4 + 8 * S * 4 + 4096)
        lrT = place("lr_T", [GRANK, S], r_u + KT * S * 4 + 8 * S * 4 + 4096 + 128)
        w_g = place("w_gate", [GRANK, GH * GDK], r_s + 8192)
        acc_start = place("ada_acc_start", [P, NCOL], r_w + 40960)
        acc_gla = place("ada_acc_gla", [P, 8, NCOL], r_aux)
        acc_att = [place("ada_acc_att0", [P, NCOL], r_s + 10240),
                   place("ada_acc_att1", [P, NCOL], r_u + (KT - 2) * S * 4)]
        mix_accs = {0: [acc_gla[:, 7, :], ada_acc] + [acc_gla[:, k, :] for k in range(3)], 1: [ada_acc] + acc_att}
        b_g = place("b_gate", [P, GH * GDK], r_s + 10240)
        dT = place("pool_T", [P, 2, 2, S], r_s + 4096)
        qkT = place("qk_T", [P, 2, 2 * S], r_s)
        prob = place("prob", [P, 2, 3 * P], r_s + 4096)
        probT = place("prob_T", [P, 2, 3 * P], r_s + 7168)

        def cst(i):
            return consts[:, i * P:(i + 1) * P]

        ident, rev, sum_inc, sum_suf, ones = (cst(i) for i in range(5))
        mask_q, mask_k = consts[0:1, 5 * P:6 * P], consts[0:1, 6 * P:7 * P]
        C_CONV = 2 * 96
        C_POOL = C_CONV + DEPTH * 4 * FT
        C_NORM = C_POOL + 8
        bn = small[:, 0:48].rearrange("p (t c s) -> p t c s", t=2, c=4)
        mv = small[:, 48:52].rearrange("p (t s) -> p t s", t=2)
        var, sd, rs, t1 = (small[:, 52 + 2 * i:54 + 2 * i] for i in range(4))
        gbn = small[:, 64:112].rearrange("p (h s) -> p h s", h=8)
        gmv = small[:, 112:128].rearrange("p (h s) -> p h s", h=8)
        gvar, gsd, grs, gt = (small[:, 128 + 8 * i:136 + 8 * i] for i in range(4))
        decay = small[:, 160:176].rearrange("p (h c) -> p h c", h=4)
        nmax = small[:, 176:180].rearrange("p (b t) -> p b t", b=2)
        rsum = small[:, 180:184].rearrange("p (b t) -> p b t", b=2)
        rinv = small[:, 184:188].rearrange("p (b t) -> p b t", b=2)

        bank = [ctx.enter_context(nc.psum_tensor(f"bank{i}", [P, NCOL], f32)) for i in range(8)]
        T = bank[4:6]
        ada_p = bank[6]

        sems = {}

        def sem(name):
            if name not in sems:
                sems[name] = ctx.enter_context(nc.semaphore(name))
            return sems[name]

        w_loaded = [sem(f"w_loaded{i}") for i in range(RAW_SLOTS)]
        w_hi = sem("w_hi_done")
        w_lo = sem("w_lo_done")
        wh_used = sem("w_hi_used")
        w_used = sem("w_used")
        acc_free = sem("acc_free")
        a_loaded = [sem(f"ada_loaded{i}") for i in range(ADA_SLOTS)]
        a_step = sem("ada_step")
        a_sum = sem("ada_summed")
        a_out = sem("ada_out")
        A0 = 2 * ADA_SLOTS

        t_full = sem("t_full")
        t_free = sem("t_free")
        u32_done = sem("u32_done")
        u_hi_done = sem("u_hi_done")
        u_ready = sem("u_ready")
        U_FIRST, U_MIX, U_LN, U_ATT = 0, 8, {0: 16, 1: 24, 2: 48}, 32
        T_X, T_MIX, T_LN = 0, 8, {0: 16, 1: 24, 2: 32}
        h_T = sem("hid_T")
        h_bias = sem("hid_bias")
        h_tap = sem("hid_tap")
        h_conv = sem("hid_conv")
        h_gelu = sem("hid_gelu")
        h_mul = sem("hid_mul")
        h_hi = sem("hid_hi_done")
        h_lo = sem("hid_lo_done")
        y_gated = sem("y_gated")
        y_sum = sem("y_sum")
        y_done = sem("y_done")

        H0 = {"up_a": 0, "up_b": FT_A // 2}
        H_LAYER = FT_A // 2 + FT_B // 2 + 1
        Y0 = {(0, "out"): 0, (0, "down_a"): 4, (0, "down_b"): 8, (1, "o"): 12, (1, "down_a"): 16,
              (1, "down_b"): 20}
        ADA = {(0, "in", 0): (0, 2, 0, 1), (0, "in", 4): (0, 2, 2, 1), (0, "out", 0): (0, 4, 2, 1),
               (0, "up_a", 1): (0, 5, 0, 1), (0, "down_a", 0): (1, 1, 0, 1), (0, "up_b", 1): (1, 0, 0, 1),
               (0, "up_b", 9): (1, 4, 0, 1),
               (0, "down_b", 0): (1, 1, 2, 1), (1, "qkv", 0): (1, 3, 0, 1), (1, "qkv", 4): (1, 2, 0, 1),
               (1, "qkv", 8): (1, 2, 2, 1), (1, "o", 0): (1, 3, 2, 1), (1, "up_a", 1): (1, 5, 0, 1)}
        MIX = {0: [(0, 3, 1), (0, 3, 2), (0, 3, 3), (0, 4, 0), (0, 4, 1)], 1: [(1, 4, n) for n in range(1, 4)]}
        GLA_FIRST = (0, 3, 0, PH[0, "mix"]["block"])
        MIX_FIRST = {0: PH[0, "mix"]["block"] + 1, 1: PH[1, "mix"]["block"]}
        GATE_NO = {(0, 2): 1, (0, 5): 2, (1, 2): 3, (1, 5): 4}
        ROW_SRC = 13

        block = ctx.enter_context(nc.Block())

        def pairs(e, lo, hi, body):
            n = (hi - lo) // 2
            assert 2 * n == hi - lo
            if n == 1:
                body(lo, 0)
                body(lo + 1, 0)
            elif n:
                with e.Fori(0, n) as i:
                    body(lo, i)
                    body(lo + 1, i)

        def ada_of(key, lo, c0, i):
            src = ADA.get((*key, lo))
            if src is None:
                return None
            layer, part, n0, rate = src
            at = i if rate == 1 else 2 * i + (c0 - lo)
            before = lo // 2 if rate == 1 else lo
            rows_here = KT // 2 * rate
            return ((layer, part, n0 + at, PH[key]["block"] + before + at),
                    (c0 - lo) * rows_here if rate == 1 else 0, rows_here)

        def unit_no(ph, c0, i, j):
            u = ph["unit"] + c0 * ph["n"] + j
            return u, u + 2 * ph["n"] * i

        def ada_rows(e, ns, acc, m, lo, hi):
            for r in range(lo, hi):
                half = r // 2
                if r % 2 == 0:
                    e.wait_ge(a_loaded[half % ADA_SLOTS], 32 * m + 16 * (half // ADA_SLOTS + 1))
                w = ada_w[:, half % ADA_SLOTS, r % 2, :]
                if r == 0:
                    ns.tensor_scalar(acc[:, :], w, silu_c[:, 0:1], None, ALU.mult).then_inc(a_step, 1)
                else:
                    e.wait_ge(a_step, m * KT + (A0 + r))
                    ns.scalar_tensor_tensor(acc[:, :], w, silu_c[:, r:r + 1], acc[:, :],
                                            ALU.mult, ALU.add).then_inc(a_step, 1)

        @block.sync
        def _(sp):
            def load_unit(ph, c0, i, j, halves):
                u, un = unit_no(ph, c0, i, j)
                sp.wait_ge(w_lo, un + 1)
                for dst, src in halves(raw[:, u % RAW_SLOTS, :]):
                    sp.dma_start(dst, src).then_inc(w_loaded[u % RAW_SLOTS], 16)

            def load_half(blk, half):
                layer, part, n, m = blk
                sp.wait_ge(a_step, m * KT + 2 * half + 2)
                w = A["w_ada"][layer].rearrange("(k p) (s n c) -> p k s n c", p=P, s=6, n=4)
                sp.dma_start(ada_w[:, half % ADA_SLOTS], w[:, 2 * half:2 * half + 2, part, n, :]
                             ).then_inc(a_loaded[half % ADA_SLOTS], 16)

            def phase(key, lo, hi, mix=False):
                layer, name = key
                ph = PH[key]
                first = [sum(ph["kts"][:j]) for j in range(ph["n"])]
                base = {"down_b": FT_A}.get(name, 0)
                if name in ("up_a", "up_b"):
                    f0 = 0 if name == "up_a" else FT_A * P
                    f1 = f0 + (FT_A if name == "up_a" else FT_B - 1) * P
                    w = A["w_up"][layer].rearrange("(k p) (s f) -> p k s f", p=P, s=2)
                    w = w[:, :, :, f0:f1].rearrange("p k s (c f) -> p k s c f", f=2 * P)
                else:
                    w = {"in": lambda: A["w_in_ab"][0][:, 0:OFF_LR], "out": lambda: A["w_out_ab"][0],
                         "qkv": lambda: A["w_qkv"][0], "o": lambda: A["w_o"][0],
                         "down_a": lambda: A["w_down"][layer], "down_b": lambda: A["w_down"][layer]}[name]()
                    w = w.rearrange("(k p) (c n) -> p k c n", p=P, n=NCOL)
                after = {(4, 8): (0, 2, 4, 8), (4, 4): (0, 1, 3, 4), (6, 4): (0, 1, 2, 3, 4, 4)}

                def body(c0, i):
                    beside, c = ada_of(key, lo, c0, i), 2 * i + c0
                    for j in range(ph["n"]):
                        k = ph["kts"][j]
                        if name in ("up_a", "up_b"):
                            load_unit(ph, c0, i, j, lambda r: [
                                (r.rearrange("p (k s f) -> p k s f", k=k, s=2)[:, :, s, :],
                                 w[:, 4 * j:4 * j + 4, s, c, :]) for s in range(2)])
                        else:
                            k0, cut = base + first[j], (k + 1) // 2
                            load_unit(ph, c0, i, j, lambda r: [
                                (r[:, a * NCOL:b * NCOL].rearrange("p (k n) -> p k n", n=NCOL),
                                 w[:, k0 + a:k0 + b, c, :]) for a, b in ((0, cut), (cut, k))])
                        if mix and j == 1 and c0 == lo and i == 0:
                            for blk in [GLA_FIRST] * (layer == 0) + [
                                    (*b, MIX_FIRST[layer] + n) for n, b in enumerate(MIX[layer])]:
                                for half in range(ADA_HALVES):
                                    load_half(blk, half)
                        if beside and j:
                            blk, row, n_rows = beside
                            so_far = after[ph["n"], n_rows // 2]
                            for half in range(so_far[j - 1], so_far[j]):
                                load_half(blk, row // 2 + half)
                if hi - lo == 1:
                    body(lo, 0)
                elif mix:
                    for c in range(lo, hi):
                        body(lo + (c - lo) % 2, (c - lo) // 2)
                else:
                    pairs(sp, lo, hi, body)

            def gate_load(layer, part, uses):
                if uses:
                    sp.wait_ge(y_done, uses)
                sp.dma_start(gate[:, :], A["b_ada"][layer:layer + 1, part * D:(part + 1) * D].broadcast_to((P, D))
                             ).then_inc(sem("gate_in"), 16)

            def ln_load(s):
                layer, which = divmod(s, 2)
                if s:
                    sp.wait_ge(sem("ln_done"), s)
                for k, name in enumerate(("ln_g", "ln_b")):
                    sp.dma_start(lnp[:, k, :], A[name][layer, which:which + 1, :].broadcast_to((P, D))
                                 ).then_inc(sem("ln_in"), 16)

            def mlp(layer, uses):
                phase((layer, "up_a"), 0, 1)
                gate_load(layer, 5, uses)
                phase((layer, "up_a"), 1, 9)
                phase((layer, "up_a"), 9, 10)
                phase((layer, "down_a"), 0, 4)
                phase((layer, "up_b"), 0, 1)
                phase((layer, "up_b"), 1, 9)
                phase((layer, "up_b"), 9, 11)
                w = A["w_up"][layer].rearrange("(k p) (s f) -> p k s f", p=P, s=2)[:, :, :, F - P:F]
                for j in range(2):
                    load_unit(PH[layer, "up_b"], 11, 0, j, lambda r: [
                        (r.rearrange("p (k s f) -> p k s f", k=8, s=2)[:, :, s, :], w[:, 8 * j:8 * j + 8, s, :])
                        for s in range(2)])
                phase((layer, "down_b"), 0, 4)

            sp.dma_start(rows[0:KT, ROW_SRC - 1, :], A["c"][0].rearrange("(r c) -> r c", c=P)
                         ).then_inc(sem("c_in"), 16)
            sp.dma_start(consts[:, :], A["consts"]).then_inc(sem("const_in"), 16)
            for half in range(ADA_HALVES):
                load_half((0, 0, 0, 0), half)
            row_list = [A["b_ada"][l] for l in range(DEPTH)]
            for l in range(DEPTH):
                row_list += [A["conv_w"][l, i] for i in range(3)] + [A["conv_b"][l]]
            row_list += [A["pool_scale"][0], A["gla_norm_g"][0]]
            for i, src in enumerate(row_list):
                sp.dma_start(rows[0:src.shape[0] // P, i, :], src.rearrange("(r c) -> r c", c=P)
                             ).then_inc(sem("rows_in"), 16)
            for half in range(ADA_HALVES):
                load_half((0, 0, 1, 1), half)
            sp.dma_start(x[:, :, :], A["x"][0].rearrange("(t p) n -> p t n", p=P)).then_inc(sem("x_in"), 16)
            for n in (2, 3):
                for half in range(ADA_HALVES):
                    load_half((0, 0, n, n), half)
            with sp.Fori(0, 4) as n:
                for half in range(ADA_HALVES):
                    load_half((0, 1, n, n + 4), half)
            gate_load(0, 2, 0)
            phase((0, "in"), 0, 4)
            sp.dma_start(w_lr[:, :, :], A["w_in_ab"][0][:, OFF_LR:OFF_LR + GRANK].rearrange("(k p) n -> p k n", p=P)
                         ).then_inc(sem("lr_in"), 16)
            sp.dma_start(w_g[:, :], A["w_gate_lr"][0]).then_inc(sem("gla_in"), 16)
            sp.dma_start(b_g[:, :], A["b_gate"][0:1, :].broadcast_to((P, GH * GDK))).then_inc(sem("gla_in"), 16)
            sp.dma_start(band[:, :, :], A["band"]).then_inc(sem("pool_in"), 16)
            for g in range(4):
                sp.dma_start(w_pool[:, g], A["w_pool"][0, g].rearrange("(k p) n -> p k n", p=P)
                             ).then_inc(sem("pool_in"), 16)
            phase((0, "in"), 4, 8)
            phase((0, "out"), 0, 4, mix=True)
            ln_load(0)
            mlp(0, 4)
            ln_load(1)
            phase((1, "qkv"), 0, 4)
            sp.wait_ge(sem("ln_done"), 2)
            rb = A["rel_bias"]
            sp.dma_start(toep[:, :, :], bass.AP(rb.tensor, REL - 127, [[1, P], [2 * REL + 1, AH], [1, S]])
                         ).then_inc(sem("toep_in"), 16)
            gate_load(1, 2, 12)
            phase((1, "qkv"), 4, 8)
            phase((1, "qkv"), 8, 12)
            phase((1, "o"), 0, 4, mix=True)
            sp.wait_ge(sem("att_s"), AH)
            ln_load(2)
            mlp(1, 16)
            ln_load(3)
            out_v = out[0].rearrange("(t p) n -> p t n", p=P)
            for n in range(4):
                sp.wait_ge(sem("ln_chunk"), 13 + n)
                sp.dma_start(out_v[:, :, n * NCOL:(n + 1) * NCOL], x[:, :, n * NCOL:(n + 1) * NCOL]
                             ).then_inc(sem("out_done"), 16)
            sp.wait_ge(sem("out_done"), 4 * 16)

        @block.scalar
        def _(act):
            def hi_unit(ph, c0, i, j, width):
                u, un = unit_no(ph, c0, i, j)
                act.wait_ge(w_loaded[u % RAW_SLOTS], 32 * (u // RAW_SLOTS + 1) + 16 * ph["n"] * i)
                if u >= HL_SLOTS:
                    act.wait_ge(wh_used, un - 1)
                    act.wait_ge(w_lo, un + (RAW_SLOTS - 1))
                nc.scalar.activation(whi[:, u % HL_SLOTS, 0:width], raw[:, u % RAW_SLOTS, 0:width], ACT.Copy
                                     ).then_inc(w_hi, 1)

            def steps(key, lo, hi, mid=None, tail=None, more=True):
                ph = PH[key]

                def body(c0, i):
                    own = 2 if key[1] == "up_b" and c0 == 11 else ph["n"]
                    for j in range(2, own + 2):
                        if j >= own and not more and c0 == hi - 1:
                            continue
                        width = ph["kts"][j] * NCOL if j < own else UNIT
                        hi_unit(ph, c0, i, j, width)
                        if j == 2 and mid:
                            mid(c0, i)
                    if tail:
                        tail(c0, i)
                if hi - lo == 1 or not more:
                    for c in range(lo, hi):
                        body(c, 0)
                else:
                    pairs(act, lo, hi, body)

            def chunk_end(key, c0, i):
                ph = PH[key]
                own = 2 if key[1] == "up_b" and c0 == 11 else ph["n"]
                act.wait_ge(w_used, unit_no(ph, c0, i, own)[1])

            def copy_out(dst, key):
                def tail(c0, i):
                    chunk_end(key, c0, i)
                    for t in range(NT):
                        ins = nc.scalar.activation(dst(t, c0, i), bank[2 * (c0 % 2) + t][:, :], ACT.Copy)
                    ins.then_inc(acc_free, 1)
                return tail

            def piece(g, t, src, kt, scale=None, bias=None, src_sbuf=False):
                act.wait_ge(u_ready, g + 1)
                slot = t % 2 if isinstance(t, int) else 0
                for k in range(2):
                    ins = nc.scalar.activation(u32[:, slot, k * S:(k + 1) * S], src(k), ACT.Identity,
                                               scale=scale(k), bias=bias(k) if bias else 0.0)
                ins.then_inc(u32_done, 1)
                act.wait_ge(u32_done, g + 1)
                if not src_sbuf:
                    pass
                nc.scalar.activation(uhi[:, kt:kt + 2, :], u32[:, slot, :].rearrange("p (k s) -> p k s", k=2),
                                     ACT.Copy).then_inc(u_hi_done, 1)

            act.wait_ge(sem("c_T"), 1)
            nc.scalar.activation(silu_c[:, :], bank[2][:, 0:KT], ACT.Silu).then_inc(sem("silu_c"), 1)
            for v in range(8):
                act.wait_ge(t_full, T_X + v + 1)
                nc.scalar.activation(xT[:, 2 * v:2 * v + 2, :], T[v % 2].rearrange("p (k s) -> p k s", k=2), ACT.Copy
                                     ).then_inc(t_free, 1)
            act.wait_ge(t_free, 2 + T_X + 8)
            with act.Fori(0, 4) as n:
                act.wait_ge(a_out, n + 6)
                for b in range(2):
                    g = 2 * n + b
                    act.wait_ge(u_ready, g + 1)
                    for k in range(2):
                        kt = 4 * n + (2 * b + k)
                        ins = nc.scalar.activation(u32[:, b, k * S:(k + 1) * S], xT[:, kt, :], ACT.Identity,
                                                   scale=mod[:, bass.ds(kt + KT, 1)], bias=mod[:, bass.ds(kt, 1)])
                    ins.then_inc(u32_done, 1)
                    act.wait_ge(u32_done, g + 1)
                    nc.scalar.activation(uhi[:, bass.ds(4 * n + 2 * b, 2), :],
                                         u32[:, b, :].rearrange("p (k s) -> p k s", k=2), ACT.Copy
                                         ).then_inc(u_hi_done, 1)
            hi_unit(PH[0, "in"], 0, 0, 0, UNIT)
            hi_unit(PH[0, "in"], 0, 0, 1, UNIT)

            def z_at(t, c0, i):
                return z[:, t, bass.ds(2 * NCOL * i + c0 * NCOL, NCOL)]
            steps((0, "in"), 0, 4, tail=copy_out(z_at, (0, "in")))
            steps((0, "in"), 4, 8, tail=copy_out(z_at, (0, "in")))

            act.wait_ge(sem("lr_in"), 16)
            nc.scalar.activation(w_lrh[:, :, :], w_lr[:, :, :], ACT.Copy).then_inc(sem("lr_hi"), 1)
            act.wait_ge(acc_free, 2 + 8)
            for t in range(NT):
                nc.scalar.activation(z[:, t, OFF_R:OFF_LR], z[:, t, OFF_R:OFF_LR], ACT.Silu).then_inc(sem("silu_r"), 1)

            def pool_T(g):
                if g >= 2:
                    act.wait_ge(t_full, T_MIX + g - 1)
                act.wait_ge(sem("pool_T"), g + 1)
                nc.scalar.activation(dT[:, g % 2], bank[g].rearrange("p (k s) -> p k s", k=2), ACT.Copy
                                     ).then_inc(sem("pool_T_out"), 1)

            def mix_piece(v, col):
                act.wait_ge(t_full, T_MIX + v + 1)
                act.wait_ge(u_ready, U_MIX + v + 1)
                for k in range(2):
                    ins = nc.scalar.activation(u32[:, v % 2, k * S:(k + 1) * S], T[v % 2][:, k * S:(k + 1) * S],
                                               ACT.Identity, scale=cols[:, col + k:col + k + 1])
                ins.then_inc(t_free, 1)
                act.wait_ge(t_free, 2 + T_MIX + v + 1)
                nc.scalar.activation(uhi[:, 2 * v:2 * v + 2, :], u32[:, v % 2, :].rearrange("p (k s) -> p k s", k=2),
                                     ACT.Copy).then_inc(u_hi_done, 1)
            pool_T(0)
            pool_T(1)
            mix_piece(0, C_POOL)
            mix_piece(1, C_POOL + 2)
            pool_T(2)
            pool_T(3)
            mix_piece(2, C_POOL + 4)
            mix_piece(3, C_POOL + 6)
            act.wait_ge(sem("gate_pre_out"), 1)
            nc.scalar.activation(kdec[:, :, :], loga[:, :, :], ACT.Abs).then_inc(sem("ls"), 1)
            act.wait_ge(sem("ls"), 1)
            nc.scalar.activation(kdec[:, :, :], kdec[:, :, :], ACT.Exp, scale=-1.0).then_inc(sem("ls"), 1)
            act.wait_ge(sem("ls"), 2)
            nc.scalar.activation(kdec[:, :, :], kdec[:, :, :], ACT.Ln, bias=1.0).then_inc(sem("ls"), 1)
            act.wait_ge(sem("qk_T"), 1)
            for j in range(2):
                nc.scalar.activation(qdT[:, 2 * j:2 * j + 2, :], bank[j].rearrange("p (h s) -> p h s", h=2), ACT.Copy,
                                     scale=float(GDK) ** -0.5)
                ins = nc.scalar.activation(kiT[:, 2 * j:2 * j + 2, :], bank[2 + j].rearrange("p (h s) -> p h s", h=2),
                                           ACT.Copy)
            ins.then_inc(sem("qk_T_out"), 1)
            act.wait_ge(sem("cum"), 1)
            for t in range(NT):
                nc.scalar.activation(kdec[:, t, :], bank[t][:, :], ACT.Exp).then_inc(sem("exp_suf"), 1)
            act.wait_ge(sem("exp_suf"), 2)
            for j in range(2):
                nc.scalar.activation(bank[j][:, :], bank[2 + j][:, :], ACT.Exp, scale=-1.0).then_inc(sem("exp_b"), 1)
            act.wait_ge(sem("exp_b"), 2)
            for j in range(2):
                nc.scalar.activation(bank[2 + j][:, :], bank[2 + j][:, :], ACT.Exp).then_inc(sem("exp_b"), 1)
            act.wait_ge(sem("gla_var"), 1)
            nc.scalar.activation(gsd, gvar, ACT.Sqrt).then_inc(sem("gla_sd"), 1)
            for v in range(4, 8):
                mix_piece(v, C_NORM + 2 * (v - 4))
            steps((0, "out"), 0, 4)

            def ln_and_u(s, shift):
                act.wait_ge(sem("ln_var"), s + 1)
                nc.scalar.activation(sd, var, ACT.Sqrt).then_inc(sem("ln_sd"), 1)
                if shift is None:
                    return
                for v in range(8):
                    act.wait_ge(t_full, T_LN[s] + v + 1)
                    act.wait_ge(u_ready, U_LN[s] + v + 1)
                    for k in range(2):
                        m = shift + 2 * v + k
                        ins = nc.scalar.activation(u32[:, v % 2, k * S:(k + 1) * S], T[v % 2][:, k * S:(k + 1) * S],
                                                   ACT.Identity, scale=mod[:, m + KT:m + KT + 1], bias=mod[:, m:m + 1])
                    ins.then_inc(t_free, 1)
                    act.wait_ge(t_free, 2 + T_LN[s] + v + 1)
                    nc.scalar.activation(uhi[:, 2 * v:2 * v + 2, :],
                                         u32[:, v % 2, :].rearrange("p (k s) -> p k s", k=2), ACT.Copy
                                         ).then_inc(u_hi_done, 1)

            def hidden(layer, name, c0, i, nf=2):
                q = H_LAYER * layer + H0[name] + c0 + 2 * i
                f = (0 if name == "up_a" else FT_A) + 2 * c0 + 4 * i
                col = C_CONV + layer * 4 * FT + f
                act.wait_ge(h_T, q + 1)
                for k in range(nf):
                    ins = nc.scalar.activation(gc[:, k, :], T[1][:, k * S:(k + 1) * S], ACT.Identity,
                                               scale=cols[:, bass.ds(col + 2 * FT + k, 1)],
                                               bias=cols[:, bass.ds(col + 3 * FT + k, 1)])
                ins.then_inc(h_bias, 1)
                act.wait_ge(h_conv, q + 1)
                nc.scalar.activation(gc[:, 0:nf, :], gc[:, 0:nf, :], ACT.Gelu_apprx_tanh).then_inc(h_gelu, 1)
                act.wait_ge(h_mul, q + 2)
                nc.scalar.activation(hhi[:, bass.ds(2 * c0 + 4 * i, nf), :], h32[:, 0:nf, :], ACT.Copy
                                     ).then_inc(h_hi, 1)

            def mlp(layer):
                for name in ("up_a", "up_b"):
                    key = (layer, name)
                    last = PH[key]["chunks"] - 1
                    out_h = copy_out(lambda t, c0, i: g_tok[:, t, :], key)
                    prev = lambda c0, i: hidden(layer, name, c0 - 1, i)
                    steps(key, 0, 1, tail=out_h)
                    steps(key, 1, 9, mid=prev, tail=out_h)
                    if name == "up_b":
                        steps(key, 9, 11, mid=prev, tail=out_h)
                    for c in range(last, last + 1):
                        if name == "up_b":
                            hidden(layer, name, c - 1, 0)
                            hi_unit(PH[key], c, 0, 2, UNIT)
                            hi_unit(PH[key], c, 0, 3, UNIT)
                            chunk_end(key, c, 0)
                            for t in range(NT):
                                ins = nc.scalar.activation(g_tok[:, t, 0:2 * P], bank[2 * (c % 2) + t][:, 0:2 * P],
                                                           ACT.Copy)
                            ins.then_inc(acc_free, 1)
                        else:
                            steps(key, c, c + 1, mid=prev, tail=out_h)
                    hidden(layer, name, last, 0, 1 if name == "up_b" else 2)
                    steps((layer, "down" + name[2:]), 0, 4, more=not (layer == DEPTH - 1 and name == "up_b"))

            ln_and_u(0, 3 * KT)
            mlp(0)
            ln_and_u(1, 96)
            steps((1, "qkv"), 0, 12, tail=copy_out(
                lambda t, c0, i: qkv[:, t, bass.ds(2 * NCOL * i + c0 * NCOL, NCOL)], (1, "qkv")))
            for s in range(AH + 3):
                if s < AH:
                    act.wait_ge(sem("att_T"), s + 1)
                    nc.scalar.activation(qkT[:, s % 2, 0:S], T[s % 2][:, 0:S], ACT.Copy, scale=float(AD) ** -0.5)
                    nc.scalar.activation(qkT[:, s % 2, S:2 * S], T[s % 2][:, S:2 * S], ACT.Copy
                                         ).then_inc(sem("att_qk"), 1)
                if 1 <= s <= AH:
                    h = s - 1
                    act.wait_ge(sem("att_max"), h + 1)
                    if h >= 2:
                        act.wait_ge(sem("att_pT"), h - 1)
                    sb = bank[6 + h % 2]
                    nc.scalar.activation(prob[:, h % 2, 0:P], sb[:, 0:P], ACT.Exp, bias=nmax[:, h % 2, 0:1],
                                         accum_out=rsum[:, h % 2, 0:1])
                    nc.scalar.activation(prob[:, h % 2, P:3 * P], sb[:, P:3 * P], ACT.Exp, bias=nmax[:, h % 2, 1:2],
                                         accum_out=rsum[:, h % 2, 1:2]).then_inc(sem("att_exp"), 1)
                if s >= 3:
                    h = s - 3
                    act.wait_ge(sem("att_o"), h + 1)
                    nc.scalar.activation(uhi[:, h, :], bank[2 + h % 2][:, 0:S], ACT.Copy).then_inc(u_hi_done, 1)
            steps((1, "o"), 0, 4)
            ln_and_u(2, 96 + 3 * KT)
            mlp(1)
            ln_and_u(3, None)

        @block.vector
        def _(dve):
            chained = [0]

            def link(ins):
                chained[0] += 1
                ins.then_inc(sem("dve_chain"), 1)
                dve.wait_ge(sem("dve_chain"), chained[0])

            def lo_unit(ph, c0, i, j, width):
                u, un = unit_no(ph, c0, i, j)
                dve.wait_ge(w_hi, un + 1)
                if u >= HL_SLOTS:
                    dve.wait_ge(w_used, un - 1)
                nc.vector.tensor_tensor(wlo[:, u % HL_SLOTS, 0:width], raw[:, u % RAW_SLOTS, 0:width],
                                        whi[:, u % HL_SLOTS, 0:width].bitcast(f32), ALU.subtract).then_inc(w_lo, 1)

            def ada_evac(blk):
                layer, part, n, m = blk
                dve.wait_ge(a_sum, m + 1)
                if part in (2, 5):
                    dve.wait_ge(sem("gate_in"), 16 * GATE_NO[layer, part])
                    to = gate[:, bass.ds(n * NCOL, NCOL)]
                    nc.vector.scalar_tensor_tensor(to, ada_p[:, :], 1.0, to, ALU.add, ALU.add).then_inc(a_out, 1)
                else:
                    at = bass.ds(n * 4 + (96 * layer + KT * part), 4)
                    nc.vector.scalar_tensor_tensor(mod[:, at], ada_p[:, 0:4], 1.0 if part in (1, 4) else 0.0,
                                                   cols[:, at], ALU.add, ALU.add).then_inc(a_out, 1)

            mixed = {0: 0, 1: 0}

            def mix_rows(layer, n):
                for r in range(mixed[layer], mixed[layer] + n):
                    k, row = divmod(r, KT)
                    ada_rows(dve, nc.vector, mix_accs[layer][k], MIX_FIRST[layer] + k, row, row + 1)
                mixed[layer] += n

            def ada_evac_mix(layer):
                dve.wait_ge(a_sum, MIX_FIRST[layer] + len(MIX[layer]))
                for part in sorted({b[1] for b in MIX[layer]}):
                    mine = [k for k, b in enumerate(MIX[layer]) if b[1] == part]
                    to = 96 * layer + KT * part + 4 * MIX[layer][mine[0]][2]
                    at, n = slice(to, to + 4 * len(mine)), 4 * mine[0]
                    ins = nc.vector.scalar_tensor_tensor(
                        mod[:, at], (ada_p if layer == 0 else T[0])[:, n:n + 4 * len(mine)],
                        1.0 if part in (1, 4) else 0.0, cols[:, at], ALU.add, ALU.add)
                ins.then_inc(a_out, len(MIX[layer]))

            def steps(key, lo, hi, mid=None, tail=None, more=True):
                ph = PH[key]
                split = {(4, 16): (6, 5, 5, 0), (4, 8): (3, 3, 2, 0), (6, 8): (2, 2, 2, 1, 1, 0)}

                def body(c0, i):
                    beside = ada_of(key, lo, c0, i)
                    own = 2 if key[1] == "up_b" and c0 == 11 else ph["n"]
                    for j in range(2, own + 2):
                        if j < own or more or c0 != hi - 1:
                            lo_unit(ph, c0, i, j, ph["kts"][j] * NCOL if j < own else UNIT)
                        if j == 2 and mid:
                            mid(c0, i)
                        if beside:
                            blk, row, n_rows = beside
                            now = split[ph["n"], n_rows]
                            row += sum(now[:j - 2])
                            ada_rows(dve, nc.vector, ada_acc, blk[3], row, row + now[j - 2])
                    if tail:
                        tail(c0, i)
                    if beside and beside[1] + beside[2] == KT:
                        ada_evac(beside[0])
                if hi - lo == 1 or not more:
                    for c in range(lo, hi):
                        body(c, 0)
                else:
                    pairs(dve, lo, hi, body)

            def u_lo(g, dst_kt, slot):
                dve.wait_ge(u_hi_done, g + 1)
                nc.vector.tensor_tensor(ulo[:, dst_kt, :], u32[:, slot, :].rearrange("p (k s) -> p k s", k=2),
                                        uhi[:, dst_kt, :].bitcast(f32), ALU.subtract).then_inc(u_ready, 1)

            def y_out(key, first, stats):
                ph = PH[key]

                def tail(c0, i):
                    y = Y0[key] + c0 + 2 * i
                    cs = bass.ds(2 * NCOL * i + c0 * NCOL, NCOL)
                    dve.wait_ge(w_used, unit_no(ph, c0, i, ph["n"])[1])
                    for t in range(NT):
                        ins = nc.vector.tensor_tensor(y_tmp[:, t, :], bank[2 * (c0 % 2) + t][:, :], gate[:, cs],
                                                      ALU.mult)
                    ins.then_inc(acc_free, 1)
                    dve.wait_ge(acc_free, ph["chunk"] + c0 + 2 * i + 3)
                    for t in range(NT):
                        ins = nc.vector.scalar_tensor_tensor(x[:, t, cs], x[:, t, cs], ALPHA if first else 1.0,
                                                             y_tmp[:, t, :], ALU.mult, ALU.add)
                    ins.then_inc(y_sum, 1)
                    dve.wait_ge(y_sum, y + 1)
                    if stats:
                        for t in range(NT):
                            ins = nc.vector.bn_stats(bn[:, t, bass.ds(c0 + 2 * i, 1), :].rearrange("p a s -> p (a s)"),
                                                     x[:, t, cs])
                        ins.then_inc(y_done, 1)
                    else:
                        nc.vector.tensor_copy(t1[:, 0:1], mod[:, 0:1]).then_inc(y_done, 1)
                return tail

            def rstd(v, sdv, r, t, var_sem, sd_sem, n):
                dve.wait_ge(sem(sd_sem), n)
                link(nc.vector.reciprocal(r, sdv))
                link(nc.vector.tensor_tensor(t, r, r, ALU.mult))
                link(nc.vector.tensor_tensor(t, t, v, ALU.mult))
                link(nc.vector.tensor_scalar(t, t, -0.5, 1.5, ALU.mult, ALU.add))
                link(nc.vector.tensor_tensor(r, r, t, ALU.mult))

            def layer_norm(s, last):
                dve.wait_ge(y_done, {0: 4, 1: 12, 2: 16, 3: 24}[s])
                for t in range(NT):
                    ins = nc.vector.bn_aggr(mv[:, t, :], bn[:, t].rearrange("p c s -> p (c s)"))
                link(ins)
                nc.vector.tensor_scalar(var, mv[:, :, 1], EPS, None, ALU.add).then_inc(sem("ln_var"), 1)
                dve.wait_ge(sem("ln_var"), s + 1)
                rstd(var, sd, rs, t1, "ln_var", "ln_sd", s + 1)
                dve.wait_ge(sem("ln_in"), 32 * (s + 1))
                done = 0
                for n in range(4):
                    cs = slice(n * NCOL, (n + 1) * NCOL)
                    for t in range(NT):
                        ins = nc.vector.scalar_tensor_tensor(x[:, t, cs], x[:, t, cs], mv[:, t, 0:1], lnp[:, 0, cs],
                                                             ALU.subtract, ALU.mult)
                    link(ins)
                    for t in range(NT):
                        ins = nc.vector.scalar_tensor_tensor(x[:, t, cs], x[:, t, cs], rs[:, t:t + 1], lnp[:, 1, cs],
                                                             ALU.mult, ALU.add)
                    ins.then_inc(sem("ln_chunk"), 1)
                    if n and not last:
                        for v in (2 * n - 2, 2 * n - 1):
                            u_lo(U_LN[s] + v, slice(2 * v, 2 * v + 2), v % 2)
                if not last:
                    dve.wait_ge(sem("ln_chunk"), 4 * s + 4)
                    for v in (6, 7):
                        u_lo(U_LN[s] + v, slice(2 * v, 2 * v + 2), v % 2)
                    nc.vector.tensor_copy(t1[:, 0:1], mod[:, 0:1]).then_inc(sem("ln_done"), 1)

            def hidden(layer, name, c0, i, nf=2):
                q = H_LAYER * layer + H0[name] + c0 + 2 * i
                f = (0 if name == "up_a" else FT_A) + 2 * c0 + 4 * i
                col = C_CONV + layer * 4 * FT + f
                dve.wait_ge(h_bias, q + 1)
                for tap, lag, s in ((1, 1, h_tap), (0, 2, h_conv)):
                    for k in range(nf):
                        ins = nc.vector.scalar_tensor_tensor(
                            gc[:, k, lag:S], T[1][:, k * S:(k + 1) * S - lag],
                            cols[:, bass.ds(col + tap * FT + k, 1)], gc[:, k, lag:S], ALU.mult, ALU.add)
                    ins.then_inc(s, 1)
                    if tap:
                        dve.wait_ge(h_tap, q + 1)
                dve.wait_ge(h_gelu, q + 1)
                nc.vector.tensor_tensor(h32[:, 0:nf, :], T[0][:, 0:nf * S].rearrange("p (k s) -> p k s", k=nf),
                                        gc[:, 0:nf, :], ALU.mult).then_inc(h_mul, 1)
                dve.wait_ge(h_hi, q + 1)
                at = bass.ds(2 * c0 + 4 * i, nf)
                nc.vector.tensor_tensor(hlo[:, at, :], h32[:, 0:nf, :], hhi[:, at, :].bitcast(f32), ALU.subtract
                                        ).then_inc(h_lo, 1)

            def mlp(layer):
                for name in ("up_a", "up_b"):
                    key = (layer, name)
                    last = PH[key]["chunks"] - 1
                    prev = lambda c0, i: hidden(layer, name, c0 - 1, i)
                    steps(key, 0, 1)
                    steps(key, 1, 9, mid=prev)
                    if name == "up_b":
                        steps(key, 9, 11, mid=prev)
                    for c in range(last, last + 1):
                        if name == "up_b":
                            hidden(layer, name, c - 1, 0)
                            lo_unit(PH[key], c, 0, 2, UNIT)
                            lo_unit(PH[key], c, 0, 3, UNIT)
                        else:
                            steps(key, c, c + 1, mid=prev)
                    hidden(layer, name, last, 0, 1 if name == "up_b" else 2)
                    down = (layer, "down" + name[2:])
                    steps(down, 0, 4, tail=y_out(down, name == "up_a", name == "up_b"),
                          more=not (layer == DEPTH - 1 and name == "up_b"))

            nc.vector.memset(t1[:, 0:1], 0.0).then_inc(w_lo, RAW_SLOTS)
            nc.vector.memset(t1[:, 1:2], 0.0).then_inc(a_step, A0)
            nc.vector.memset(var[:, 0:1], 0.0).then_inc(a_out, 1)
            nc.vector.memset(var[:, 1:2], 0.0).then_inc(u_ready, 2)
            nc.vector.memset(sd[:, 0:1], 0.0).then_inc(t_free, 2)
            nc.vector.memset(sd[:, 1:2], 0.0).then_inc(acc_free, 2)
            nc.vector.memset(rs[:, 0:1], 0.0).then_inc(h_mul, 1)
            def start_acc(b):
                return acc_start if b % 2 else ada_acc

            dve.wait_ge(sem("silu_c"), 1)
            ada_rows(dve, nc.vector, ada_acc, 0, 0, KT)
            dve.wait_ge(sem("rows_T"), 1)
            nc.vector.tensor_copy(cols[:, 0:2 * 96 + 4 * FT], bank[0][:, 0:2 * 96 + 4 * FT]).then_inc(sem("cols_in"), 1)
            nc.vector.tensor_copy(cols[:, 2 * 96 + 4 * FT:n_cols], bank[1][:, 0:n_cols - 2 * 96 - 4 * FT]
                                  ).then_inc(sem("cols_in"), 1)
            dve.wait_ge(sem("cols_in"), 2)
            with dve.Fori(0, 2) as i:
                for b in (1, 2):
                    ada_rows(dve, nc.vector, start_acc(b), b + 2 * i, 0, KT)
                    ada_evac((0, 0, b - 1 + 2 * i, b - 1 + 2 * i))
            for b in range(5, 10):
                if b < 8:
                    ada_rows(dve, nc.vector, start_acc(b), b, 0, KT)
                if b >= 6:
                    for v in (2 * (b - 6), 2 * (b - 6) + 1):
                        u_lo(v, slice(2 * v, 2 * v + 2), v % 2)
                if b <= 8:
                    ada_evac((0, 1, b - 5, b - 1))
            lo_unit(PH[0, "in"], 0, 0, 0, UNIT)
            lo_unit(PH[0, "in"], 0, 0, 1, UNIT)
            steps((0, "in"), 0, 4)
            steps((0, "in"), 4, 8)

            dve.wait_ge(sem("lr_hi"), 1)
            nc.vector.tensor_tensor(w_lrl[:, :, :], w_lr[:, :, :], w_lrh[:, :, :].bitcast(f32), ALU.subtract
                                    ).then_inc(sem("lr_lo"), 1)
            ada_rows(dve, nc.vector, ada_acc, GLA_FIRST[3], 0, KT)
            dve.wait_ge(sem("lr"), 1)
            nc.vector.tensor_copy(lr[:, :, :], bank[7][:, 0:NT * GRANK].rearrange("p (t r) -> p t r", t=NT)
                                  ).then_inc(sem("lr_out"), 1)
            ada_evac(GLA_FIRST)
            dve.wait_ge(sem("lr_T"), 1)
            nc.vector.tensor_copy(lrT[:, :], bank[7][0:GRANK, 0:S]).then_inc(sem("lr_T_out"), 1)
            mix_rows(0, 6)

            def mix_lo(v):
                u_lo(U_MIX + v, slice(2 * v, 2 * v + 2), v % 2)
            mix_lo(0)
            mix_lo(1)
            mix_rows(0, 6)
            dve.wait_ge(sem("gate_pre"), 1)
            dve.wait_ge(sem("gla_in"), 32)
            for t in range(NT):
                ins = nc.vector.tensor_tensor(loga[:, t, :], bank[6 + t][:, :], b_g[:, :], ALU.add)
            ins.then_inc(sem("gate_pre_out"), 1)
            mix_rows(0, 4)
            mix_lo(2)
            mix_lo(3)
            mix_rows(0, 8)
            dve.wait_ge(sem("gate_pre_out"), 1)
            dve.wait_ge(sem("ls"), 3)
            nc.vector.scalar_tensor_tensor(loga[:, :, :].rearrange("p t c -> p (t c)"),
                                           loga[:, :, :].rearrange("p t c -> p (t c)"), 0.0,
                                           kdec[:, :, :].rearrange("p t c -> p (t c)"), ALU.min, ALU.subtract
                                           ).then_inc(sem("log_a"), 1)
            nc.vector.memset(scT[:, :, :, :], 0.0).then_inc(sem("sc_zero"), 1)
            mix_rows(0, 8)
            dve.wait_ge(t_full, T_MIX + 4)
            mix_rows(0, 8)
            dve.wait_ge(sem("exp_suf"), 2)
            nc.vector.tensor_tensor(kdec[:, :, :], kdec[:, :, :], z[:, :, OFF_K:OFF_V], ALU.mult).then_inc(sem("kdec"), 1)
            mix_rows(0, 4)
            dve.wait_ge(sem("qk_T_out"), 1)
            dve.wait_ge(sem("exp_b"), 4)
            for j in range(2):
                hs = slice(2 * j, 2 * j + 2)
                e_b = bank[2 + j].rearrange("p (h s) -> p h s", h=2)
                nc.vector.tensor_copy(decay[:, hs, :], e_b[:, :, CH - 1::CH])
                nc.vector.tensor_tensor(qdT[:, hs, :], qdT[:, hs, :], e_b, ALU.mult)
                ins = nc.vector.tensor_tensor(kiT[:, hs, :], kiT[:, hs, :], bank[j].rearrange("p (h s) -> p h s", h=2),
                                              ALU.mult)
            ins.then_inc(sem("qk_dec"), 1)
            mix_rows(0, 8)
            dve.wait_ge(sem("qk_dec"), 1)
            dve.wait_ge(sem("scores"), 1)
            dve.wait_ge(sem("sc_zero"), 1)
            for t in range(NT):
                for h in range(GH):
                    ins = nc.vector.copy_predicated(scT[:, t, h, :], sum_inc.bitcast(i32),
                                                    bank[6 + t][:, h * P:(h + 1) * P])
            ins.then_inc(sem("scores_out"), 1)
            mix_rows(0, 14)
            dve.wait_ge(sem("outer"), 1)
            for j in range(2):
                ins = nc.vector.tensor_copy(state[:, 0, 2 * j:2 * j + 2, :],
                                            bank[j].rearrange("p (h v) -> p h v", h=2))
            link(ins)
            for c in (1, 2):
                for h in range(GH):
                    to = state[:, 1, h, :] if c == 1 else state3[:, h, :]
                    ins = nc.vector.scalar_tensor_tensor(to, state[:, c - 1, h, :], decay[:, h, c:c + 1],
                                                         bank[2 * c + h // 2][:, (h % 2) * GDV:(h % 2 + 1) * GDV],
                                                         ALU.mult, ALU.add)
                if c == 1:
                    link(ins)
            ins.then_inc(sem("states"), 1)
            mix_rows(0, 14)
            dve.wait_ge(sem("gla_o"), 1)
            for q in range(8):
                t, h = divmod(q, GH)
                ins = nc.vector.bn_stats(gbn[:, q, :], bank[2 * t + h // 2][:, (h % 2) * GDV:(h % 2 + 1) * GDV])
            link(ins)
            for q in range(8):
                ins = nc.vector.bn_aggr(gmv[:, q, :], gbn[:, q, :])
            link(ins)
            nc.vector.tensor_scalar(gvar, gmv[:, :, 1], EPS, None, ALU.add).then_inc(sem("gla_var"), 1)
            dve.wait_ge(sem("gla_var"), 1)
            rstd(gvar, gsd, grs, gt, "gla_var", "gla_sd", 1)
            dve.wait_ge(sem("silu_r"), 2)
            for q in range(8):
                t, h = divmod(q, GH)
                ins = nc.vector.scalar_tensor_tensor(
                    z[:, t, OFF_Q + h * GDV:OFF_Q + (h + 1) * GDV], bank[2 * t + h // 2][:, (h % 2) * GDV:(h % 2 + 1) * GDV],
                    gmv[:, q, 0:1], z[:, t, OFF_R + h * GDV:OFF_R + (h + 1) * GDV], ALU.subtract, ALU.mult)
            link(ins)
            for h in range(GH):
                for t in range(NT):
                    o = z[:, t, OFF_Q + h * GDV:OFF_Q + (h + 1) * GDV]
                    ins = nc.vector.tensor_scalar(o, o, grs[:, t * GH + h:t * GH + h + 1], None, ALU.mult)
                ins.then_inc(sem("y_b"), 1)
            dve.wait_ge(sem("y_b"), 4)
            ada_evac_mix(0)
            for v in range(4, 8):
                mix_lo(v)
            steps((0, "out"), 0, 4, tail=y_out((0, "out"), True, True))
            layer_norm(0, False)
            mlp(0)
            layer_norm(1, False)
            steps((1, "qkv"), 0, 4)
            steps((1, "qkv"), 4, 8)
            steps((1, "qkv"), 8, 12)
            for s in range(1, AH + 3):
                if s <= AH:
                    h = s - 1
                    dve.wait_ge(sem("att_s"), h + 1)
                    sb = bank[6 + h % 2]
                    nc.vector.reduce_max(nmax[:, h % 2, 0:1], sb[:, 0:P], AX.X, negate=True)
                    nc.vector.reduce_max(nmax[:, h % 2, 1:2], sb[:, P:3 * P], AX.X, negate=True
                                         ).then_inc(sem("att_max"), 1)
                if 2 <= s <= AH + 1:
                    h = s - 2
                    dve.wait_ge(sem("att_pT"), h + 1)
                    nc.vector.tensor_copy(probT[:, h % 2, :], bank[h % 2][:, 0:3 * P]).then_inc(sem("att_pT_out"), 1)
                mix_rows(1, min(4, len(MIX[1]) * KT - mixed[1]))
                if s <= AH:
                    h = s - 1
                    dve.wait_ge(sem("att_exp"), h + 1)
                    link(nc.vector.reciprocal(rinv[:, h % 2, :], rsum[:, h % 2, :]))
                    for a, b, t in ((0, P, 0), (P, 3 * P, 1)):
                        ins = nc.vector.tensor_scalar(prob[:, h % 2, a:b], prob[:, h % 2, a:b], rinv[:, h % 2, t:t + 1],
                                                      None, ALU.mult)
                    ins.then_inc(sem("att_p"), 1)
                if s == AH:
                    ada_evac_mix(1)
                if s >= 3:
                    h = s - 3
                    dve.wait_ge(u_hi_done, U_ATT + h + 1)
                    nc.vector.tensor_tensor(ulo[:, h, :], bank[2 + h % 2][:, 0:S], uhi[:, h, :].bitcast(f32),
                                            ALU.subtract).then_inc(u_ready, 1)
            steps((1, "o"), 0, 4, tail=y_out((1, "o"), True, True))
            layer_norm(2, False)
            mlp(1)
            layer_norm(3, True)

        @block.tensor
        def _(pe):
            def unit(ph, c0, i, j, parts, u_of, first, last, banks, after=None, late=None):
                u, un = unit_no(ph, c0, i, j)
                pe.wait_ge(w_hi, un + 1)
                if after is not None:
                    pe.wait_ge(u_ready, after)
                h, l = u_of
                width = UNIT // (8 if len(parts) == 8 else 4)
                slot = u % HL_SLOTS
                for n, (k, kt) in enumerate(parts):
                    if late is not None and kt == late[0]:
                        pe.wait_ge(h_lo, late[1])
                    w = whi[:, slot, k * width:(k + 1) * width]
                    for t in range(NT):
                        nc.tensor.matmul(banks[t][:, 0:width], h[:, kt, t * P:(t + 1) * P], w,
                                         start=first and n == 0, stop=False)
                        ins = nc.tensor.matmul(banks[t][:, 0:width], l[:, kt, t * P:(t + 1) * P], w,
                                               start=False, stop=False)
                ins.then_inc(wh_used, 1)
                pe.wait_ge(w_lo, un + (RAW_SLOTS + 1))
                for n, (k, kt) in enumerate(parts):
                    w = wlo[:, slot, k * width:(k + 1) * width]
                    for t in range(NT):
                        ins = nc.tensor.matmul(banks[t][:, 0:width], h[:, kt, t * P:(t + 1) * P], w,
                                               start=False, stop=last and n == len(parts) - 1)
                ins.then_inc(w_used, 1)

            def ada_sum_mix(layer):
                m = MIX_FIRST[layer]
                pe.wait_ge(a_step, (m + len(MIX[layer])) * KT + A0)
                pe.wait_ge(a_out, m + 1)
                to = ada_p if layer == 0 else T[0]
                for n, acc in enumerate(mix_accs[layer]):
                    for q in range(4):
                        ins = nc.tensor.matmul(to[:, 4 * n + q:4 * n + q + 1], acc[:, q * P:(q + 1) * P],
                                               ones[:, 0:1], start=True, stop=True)
                ins.then_inc(a_sum, len(MIX[layer]))

            def ada_sum(blk, acc=ada_acc):
                layer, part, n, m = blk
                pe.wait_ge(a_step, m * KT + (A0 + KT))
                pe.wait_ge(a_out, m + 1)
                if part in (2, 5):
                    ins = nc.tensor.matmul(ada_p[:, :], ones, acc[:, :], start=True, stop=True)
                else:
                    for q in range(4):
                        ins = nc.tensor.matmul(ada_p[:, q:q + 1], acc[:, q * P:(q + 1) * P], ones[:, 0:1],
                                               start=True, stop=True)
                ins.then_inc(a_sum, 1)

            def chunks(key, lo, hi, u_of=(uhi, ulo), u_from=None, mid=None, late=None):
                ph = PH[key]
                start = [sum(ph["kts"][:j]) for j in range(ph["n"])]

                def body(c0, i):
                    small = key[1] == "up_b" and c0 == 11
                    n = 2 if small else ph["n"]
                    pe.wait_ge(acc_free, ph["chunk"] + c0 + 2 * i + 1)
                    banks = bank[2 * (c0 % 2):2 * (c0 % 2) + 2]
                    for j in range(n):
                        k0, kn = (8 * j, 8) if small else (start[j], ph["kts"][j])
                        unit(ph, c0, i, j, [(k, k0 + k) for k in range(kn)], u_of, j == 0, j == n - 1, banks,
                             None if u_from is None else u_from + (k0 + kn) // 2, late)
                        if j == 0 and mid:
                            mid(c0, i)
                    beside = ada_of(key, lo, c0, i)
                    if beside and beside[1] + beside[2] == KT:
                        ada_sum(beside[0])
                if hi - lo == 1:
                    body(lo, 0)
                else:
                    pairs(pe, lo, hi, body)

            def hidden_T(layer, name, c0, i, nf=2):
                q = H_LAYER * layer + H0[name] + c0 + 2 * i
                pe.wait_ge(acc_free, PH[layer, name]["chunk"] + c0 + 2 * i + 3)
                pe.wait_ge(h_mul, q + 1)
                for s in range(2):
                    for k in range(nf):
                        for t in range(NT):
                            ins = nc.tensor.transpose(T[s][:, k * S + t * P:k * S + (t + 1) * P],
                                                      g_tok[:, t, (s * nf + k) * P:(s * nf + k + 1) * P], ident)
                ins.then_inc(h_T, 1)

            def mlp(layer, u_from):
                for name in ("up_a", "up_b"):
                    key = (layer, name)
                    last = PH[key]["chunks"] - 1
                    prev = lambda c0, i: hidden_T(layer, name, c0 - 1, i)
                    chunks(key, 0, 1, u_from=u_from)
                    chunks(key, 1, 9, mid=prev)
                    if name == "up_b":
                        chunks(key, 9, 11, mid=prev)
                    chunks(key, last, last + 1, mid=prev)
                    hidden_T(layer, name, last, 0, 1 if name == "up_b" else 2)
                    done = H_LAYER * layer + H0[name] + last + 1
                    pe.wait_ge(h_lo, done - 1)
                    kt = 2 * last
                    chunks((layer, "down" + name[2:]), 0, 4, u_of=(hhi, hlo), late=(kt, done))
                    u_from = None

            def channels_T(src, base, v):
                pe.wait_ge(t_free, base + v + 1)
                for k in range(2):
                    for t in range(NT):
                        ins = nc.tensor.transpose(T[v % 2][:, k * S + t * P:k * S + (t + 1) * P], src(t, 2 * v + k), ident)
                ins.then_inc(t_full, 1)

            sizes = [96] * 2 + [FT] * 8 + [8, 8, KT]
            pe.wait_ge(sem("const_in"), 16)
            pe.wait_ge(sem("c_in"), 16)
            nc.tensor.transpose(bank[2][:, 0:KT], rows[0:KT, ROW_SRC - 1, :], ident[0:KT, 0:KT]
                                ).then_inc(sem("c_T"), 1)
            pe.wait_ge(sem("rows_in"), 16 * (ROW_SRC - 1))
            at = 0
            for i, size in enumerate(sizes[:-1]):
                if i == 6:
                    at = 0
                to = bank[0 if i < 6 else 1]
                ins = nc.tensor.transpose(to[:, at:at + size], rows[0:size, i, :], ident[0:size, 0:size])
                at += size
            ins.then_inc(sem("rows_T"), 1)
            ada_sum((0, 0, 0, 0))
            pe.wait_ge(sem("x_in"), 16)
            for v in range(8):
                channels_T(lambda t, k: x[:, t, k * P:(k + 1) * P], T_X, v)
            for b in range(1, 8):
                ada_sum((0, b // 4, b % 4, b), acc_start if b % 2 else ada_acc)
            pe.wait_ge(sem("cols_in"), 2)
            chunks((0, "in"), 0, 4, u_from=2 + U_FIRST)
            chunks((0, "in"), 4, 8)

            pe.wait_ge(sem("lr_lo"), 1)
            for t in range(NT):
                for kt in range(KT):
                    uh, ul = uhi[:, kt, t * P:(t + 1) * P], ulo[:, kt, t * P:(t + 1) * P]
                    to = bank[7][:, t * GRANK:(t + 1) * GRANK]
                    nc.tensor.matmul(to, uh, w_lrh[:, kt, :], start=kt == 0, stop=False)
                    nc.tensor.matmul(to, uh, w_lrl[:, kt, :], start=False, stop=False)
                    ins = nc.tensor.matmul(to, ul, w_lrh[:, kt, :], start=False, stop=kt == KT - 1)
            ins.then_inc(sem("lr"), 1)
            ada_sum(GLA_FIRST)
            pe.wait_ge(acc_free, 2 + 8)
            pe.wait_ge(sem("pool_in"), 16 * 5)

            def pool_mean(g):
                for k in range(2):
                    col = (2 * g + k) * P
                    nc.tensor.matmul(bank[g][:, k * S:(k + 1) * S], z[:, 0, col:col + P], band[:, g, 0:S],
                                     start=True, stop=False)
                    ins = nc.tensor.matmul(bank[g][:, k * S + P:(k + 1) * S], z[:, 1, col:col + P], band[:, g, S:S + P],
                                           start=False, stop=True)
                ins.then_inc(sem("pool_T"), 1)

            def pool_map(g):
                pe.wait_ge(t_free, T_MIX + g + 1)
                pe.wait_ge(sem("pool_T_out"), g + 1)
                for d in range(2):
                    for k in range(2):
                        ins = nc.tensor.matmul(T[g % 2][:, d * S:(d + 1) * S], w_pool[:, g, k, d * P:(d + 1) * P],
                                               dT[:, g % 2, k, :], start=k == 0, stop=k == 1)
                ins.then_inc(t_full, 1)
            pool_mean(0)
            pool_mean(1)
            pool_mean(2)
            pool_mean(3)
            pe.wait_ge(sem("lr_out"), 1)
            for t in range(NT):
                ins = nc.tensor.transpose(bank[7][0:GRANK, t * P:(t + 1) * P], lr[:, t, :], ident)
            ins.then_inc(sem("lr_T"), 1)
            pool_map(0)
            pe.wait_ge(sem("lr_T_out"), 1)
            pe.wait_ge(sem("gla_in"), 32)
            pe.wait_ge(a_out, MIX_FIRST[0] + 1)
            for t in range(NT):
                ins = nc.tensor.matmul(bank[6 + t][:, :], lrT[:, t * P:(t + 1) * P], w_g[:, :], start=True, stop=True)
            ins.then_inc(sem("gate_pre"), 1)
            for g in range(1, 4):
                pool_map(g)
            for j, off in ((0, OFF_Q), (2, OFF_K)):
                for h in range(GH):
                    for t in range(NT):
                        ins = nc.tensor.transpose(bank[j + h // 2][:, (h % 2) * S + t * P:(h % 2) * S + (t + 1) * P],
                                                  z[:, t, off + h * GDK:off + (h + 1) * GDK], ident)
            ins.then_inc(sem("qk_T"), 1)
            pe.wait_ge(sem("log_a"), 1)
            pe.wait_ge(sem("qk_T_out"), 1)
            for t in range(NT):
                nc.tensor.matmul(bank[t][:, :], sum_suf, loga[:, t, :], start=True, stop=True)
            for h in range(GH):
                for t in range(NT):
                    ins = nc.tensor.matmul(bank[2 + h // 2][:, (h % 2) * S + t * P:(h % 2) * S + (t + 1) * P],
                                           loga[:, t, h * GDK:(h + 1) * GDK], sum_inc, start=True, stop=True)
            ins.then_inc(sem("cum"), 1)
            pe.wait_ge(sem("qk_dec"), 1)
            for t in range(NT):
                for h in range(GH):
                    ins = nc.tensor.matmul(bank[6 + t][:, h * P:(h + 1) * P], kiT[:, h, t * P:(t + 1) * P],
                                           qdT[:, h, t * P:(t + 1) * P], start=True, stop=True)
            ins.then_inc(sem("scores"), 1)
            pe.wait_ge(sem("kdec"), 1)
            pe.wait_ge(t_free, 2 + T_MIX + 4)
            for c in range(3):
                t, r = c // 2, slice(c % 2 * CH, (c % 2 + 1) * CH)
                for h in range(GH):
                    ins = nc.tensor.matmul(bank[2 * c + h // 2][:, (h % 2) * GDV:(h % 2 + 1) * GDV],
                                           kdec[r, t, h * GDK:(h + 1) * GDK],
                                           z[r, t, OFF_V + h * GDV:OFF_V + (h + 1) * GDV], start=True, stop=True)
            ins.then_inc(sem("outer"), 1)
            pe.wait_ge(sem("scores_out"), 1)
            pe.wait_ge(sem("states"), 1)
            for t in range(NT):
                for h in range(GH):
                    to = bank[2 * t + h // 2][:, (h % 2) * GDV:(h % 2 + 1) * GDV]
                    ins = nc.tensor.matmul(to, scT[:, t, h, :], z[:, t, OFF_V + h * GDV:OFF_V + (h + 1) * GDV],
                                           start=True, stop=False, skip_group_check=True)
                    for c in (2 * t, 2 * t + 1):
                        if c:
                            st = state[:, c - 1, h, :] if c < 3 else state3[:, h, :]
                            r = slice(c % 2 * CH, (c % 2 + 1) * CH)
                            ins = nc.tensor.matmul(to[r, :], qdT[:, h, c * CH:(c + 1) * CH], st, start=False,
                                                   stop=True, skip_group_check=True)
            ins.then_inc(sem("gla_o"), 1)
            for v in range(4, 8):
                pe.wait_ge(sem("y_b"), v - 3)
                channels_T(lambda t, k: z[:, t, OFF_Q + (k - 8) * P:OFF_Q + (k - 7) * P], T_MIX, v)
            ada_sum_mix(0)
            chunks((0, "out"), 0, 4, u_from=2 + U_MIX)

            def ln_T(s):
                for v in range(8):
                    pe.wait_ge(sem("ln_chunk"), 4 * s + v // 2 + 1)
                    channels_T(lambda t, k: x[:, t, k * P:(k + 1) * P], T_LN[s], v)
            ln_T(0)
            mlp(0, 2 + U_LN[0])
            ln_T(1)
            chunks((1, "qkv"), 0, 4, u_from=2 + U_LN[1])
            chunks((1, "qkv"), 4, 8)
            chunks((1, "qkv"), 8, 12)

            C_QKV = PH[1, "qkv"]["chunk"] + 12
            pe.wait_ge(acc_free, 2 + C_QKV)
            pe.wait_ge(t_free, 2 + T_LN[1] + 8)
            pe.wait_ge(a_out, MIX_FIRST[1] + 1)
            pe.wait_ge(sem("toep_in"), 16)
            for s in range(AH + 3):
                if s < AH:
                    if s >= 2:
                        pe.wait_ge(sem("att_qk"), s - 1)
                    for j in range(2):
                        for t in range(NT):
                            ins = nc.tensor.transpose(T[s % 2][:, j * S + t * P:j * S + (t + 1) * P],
                                                      qkv[:, t, j * D + s * AD:j * D + (s + 1) * AD], ident)
                    ins.then_inc(sem("att_T"), 1)
                if 1 <= s <= AH:
                    h = s - 1
                    pe.wait_ge(sem("att_qk"), h + 1)
                    if h >= 2:
                        pe.wait_ge(sem("att_exp"), h - 1)
                    sb, q, k = bank[6 + h % 2], qkT[:, h % 2, 0:S], qkT[:, h % 2, S:2 * S]
                    nc.tensor.matmul(sb[:, 0:P], q[:, 0:P], k[:, 0:P], start=True, stop=False)
                    nc.tensor.matmul(sb[:, 0:P], toep[:, h, 0:P], rev, start=False, stop=False)
                    nc.tensor.matmul(sb[:, 0:P], mask_q, mask_k, start=False, stop=True)
                    nc.tensor.matmul(sb[:, P:3 * P], q[:, P:S], k[:, 0:S], start=True, stop=False)
                    nc.tensor.matmul(sb[:, P:2 * P], toep[:, h, P:S], rev, start=False, stop=False)
                    nc.tensor.matmul(sb[:, 2 * P:3 * P], toep[:, h, 0:P], rev, start=False, stop=False)
                    nc.tensor.matmul(sb[:, 2 * P:3 * P], mask_q, mask_k, start=False, stop=True
                                     ).then_inc(sem("att_s"), 1)
                if 2 <= s <= AH + 1:
                    h = s - 2
                    pe.wait_ge(sem("att_p"), h + 1)
                    if h >= 2:
                        pe.wait_ge(sem("att_pT_out"), h - 1)
                    for j in range(3):
                        to = (0, P, 2 * P)[(0, 1, 2)[j]]
                        ins = nc.tensor.transpose(bank[h % 2][:, to:to + P], prob[:, h % 2, j * P:(j + 1) * P], ident)
                    ins.then_inc(sem("att_pT"), 1)
                if s == AH:
                    ada_sum_mix(1)
                if s >= 3:
                    h = s - 3
                    pe.wait_ge(sem("att_pT_out"), h + 1)
                    if h >= 2:
                        pe.wait_ge(u_ready, 2 + U_ATT + h - 1)
                    v0 = 2 * D + h * AD
                    nc.tensor.matmul(bank[2 + h % 2][:, 0:S], qkv[:, 0, v0:v0 + AD], probT[:, h % 2, 0:S],
                                     start=True, stop=False)
                    nc.tensor.matmul(bank[2 + h % 2][:, P:S], qkv[:, 1, v0:v0 + AD], probT[:, h % 2, 2 * P:3 * P],
                                     start=False, stop=True).then_inc(sem("att_o"), 1)
            pe.wait_ge(u_ready, 2 + U_ATT + AH)
            chunks((1, "o"), 0, 4)
            ln_T(2)
            mlp(1, 2 + U_LN[2])


_INS = ["x", "c", "w_ada", "b_ada", "ln_g", "ln_b", "w_in_ab", "w_gate_lr", "b_gate", "gla_norm_g", "w_pool",
        "pool_scale", "w_out_ab", "w_qkv", "rel_bias", "w_o", "w_up", "conv_w", "conv_b", "w_down"]


def constant_tables():
    import numpy as np
    j, i = np.arange(P)[:, None], np.arange(P)[None, :]
    same = j // CH == i // CH
    consts = np.zeros((P, CONST_COLS), np.float32)
    consts[:, 0:P] = j == i
    consts[:, P:2 * P] = j == P - 1 - i
    consts[:, 2 * P:3 * P] = (same & (j <= i)) / GTAU
    consts[:, 3 * P:4 * P] = (same & (j > i)) / GTAU
    consts[:, 4 * P:5 * P] = 1.0
    consts[0, 5 * P:5 * P + CH] = 1.0
    consts[0, 6 * P + CH:7 * P] = NEG
    band = np.zeros((P, 4, BAND), np.float32)
    src, dst = np.arange(S)[:, None], np.arange(S)[None, :]
    for g, w in enumerate(WINDOWS):
        m = ((src <= dst) & (src > dst - w)) / np.minimum(dst + 1, w) - (src == dst)
        band[:, g, 0:S] = m[0:P]
        band[:, g, S:] = m[P:, P:]
    return {"consts": consts, "band": band}


def kernel(**inputs):
    import numpy as np
    import concourse.bacc as bacc
    from concourse.bass_utils import run_bass_kernel_spmd as run

    nc = bacc.Bacc("TRN2", target_bir_lowering=False, num_devices=1, dynamic_dma_scratch_size=1024)
    arrays, args = {}, {}
    for name, a in [(n, inputs[n]) for n in _INS] + list(constant_tables().items()):
        a = np.ascontiguousarray(a)
        arrays[f"in_{name}"] = a
        args[name] = nc.dram_tensor(f"in_{name}", a.shape, mybir.dt.from_np(a.dtype), kind="ExternalInput").ap()
    out = nc.dram_tensor("out_x", (1, S, D), mybir.dt.float32, kind="ExternalOutput").ap()
    build(nc, args, out)
    r = run(nc, [arrays], core_ids=[0])
    return r.results[0]["out_x"]
```

```python
import concourse.bass as bass
from concourse import mybir
from contextlib import ExitStack

D = 2048
S = 256
P = 128
F = 5504
KT = D // P
NT = S // P
NCOL = 512
UNIT = 2048
CH = 64
POOL_W = D // 2
WINDOWS = (2, 4, 8, 16)
PG = POOL_W // len(WINDOWS)
GH, GDV, GDK, GRANK, GTAU = 4, 256, 128, 16, 16.0
OFF_Q = POOL_W
OFF_K = OFF_Q + GH * GDK
OFF_V = OFF_K + GH * GDK
OFF_R = OFF_V + GH * GDV
OFF_LR = OFF_R + GH * GDV
AH, AD = 16, 128
REL = 256
DEPTH = 2
ALPHA = (2.0 * DEPTH) ** 0.25
EPS = 1e-5
FT = F // P
FT_A = 20
FT_B = FT - FT_A
NEG = -1e30
RAW_SLOTS, HL_SLOTS, ADA_SLOTS = 4, 2, 4
ADA_HALVES = KT // 2
CONST_COLS = 7 * P
BAND = 3 * P


def plan():
    four = (4, 4, 4, 4)
    phases = []
    for layer in range(DEPTH):
        if layer % 2 == 0:
            phases += [(layer, "in", 8, four, 3), (layer, "mix", 0, four, 7), (layer, "out", 4, four, 2)]
        else:
            phases += [(layer, "qkv", 12, four, 6), (layer, "mix", 0, four, 3), (layer, "o", 4, four, 2)]
        last = layer == DEPTH - 1
        phases += [(layer, "up_a", FT_A // 2, four, 4),
                   (layer, "down_a", 4, (4, 4, 4, 4, 2, 2), 0 if last else 2),
                   (layer, "up_b", FT_B // 2 + 1, four, 0 if last else 5),
                   (layer, "down_b", 4, (4, 4, 4, 4, 4, 3), 0 if last else 2)]
    out, unit, chunk, block = {}, 0, 0, 8
    for layer, name, chunks, kts, blocks in phases:
        out[layer, name] = dict(chunks=chunks, kts=kts, n=len(kts), unit=unit, chunk=chunk, block=block,
                                blocks=blocks)
        unit += chunks * len(kts) - (2 if name == "up_b" else 0)
        chunk += chunks
        block += blocks
    return out


def build(nc, A, out):
    f32, f32r, i32 = mybir.dt.float32, mybir.dt.float32r, mybir.dt.int32
    ALU = mybir.AluOpType
    ACT = mybir.ActivationFunctionType
    AX = mybir.AxisListType
    PH = plan()

    ctx = ExitStack()
    with ctx:
        used = [2048]

        def region(size):
            at = used[0]
            used[0] += (size + 31) // 32 * 32
            return at

        def place(name, shape, at, dt=f32):
            return nc.alloc_sbuf_tensor_at(name, shape, dt, offset=at)

        raw = place("w_raw", [P, RAW_SLOTS, UNIT], region(RAW_SLOTS * UNIT * 4))
        whi = place("w_hi", [P, HL_SLOTS, UNIT], region(HL_SLOTS * UNIT * 4), f32r)
        wlo = place("w_lo", [P, HL_SLOTS, UNIT], region(HL_SLOTS * UNIT * 4), f32r)
        ada_w = place("ada_w", [P, ADA_SLOTS, 2, NCOL], region(ADA_SLOTS * 2 * NCOL * 4))
        ada_acc = place("ada_acc", [P, NCOL], region(NCOL * 4))
        gate = place("gate", [P, D], region(D * 4))
        r_u = region(2 * KT * S * 4)
        uhi = place("u_hi", [P, KT, S], r_u, f32r)
        ulo = place("u_lo", [P, KT, S], r_u + KT * S * 4, f32r)
        x = place("x_tok", [P, NT, D], region(NT * D * 4))
        r_w = region(48 * 1024)
        r_aux = region(16 * 1024)
        r_s = region(12 * 1024)
        consts = place("consts", [P, CONST_COLS], region(CONST_COLS * 4))
        n_cols = 2 * 96 + DEPTH * 4 * FT + 8 + 8 + 2 * 64
        cols = place("cols", [P, n_cols], region(n_cols * 4))
        mod = place("mod", [P, DEPTH * 96], region(DEPTH * 96 * 4))
        ln_cols = place("ln_cols", [P, 2, KT], region(2 * KT * 4))
        silu_c = place("silu_c", [P, KT], region(KT * 4))
        small = place("small", [P, 192], region(192 * 4))
        assert used[0] <= 229368, used[0]

        xT = place("x_T", [P, KT, S], r_w)
        rows = place("rows", [P, 15, P], r_w + 32 * 1024)
        z = place("z", [P, NT, OFF_LR], r_w)
        kdec = place("k_dec", [P, NT, GH * GDK], r_w + 32768)
        loga = place("log_a", [P, NT, GH * GDK], r_w + 32768 + 4096)
        qdT = place("q_dec_T", [P, GH, S], r_w + 32768 + 8192)
        kiT = place("k_inv_T", [P, GH, S], r_w + 32768 + 12288)
        hhi = place("hid_hi", [P, FT_B, S], r_w, f32r)
        hlo = place("hid_lo", [P, FT_B, S], r_w + FT_B * S * 4, f32r)
        qkv = place("qkv", [P, NT, 3 * D], r_w)
        state = place("gla_state", [P, 2, GH, GDV], r_u + 8 * S * 4)
        state3 = place("gla_state3", [P, GH, GDV], r_u + KT * S * 4 + 8 * S * 4)
        scT = place("scores_T", [P, NT, GH, P], r_u + KT * S * 4 + 8 * S * 4 + 4096)
        band = place("band", [P, 4, BAND], r_aux)
        w_pool = place("w_pool_sb", [P, 4, 2, PG], r_aux + 4 * BAND * 4)
        toep = place("toeplitz", [P, AH, S], r_aux)
        lnp = place("ln_params", [P, 2, D], r_aux)
        g_tok = place("hid_tok", [P, NT, NCOL], r_s)
        gc = place("conv", [P, 2, S], r_s + 4096)
        h32 = place("h_f32", [P, 2, S], r_s + 6144)
        y_tmp = place("y_gated", [P, NT, NCOL], r_s + 8192)
        u32 = place("u_f32", [P, 2, 2 * S], r_s)
        w_lr = place("w_lr", [P, KT, GRANK], r_w + 40960)
        w_lrh = place("w_lr_hi", [P, KT, GRANK], r_w + 40960 + 1024, f32r)
        w_lrl = place("w_lr_lo", [P, KT, GRANK], r_w + 40960 + 2048, f32r)
        lr = place("lr", [P, NT, GRANK], r_u + KT * S * 4 + 8 * S * 4 + 4096)
        lrT = place("lr_T", [GRANK, S], r_u + KT * S * 4 + 8 * S * 4 + 4096 + 128)
        w_g = place("w_gate", [GRANK, GH * GDK], r_s + 8192)
        acc_start = place("ada_acc_start", [P, NCOL], r_w + 40960)
        acc_gla = place("ada_acc_gla", [P, 8, NCOL], r_aux)
        acc_att = [place("ada_acc_att0", [P, NCOL], r_s + 10240),
                   place("ada_acc_att1", [P, NCOL], r_u + (KT - 2) * S * 4)]
        mix_accs = {0: [acc_gla[:, 7, :], ada_acc] + [acc_gla[:, k, :] for k in range(4)], 1: [ada_acc] + acc_att}
        b_g = place("b_gate", [P, GH * GDK], r_s + 10240)
        dT = place("pool_T", [P, 2, 2, S], r_s + 4096)
        qkT = place("qk_T", [P, 2, 2 * S], r_s)
        prob = place("prob", [P, 2, 3 * P], r_s + 4096)
        probT = place("prob_T", [P, 2, 3 * P], r_s + 7168)

        def cst(i):
            return consts[:, i * P:(i + 1) * P]

        ident, rev, sum_inc, sum_suf, ones = (cst(i) for i in range(5))
        mask_q, mask_k = consts[0:1, 5 * P:6 * P], consts[0:1, 6 * P:7 * P]
        C_CONV = 2 * 96
        C_POOL = C_CONV + DEPTH * 4 * FT
        C_NORM = C_POOL + 8
        C_LNG = C_NORM + 8
        C_LNB = C_LNG + 64
        bn = small[:, 0:48].rearrange("p (t c s) -> p t c s", t=2, c=4)
        mv = small[:, 48:52].rearrange("p (t s) -> p t s", t=2)
        var, sd, rs, t1 = (small[:, 52 + 2 * i:54 + 2 * i] for i in range(4))
        gbn = small[:, 64:112].rearrange("p (h s) -> p h s", h=8)
        gmv = small[:, 112:128].rearrange("p (h s) -> p h s", h=8)
        gvar, gsd, grs, gt = (small[:, 128 + 8 * i:136 + 8 * i] for i in range(4))
        decay = small[:, 160:176].rearrange("p (h c) -> p h c", h=4)
        nmax = small[:, 176:180].rearrange("p (b t) -> p b t", b=2)
        rsum = small[:, 180:184].rearrange("p (b t) -> p b t", b=2)
        rinv = small[:, 184:188].rearrange("p (b t) -> p b t", b=2)

        bank = [ctx.enter_context(nc.psum_tensor(f"bank{i}", [P, NCOL], f32)) for i in range(8)]
        T = bank[4:6]
        ada_p = bank[6]

        sems = {}

        def sem(name):
            if name not in sems:
                sems[name] = ctx.enter_context(nc.semaphore(name))
            return sems[name]

        w_loaded = [sem(f"w_loaded{i}") for i in range(RAW_SLOTS)]
        w_hi = sem("w_hi_done")
        w_lo = sem("w_lo_done")
        wh_used = sem("w_hi_used")
        w_used = sem("w_used")
        acc_free = sem("acc_free")
        a_loaded = [sem(f"ada_loaded{i}") for i in range(ADA_SLOTS)]
        a_step = sem("ada_step")
        a_sum = sem("ada_summed")
        a_out = sem("ada_out")
        A0 = 2 * ADA_SLOTS

        t_full = sem("t_full")
        t_free = sem("t_free")
        u32_done = sem("u32_done")
        u_hi_done = sem("u_hi_done")
        u_ready = sem("u_ready")
        U_FIRST, U_MIX, U_LN, U_ATT = 0, 8, {0: 16, 1: 24, 2: 48}, 32
        T_X, T_MIX, T_LN = 0, 8, {0: 16, 1: 24, 2: 32}
        h_T = sem("hid_T")
        h_bias = sem("hid_bias")
        h_tap = sem("hid_tap")
        h_conv = sem("hid_conv")
        h_gelu = sem("hid_gelu")
        h_mul = sem("hid_mul")
        h_hi = sem("hid_hi_done")
        h_lo = sem("hid_lo_done")
        y_gated = sem("y_gated")
        y_sum = sem("y_sum")
        y_done = sem("y_done")

        H0 = {"up_a": 0, "up_b": FT_A // 2}
        H_LAYER = FT_A // 2 + FT_B // 2 + 1
        Y0 = {(0, "out"): 0, (0, "down_a"): 4, (0, "down_b"): 8, (1, "o"): 12, (1, "down_a"): 16,
              (1, "down_b"): 20}
        ADA = {(0, "in", 2): (0, 2, 0), (0, "in", 4): (0, 2, 1), (0, "out", 0): (0, 4, 2),
               (0, "up_a", 1): (0, 5, 0), (0, "down_a", 0): (1, 1, 0), (0, "up_b", 1): (1, 0, 0),
               (0, "up_b", 9): (1, 4, 0),
               (0, "down_b", 0): (1, 1, 2), (1, "qkv", 0): (1, 3, 0), (1, "qkv", 4): (1, 2, 0),
               (1, "qkv", 8): (1, 2, 2), (1, "o", 0): (1, 3, 2), (1, "up_a", 1): (1, 5, 0)}
        MIX = {0: [(0, 3, 0), (0, 3, 1), (0, 3, 2), (0, 3, 3), (0, 4, 0), (0, 4, 1)], 1: [(1, 4, n) for n in range(1, 4)]}
        GLA_FIRST = (0, 2, 3, PH[0, "mix"]["block"])
        MIX_FIRST = {0: PH[0, "mix"]["block"] + 1, 1: PH[1, "mix"]["block"]}
        GATE_NO = {(0, 2): 1, (0, 5): 2, (1, 2): 3, (1, 5): 4}
        ROW_SRC = 15
        ROW_DMAS = 1 + 2 * DEPTH + 4

        block = ctx.enter_context(nc.Block())

        def pairs(e, lo, hi, body):
            n = (hi - lo) // 2
            assert 2 * n == hi - lo
            if n == 1:
                body(lo, 0)
                body(lo + 1, 0)
            elif n:
                with e.Fori(0, n) as i:
                    body(lo, i)
                    body(lo + 1, i)

        def ada_of(key, lo, c0, i):
            src = ADA.get((*key, lo))
            if src is None:
                return None
            layer, part, n0 = src
            before = lo // 2 - (key[1] == "in")
            return (layer, part, n0 + i, PH[key]["block"] + before + i), (c0 - lo) * KT // 2

        def unit_no(ph, c0, i, j):
            u = ph["unit"] + c0 * ph["n"] + j
            return u, u + 2 * ph["n"] * i

        def ada_rows(e, ns, acc, m, lo, hi):
            for r in range(lo, hi):
                half = r // 2
                if r % 2 == 0:
                    e.wait_ge(a_loaded[half % ADA_SLOTS], 32 * m + 16 * (half // ADA_SLOTS + 1))
                w = ada_w[:, half % ADA_SLOTS, r % 2, :]
                if r == 0:
                    ns.tensor_scalar(acc[:, :], w, silu_c[:, 0:1], None, ALU.mult).then_inc(a_step, 1)
                else:
                    e.wait_ge(a_step, m * KT + (A0 + r))
                    ns.scalar_tensor_tensor(acc[:, :], w, silu_c[:, r:r + 1], acc[:, :],
                                            ALU.mult, ALU.add).then_inc(a_step, 1)

        @block.sync
        def _(sp):
            def load_unit(ph, c0, i, j, halves):
                u, un = unit_no(ph, c0, i, j)
                sp.wait_ge(w_lo, un + 1)
                for dst, src in halves(raw[:, u % RAW_SLOTS, :]):
                    sp.dma_start(dst, src).then_inc(w_loaded[u % RAW_SLOTS], 16)

            def load_half(blk, half):
                layer, part, n, m = blk
                sp.wait_ge(a_step, m * KT + 2 * half + 2)
                w = A["w_ada"][layer].rearrange("(k p) (s n c) -> p k s n c", p=P, s=6, n=4)
                sp.dma_start(ada_w[:, half % ADA_SLOTS], w[:, 2 * half:2 * half + 2, part, n, :]
                             ).then_inc(a_loaded[half % ADA_SLOTS], 16)

            def phase(key, lo, hi, mix=False):
                layer, name = key
                ph = PH[key]
                first = [sum(ph["kts"][:j]) for j in range(ph["n"])]
                base = {"down_b": FT_A}.get(name, 0)
                if name in ("up_a", "up_b"):
                    f0 = 0 if name == "up_a" else FT_A * P
                    f1 = f0 + (FT_A if name == "up_a" else FT_B - 1) * P
                    w = A["w_up"][layer].rearrange("(k p) (s f) -> p k s f", p=P, s=2)
                    w = w[:, :, :, f0:f1].rearrange("p k s (c f) -> p k s c f", f=2 * P)
                else:
                    w = {"in": lambda: A["w_in_ab"][0][:, 0:OFF_LR], "out": lambda: A["w_out_ab"][0],
                         "qkv": lambda: A["w_qkv"][0], "o": lambda: A["w_o"][0],
                         "down_a": lambda: A["w_down"][layer], "down_b": lambda: A["w_down"][layer]}[name]()
                    w = w.rearrange("(k p) (c n) -> p k c n", p=P, n=NCOL)
                after = {4: (0, 1, 3, 4), 6: (0, 1, 2, 3, 4, 4)}[ph["n"]]

                def body(c0, i):
                    beside, c = ada_of(key, lo, c0, i), 2 * i + c0
                    for j in range(ph["n"]):
                        k = ph["kts"][j]
                        if name in ("up_a", "up_b"):
                            load_unit(ph, c0, i, j, lambda r: [
                                (r.rearrange("p (k s f) -> p k s f", k=k, s=2)[:, :, s, :],
                                 w[:, 4 * j:4 * j + 4, s, c, :]) for s in range(2)])
                        else:
                            k0, cut = base + first[j], (k + 1) // 2
                            load_unit(ph, c0, i, j, lambda r: [
                                (r[:, a * NCOL:b * NCOL].rearrange("p (k n) -> p k n", n=NCOL),
                                 w[:, k0 + a:k0 + b, c, :]) for a, b in ((0, cut), (cut, k))])
                        if mix and j == 1 and c0 == lo and i == 0:
                            for blk in [GLA_FIRST] * (layer == 0) + [
                                    (*b, MIX_FIRST[layer] + n) for n, b in enumerate(MIX[layer])]:
                                for half in range(ADA_HALVES):
                                    load_half(blk, half)
                        if beside and j:
                            blk, row = beside
                            for half in range(after[j - 1], after[j]):
                                load_half(blk, row // 2 + half)
                if hi - lo == 1:
                    body(lo, 0)
                elif mix:
                    for c in range(lo, hi):
                        body(lo + (c - lo) % 2, (c - lo) // 2)
                else:
                    pairs(sp, lo, hi, body)

            def gate_load(layer, part, uses):
                if uses:
                    sp.wait_ge(y_done, uses)
                sp.dma_start(gate[:, :], A["b_ada"][layer:layer + 1, part * D:(part + 1) * D].broadcast_to((P, D))
                             ).then_inc(sem("gate_in"), 16)

            def ln_load(s):
                layer, which = divmod(s, 2)
                if s:
                    sp.wait_ge(sem("ln_affine"), 4 * s)
                for k, name in enumerate(("ln_g", "ln_b")):
                    sp.dma_start(lnp[:, k, :], A[name][layer, which:which + 1, :].broadcast_to((P, D))
                                 ).then_inc(sem("ln_in"), 16)

            def mlp(layer, uses):
                phase((layer, "up_a"), 0, 1)
                gate_load(layer, 5, uses)
                phase((layer, "up_a"), 1, 9)
                phase((layer, "up_a"), 9, 10)
                phase((layer, "down_a"), 0, 4)
                phase((layer, "up_b"), 0, 1)
                phase((layer, "up_b"), 1, 9)
                phase((layer, "up_b"), 9, 11)
                w = A["w_up"][layer].rearrange("(k p) (s f) -> p k s f", p=P, s=2)[:, :, :, F - P:F]
                for j in range(2):
                    load_unit(PH[layer, "up_b"], 11, 0, j, lambda r: [
                        (r.rearrange("p (k s f) -> p k s f", k=8, s=2)[:, :, s, :], w[:, 8 * j:8 * j + 8, s, :])
                        for s in range(2)])
                phase((layer, "down_b"), 0, 4)

            sp.dma_start(rows[0:KT, ROW_SRC - 1, :], A["c"][0].rearrange("(r c) -> r c", c=P)
                         ).then_inc(sem("c_in"), 16)
            sp.dma_start(consts[:, :], A["consts"]).then_inc(sem("const_in"), 16)
            for half in range(ADA_HALVES):
                load_half((0, 0, 0, 0), half)
            sp.dma_start(rows[0:96, 0:DEPTH, :], A["b_ada"].rearrange("l (r c) -> r l c", c=P)
                         ).then_inc(sem("rows_in"), 16)
            for l in range(DEPTH):
                sp.dma_start(rows[0:FT, 2 + 4 * l:5 + 4 * l, :], A["conv_w"][l].rearrange("w (r c) -> r w c", c=P)
                             ).then_inc(sem("rows_in"), 16)
                sp.dma_start(rows[0:FT, 5 + 4 * l, :], A["conv_b"][l].rearrange("(r c) -> r c", c=P)
                             ).then_inc(sem("rows_in"), 16)
            for i, src in enumerate((A["pool_scale"][0], A["gla_norm_g"][0],
                                     A["ln_g"].rearrange("l w n -> (l w n)"), A["ln_b"].rearrange("l w n -> (l w n)"))):
                sp.dma_start(rows[0:src.shape[0] // P, 10 + i, :], src.rearrange("(r c) -> r c", c=P)
                             ).then_inc(sem("rows_in"), 16)
            for half in range(ADA_HALVES):
                load_half((0, 1, 0, 1), half)
            sp.dma_start(x[:, :, :], A["x"][0].rearrange("(t p) n -> p t n", p=P)).then_inc(sem("x_in"), 16)
            w_in = A["w_in_ab"][0][:, 0:OFF_LR].rearrange("(k p) (c n) -> p k c n", p=P, n=NCOL)
            for g in range(4):
                for b in (2 * g, 2 * g + 1):
                    if g:
                        for half in range(ADA_HALVES):
                            load_half((0, b % 2, b // 2, b), half)
                for c in range(2):
                    load_unit(PH[0, "in"], 0, 0, 2 * g + c, lambda r: [
                        (r[:, a * NCOL:(a + 2) * NCOL].rearrange("p (k n) -> p k n", n=NCOL),
                         w_in[:, 4 * g + a:4 * g + a + 2, c, :]) for a in (0, 2)])
            gate_load(0, 2, 0)
            phase((0, "in"), 2, 4)
            sp.dma_start(w_lr[:, :, :], A["w_in_ab"][0][:, OFF_LR:OFF_LR + GRANK].rearrange("(k p) n -> p k n", p=P)
                         ).then_inc(sem("lr_in"), 16)
            sp.dma_start(w_g[:, :], A["w_gate_lr"][0]).then_inc(sem("gla_in"), 16)
            sp.dma_start(b_g[:, :], A["b_gate"][0:1, :].broadcast_to((P, GH * GDK))).then_inc(sem("gla_in"), 16)
            sp.dma_start(band[:, :, :], A["band"]).then_inc(sem("pool_in"), 16)
            for g in range(4):
                sp.dma_start(w_pool[:, g], A["w_pool"][0, g].rearrange("(k p) n -> p k n", p=P)
                             ).then_inc(sem("pool_in"), 16)
            phase((0, "in"), 4, 8)
            phase((0, "out"), 0, 4, mix=True)
            ln_load(0)
            mlp(0, 4)
            ln_load(1)
            phase((1, "qkv"), 0, 4)
            sp.wait_ge(sem("ln_affine"), 8)
            rb = A["rel_bias"]
            sp.dma_start(toep[:, :, :], bass.AP(rb.tensor, REL - 127, [[1, P], [2 * REL + 1, AH], [1, S]])
                         ).then_inc(sem("toep_in"), 16)
            gate_load(1, 2, 12)
            phase((1, "qkv"), 4, 8)
            phase((1, "qkv"), 8, 12)
            phase((1, "o"), 0, 4, mix=True)
            sp.wait_ge(sem("att_s"), AH)
            ln_load(2)
            mlp(1, 16)
            ln_load(3)
            out_v = out[0].rearrange("(t p) n -> p t n", p=P)
            for n in range(4):
                sp.wait_ge(sem("ln_affine"), 13 + n)
                sp.dma_start(out_v[:, :, n * NCOL:(n + 1) * NCOL], x[:, :, n * NCOL:(n + 1) * NCOL]
                             ).then_inc(sem("out_done"), 16)
            sp.wait_ge(sem("out_done"), 4 * 16)

        @block.scalar
        def _(act):
            def hi_unit(ph, c0, i, j, width):
                u, un = unit_no(ph, c0, i, j)
                act.wait_ge(w_loaded[u % RAW_SLOTS], 32 * (u // RAW_SLOTS + 1) + 16 * ph["n"] * i)
                if u >= HL_SLOTS:
                    act.wait_ge(wh_used, un - 1)
                    act.wait_ge(w_lo, un + (RAW_SLOTS - 1))
                nc.scalar.activation(whi[:, u % HL_SLOTS, 0:width], raw[:, u % RAW_SLOTS, 0:width], ACT.Copy
                                     ).then_inc(w_hi, 1)

            def steps(key, lo, hi, mid=None, tail=None, more=True):
                ph = PH[key]

                def body(c0, i):
                    own = 2 if key[1] == "up_b" and c0 == 11 else ph["n"]
                    for j in range(2, own + 2):
                        if j >= own and not more and c0 == hi - 1:
                            continue
                        width = ph["kts"][j] * NCOL if j < own else UNIT
                        hi_unit(ph, c0, i, j, width)
                        if j == 2 and mid:
                            mid(c0, i)
                    if tail:
                        tail(c0, i)
                if hi - lo == 1 or not more:
                    for c in range(lo, hi):
                        body(c, 0)
                else:
                    pairs(act, lo, hi, body)

            def chunk_end(key, c0, i):
                ph = PH[key]
                own = 2 if key[1] == "up_b" and c0 == 11 else ph["n"]
                act.wait_ge(w_used, unit_no(ph, c0, i, own)[1])

            def copy_out(dst, key):
                def tail(c0, i):
                    chunk_end(key, c0, i)
                    for t in range(NT):
                        ins = nc.scalar.activation(dst(t, c0, i), bank[2 * (c0 % 2) + t][:, :], ACT.Copy)
                    ins.then_inc(acc_free, 1)
                return tail

            act.wait_ge(sem("c_T"), 1)
            nc.scalar.activation(silu_c[:, :], bank[2][:, 0:KT], ACT.Silu).then_inc(sem("silu_c"), 1)
            for v in range(8):
                act.wait_ge(t_full, T_X + v + 1)
                nc.scalar.activation(xT[:, 2 * v:2 * v + 2, :], T[v % 2].rearrange("p (k s) -> p k s", k=2), ACT.Copy
                                     ).then_inc(t_free, 1)
            act.wait_ge(t_free, 2 + T_X + 8)
            ph_in = PH[0, "in"]
            for n in range(4):
                act.wait_ge(a_out, 2 * n + 3)
                for b in range(2):
                    v = 2 * n + b
                    act.wait_ge(u_ready, v + 1)
                    for k in range(2):
                        kt = 2 * v + k
                        ins = nc.scalar.activation(u32[:, b, k * S:(k + 1) * S], xT[:, kt, :], ACT.Identity,
                                                   scale=mod[:, kt + KT:kt + KT + 1], bias=mod[:, kt:kt + 1])
                    ins.then_inc(u32_done, 1)
                    act.wait_ge(u32_done, v + 1)
                    nc.scalar.activation(uhi[:, 2 * v:2 * v + 2, :],
                                         u32[:, b, :].rearrange("p (k s) -> p k s", k=2), ACT.Copy
                                         ).then_inc(u_hi_done, 1)
                for c in range(2):
                    hi_unit(ph_in, 0, 0, 2 * n + c, UNIT)

            def z_at(t, c0, i):
                return z[:, t, bass.ds(2 * NCOL * i + c0 * NCOL, NCOL)]
            for c in range(2):
                hi_unit(ph_in, 2, 0, c, UNIT)
                act.wait_ge(w_used, 7 + c)
                for t in range(NT):
                    ins = nc.scalar.activation(z_at(t, c, 0), bank[2 * c + t][:, :], ACT.Copy)
                ins.then_inc(acc_free, 1)
            steps((0, "in"), 2, 4, tail=copy_out(z_at, (0, "in")))
            steps((0, "in"), 4, 8, tail=copy_out(z_at, (0, "in")))

            act.wait_ge(sem("lr_in"), 16)
            nc.scalar.activation(w_lrh[:, :, :], w_lr[:, :, :], ACT.Copy).then_inc(sem("lr_hi"), 1)
            act.wait_ge(acc_free, 2 + 8)
            for t in range(NT):
                nc.scalar.activation(z[:, t, OFF_R:OFF_LR], z[:, t, OFF_R:OFF_LR], ACT.Silu).then_inc(sem("silu_r"), 1)

            def pool_T(g):
                if g >= 2:
                    act.wait_ge(t_full, T_MIX + g - 1)
                act.wait_ge(sem("pool_T"), g + 1)
                nc.scalar.activation(dT[:, g % 2], bank[g].rearrange("p (k s) -> p k s", k=2), ACT.Copy
                                     ).then_inc(sem("pool_T_out"), 1)

            def mix_piece(v, col):
                act.wait_ge(t_full, T_MIX + v + 1)
                act.wait_ge(u_ready, U_MIX + v + 1)
                for k in range(2):
                    ins = nc.scalar.activation(u32[:, v % 2, k * S:(k + 1) * S], T[v % 2][:, k * S:(k + 1) * S],
                                               ACT.Identity, scale=cols[:, col + k:col + k + 1])
                ins.then_inc(t_free, 1)
                act.wait_ge(t_free, 2 + T_MIX + v + 1)
                nc.scalar.activation(uhi[:, 2 * v:2 * v + 2, :], u32[:, v % 2, :].rearrange("p (k s) -> p k s", k=2),
                                     ACT.Copy).then_inc(u_hi_done, 1)
            pool_T(0)
            pool_T(1)
            mix_piece(0, C_POOL)
            mix_piece(1, C_POOL + 2)
            pool_T(2)
            pool_T(3)
            mix_piece(2, C_POOL + 4)
            mix_piece(3, C_POOL + 6)
            act.wait_ge(sem("gate_pre_out"), 1)
            nc.scalar.activation(kdec[:, :, :], loga[:, :, :], ACT.Abs).then_inc(sem("ls"), 1)
            act.wait_ge(sem("ls"), 1)
            nc.scalar.activation(kdec[:, :, :], kdec[:, :, :], ACT.Exp, scale=-1.0).then_inc(sem("ls"), 1)
            act.wait_ge(sem("ls"), 2)
            nc.scalar.activation(kdec[:, :, :], kdec[:, :, :], ACT.Ln, bias=1.0).then_inc(sem("ls"), 1)
            act.wait_ge(sem("qk_T"), 1)
            for j in range(2):
                nc.scalar.activation(qdT[:, 2 * j:2 * j + 2, :], bank[j].rearrange("p (h s) -> p h s", h=2), ACT.Copy,
                                     scale=float(GDK) ** -0.5)
                ins = nc.scalar.activation(kiT[:, 2 * j:2 * j + 2, :], bank[2 + j].rearrange("p (h s) -> p h s", h=2),
                                           ACT.Copy)
            ins.then_inc(sem("qk_T_out"), 1)
            act.wait_ge(sem("cum"), 1)
            for t in range(NT):
                nc.scalar.activation(kdec[:, t, :], bank[t][:, :], ACT.Exp).then_inc(sem("exp_suf"), 1)
            act.wait_ge(sem("exp_suf"), 2)
            for j in range(2):
                nc.scalar.activation(bank[j][:, :], bank[2 + j][:, :], ACT.Exp, scale=-1.0).then_inc(sem("exp_b"), 1)
            act.wait_ge(sem("exp_b"), 2)
            for j in range(2):
                nc.scalar.activation(bank[2 + j][:, :], bank[2 + j][:, :], ACT.Exp).then_inc(sem("exp_b"), 1)
            act.wait_ge(sem("gla_var"), 1)
            nc.scalar.activation(gsd, gvar, ACT.Sqrt).then_inc(sem("gla_sd"), 1)
            for v in range(4, 8):
                mix_piece(v, C_NORM + 2 * (v - 4))
            steps((0, "out"), 0, 4)

            def ln_and_u(s, with_u=True):
                act.wait_ge(sem("ln_var"), s + 1)
                nc.scalar.activation(sd, var, ACT.Sqrt).then_inc(sem("ln_sd"), 1)
                if not with_u:
                    return
                for v in range(8):
                    act.wait_ge(t_full, T_LN[s] + v + 1)
                    act.wait_ge(u_ready, U_LN[s] + v + 1)
                    for k in range(2):
                        kt = 2 * v + k
                        ins = nc.scalar.activation(u32[:, v % 2, k * S:(k + 1) * S], T[v % 2][:, k * S:(k + 1) * S],
                                                   ACT.Identity, scale=ln_cols[:, 0, kt:kt + 1],
                                                   bias=ln_cols[:, 1, kt:kt + 1])
                    ins.then_inc(t_free, 1)
                    act.wait_ge(t_free, 2 + T_LN[s] + v + 1)
                    nc.scalar.activation(uhi[:, 2 * v:2 * v + 2, :],
                                         u32[:, v % 2, :].rearrange("p (k s) -> p k s", k=2), ACT.Copy
                                         ).then_inc(u_hi_done, 1)

            def hidden(layer, name, c0, i, nf=2):
                q = H_LAYER * layer + H0[name] + c0 + 2 * i
                f = (0 if name == "up_a" else FT_A) + 2 * c0 + 4 * i
                col = C_CONV + layer * 4 * FT + f
                act.wait_ge(h_T, q + 1)
                for k in range(nf):
                    ins = nc.scalar.activation(gc[:, k, :], T[1][:, k * S:(k + 1) * S], ACT.Identity,
                                               scale=cols[:, bass.ds(col + 2 * FT + k, 1)],
                                               bias=cols[:, bass.ds(col + 3 * FT + k, 1)])
                ins.then_inc(h_bias, 1)
                act.wait_ge(h_conv, q + 1)
                nc.scalar.activation(gc[:, 0:nf, :], gc[:, 0:nf, :], ACT.Gelu_apprx_tanh).then_inc(h_gelu, 1)
                act.wait_ge(h_mul, q + 2)
                nc.scalar.activation(hhi[:, bass.ds(2 * c0 + 4 * i, nf), :], h32[:, 0:nf, :], ACT.Copy
                                     ).then_inc(h_hi, 1)

            def mlp(layer):
                for name in ("up_a", "up_b"):
                    key = (layer, name)
                    last = PH[key]["chunks"] - 1
                    out_h = copy_out(lambda t, c0, i: g_tok[:, t, :], key)
                    prev = lambda c0, i: hidden(layer, name, c0 - 1, i)
                    steps(key, 0, 1, tail=out_h)
                    steps(key, 1, 9, mid=prev, tail=out_h)
                    if name == "up_b":
                        steps(key, 9, 11, mid=prev, tail=out_h)
                        hidden(layer, name, last - 1, 0)
                        hi_unit(PH[key], last, 0, 2, UNIT)
                        hi_unit(PH[key], last, 0, 3, UNIT)
                        chunk_end(key, last, 0)
                        for t in range(NT):
                            ins = nc.scalar.activation(g_tok[:, t, 0:2 * P], bank[2 * (last % 2) + t][:, 0:2 * P],
                                                       ACT.Copy)
                        ins.then_inc(acc_free, 1)
                    else:
                        steps(key, last, last + 1, mid=prev, tail=out_h)
                    hidden(layer, name, last, 0, 1 if name == "up_b" else 2)
                    steps((layer, "down" + name[2:]), 0, 4, more=not (layer == DEPTH - 1 and name == "up_b"))

            ln_and_u(0)
            mlp(0)
            ln_and_u(1)
            steps((1, "qkv"), 0, 12, tail=copy_out(
                lambda t, c0, i: qkv[:, t, bass.ds(2 * NCOL * i + c0 * NCOL, NCOL)], (1, "qkv")))
            for s in range(AH + 3):
                if s < AH:
                    act.wait_ge(sem("att_T"), s + 1)
                    nc.scalar.activation(qkT[:, s % 2, 0:S], T[s % 2][:, 0:S], ACT.Copy, scale=float(AD) ** -0.5)
                    nc.scalar.activation(qkT[:, s % 2, S:2 * S], T[s % 2][:, S:2 * S], ACT.Copy
                                         ).then_inc(sem("att_qk"), 1)
                if 1 <= s <= AH:
                    h = s - 1
                    act.wait_ge(sem("att_max"), h + 1)
                    if h >= 2:
                        act.wait_ge(sem("att_pT"), h - 1)
                    sb = bank[6 + h % 2]
                    nc.scalar.activation(prob[:, h % 2, 0:P], sb[:, 0:P], ACT.Exp, bias=nmax[:, h % 2, 0:1],
                                         accum_out=rsum[:, h % 2, 0:1])
                    nc.scalar.activation(prob[:, h % 2, P:3 * P], sb[:, P:3 * P], ACT.Exp, bias=nmax[:, h % 2, 1:2],
                                         accum_out=rsum[:, h % 2, 1:2]).then_inc(sem("att_exp"), 1)
                if s >= 3:
                    h = s - 3
                    act.wait_ge(sem("att_o"), h + 1)
                    nc.scalar.activation(uhi[:, h, :], bank[2 + h % 2][:, 0:S], ACT.Copy).then_inc(u_hi_done, 1)
                if 1 <= s <= AH:
                    h = s - 1
                    act.wait_ge(sem("att_rinv"), h + 1)
                    for a, b, t in ((0, P, 0), (P, 3 * P, 1)):
                        ins = nc.scalar.activation(prob[:, h % 2, a:b], prob[:, h % 2, a:b], ACT.Copy,
                                                   scale=rinv[:, h % 2, t:t + 1])
                    ins.then_inc(sem("att_p"), 1)
            steps((1, "o"), 0, 4)
            ln_and_u(2)
            mlp(1)
            ln_and_u(3, False)

        @block.vector
        def _(dve):
            chained = [0]

            def link(ins):
                chained[0] += 1
                ins.then_inc(sem("dve_chain"), 1)
                dve.wait_ge(sem("dve_chain"), chained[0])

            def lo_unit(ph, c0, i, j, width):
                u, un = unit_no(ph, c0, i, j)
                dve.wait_ge(w_hi, un + 1)
                if u >= HL_SLOTS:
                    dve.wait_ge(w_used, un - 1)
                nc.vector.tensor_tensor(wlo[:, u % HL_SLOTS, 0:width], raw[:, u % RAW_SLOTS, 0:width],
                                        whi[:, u % HL_SLOTS, 0:width].bitcast(f32), ALU.subtract).then_inc(w_lo, 1)

            def ada_evac(blk):
                layer, part, n, m = blk
                dve.wait_ge(a_sum, m + 1)
                if part in (2, 5):
                    dve.wait_ge(sem("gate_in"), 16 * GATE_NO[layer, part])
                    to = gate[:, bass.ds(n * NCOL, NCOL)]
                    nc.vector.scalar_tensor_tensor(to, ada_p[:, :], 1.0, to, ALU.add, ALU.add).then_inc(a_out, 1)
                else:
                    at = bass.ds(n * 4 + (96 * layer + KT * part), 4)
                    nc.vector.scalar_tensor_tensor(mod[:, at], ada_p[:, 0:4], 1.0 if part in (1, 4) else 0.0,
                                                   cols[:, at], ALU.add, ALU.add).then_inc(a_out, 1)

            mixed = {0: 0, 1: 0}

            def mix_rows(layer, n):
                for r in range(mixed[layer], mixed[layer] + n):
                    k, row = divmod(r, KT)
                    ada_rows(dve, nc.vector, mix_accs[layer][k], MIX_FIRST[layer] + k, row, row + 1)
                mixed[layer] += n

            def ada_evac_mix(layer):
                dve.wait_ge(a_sum, MIX_FIRST[layer] + len(MIX[layer]))
                for part in sorted({b[1] for b in MIX[layer]}):
                    mine = [k for k, b in enumerate(MIX[layer]) if b[1] == part]
                    to = 96 * layer + KT * part + 4 * MIX[layer][mine[0]][2]
                    at, n = slice(to, to + 4 * len(mine)), 4 * mine[0]
                    ins = nc.vector.scalar_tensor_tensor(
                        mod[:, at], (ada_p if layer == 0 else T[0])[:, n:n + 4 * len(mine)],
                        1.0 if part in (1, 4) else 0.0, cols[:, at], ALU.add, ALU.add)
                ins.then_inc(a_out, len(MIX[layer]))

            def steps(key, lo, hi, mid=None, tail=None, more=True, norm=None):
                ph = PH[key]
                now = {4: (4, 4, 0, 0), 6: (2, 2, 2, 2, 0, 0)}[ph["n"]]

                def body(c0, i):
                    beside = ada_of(key, lo, c0, i)
                    own = 2 if key[1] == "up_b" and c0 == 11 else ph["n"]
                    for j in range(2, own + 2):
                        if j < own or more or c0 != hi - 1:
                            lo_unit(ph, c0, i, j, ph["kts"][j] * NCOL if j < own else UNIT)
                        if j == 2 and mid:
                            mid(c0, i)
                        if norm is not None and c0 == lo and i == 0:
                            ln_affine(norm, j - 2)
                        if beside:
                            blk, row = beside
                            row += sum(now[:j - 2])
                            ada_rows(dve, nc.vector, ada_acc, blk[3], row, row + now[j - 2])
                    if tail:
                        tail(c0, i)
                    if beside and beside[1]:
                        ada_evac(beside[0])
                if hi - lo == 1 or not more:
                    for c in range(lo, hi):
                        body(c, 0)
                elif norm is not None:
                    for c in range(lo, hi):
                        body(lo + (c - lo) % 2, (c - lo) // 2)
                else:
                    pairs(dve, lo, hi, body)

            def u_lo(g, dst_kt, slot):
                dve.wait_ge(u_hi_done, g + 1)
                nc.vector.tensor_tensor(ulo[:, dst_kt, :], u32[:, slot, :].rearrange("p (k s) -> p k s", k=2),
                                        uhi[:, dst_kt, :].bitcast(f32), ALU.subtract).then_inc(u_ready, 1)

            def y_out(key, first, stats):
                ph = PH[key]

                def tail(c0, i):
                    y = Y0[key] + c0 + 2 * i
                    cs = bass.ds(2 * NCOL * i + c0 * NCOL, NCOL)
                    dve.wait_ge(w_used, unit_no(ph, c0, i, ph["n"])[1])
                    for t in range(NT):
                        ins = nc.vector.tensor_tensor(y_tmp[:, t, :], bank[2 * (c0 % 2) + t][:, :], gate[:, cs],
                                                      ALU.mult)
                    ins.then_inc(acc_free, 1)
                    dve.wait_ge(acc_free, ph["chunk"] + c0 + 2 * i + 3)
                    for t in range(NT):
                        ins = nc.vector.scalar_tensor_tensor(x[:, t, cs], x[:, t, cs], ALPHA if first else 1.0,
                                                             y_tmp[:, t, :], ALU.mult, ALU.add)
                    ins.then_inc(y_sum, 1)
                    dve.wait_ge(y_sum, y + 1)
                    if stats:
                        for t in range(NT):
                            ins = nc.vector.bn_stats(bn[:, t, bass.ds(c0 + 2 * i, 1), :].rearrange("p a s -> p (a s)"),
                                                     x[:, t, cs])
                        ins.then_inc(y_done, 1)
                    else:
                        nc.vector.memset(t1[:, 0:1], 0.0).then_inc(y_done, 1)
                return tail

            def rstd(v, sdv, r, t, var_sem, sd_sem, n):
                dve.wait_ge(sem(sd_sem), n)
                link(nc.vector.reciprocal(r, sdv))
                link(nc.vector.tensor_tensor(t, r, r, ALU.mult))
                link(nc.vector.tensor_tensor(t, t, v, ALU.mult))
                link(nc.vector.tensor_scalar(t, t, -0.5, 1.5, ALU.mult, ALU.add))
                link(nc.vector.tensor_tensor(r, r, t, ALU.mult))

            def layer_norm(s, last):
                dve.wait_ge(y_done, {0: 4, 1: 12, 2: 16, 3: 24}[s])
                for t in range(NT):
                    ins = nc.vector.bn_aggr(mv[:, t, :], bn[:, t].rearrange("p c s -> p (c s)"))
                link(ins)
                nc.vector.tensor_scalar(var, mv[:, :, 1], EPS, None, ALU.add).then_inc(sem("ln_var"), 1)
                if not last:
                    at = (48, 96, 144)[s]
                    scale = mod[:, at + KT:at + 2 * KT]
                    g, b = (cols[:, c + s * KT:c + (s + 1) * KT] for c in (C_LNG, C_LNB))
                    nc.vector.tensor_tensor(ln_cols[:, 0, :], g, scale, ALU.mult)
                    link(nc.vector.tensor_tensor(ln_cols[:, 1, :], b, scale, ALU.mult))
                    nc.vector.tensor_tensor(ln_cols[:, 1, :], ln_cols[:, 1, :], mod[:, at:at + KT], ALU.add)
                dve.wait_ge(sem("ln_var"), s + 1)
                rstd(var, sd, rs, t1, "ln_var", "ln_sd", s + 1)
                if last:
                    dve.wait_ge(sem("ln_in"), 32 * (s + 1))
                    for n in range(4):
                        cs = slice(n * NCOL, (n + 1) * NCOL)
                        for t in range(NT):
                            ins = nc.vector.scalar_tensor_tensor(x[:, t, cs], x[:, t, cs], mv[:, t, 0:1],
                                                                 lnp[:, 0, cs], ALU.subtract, ALU.mult)
                        link(ins)
                        for t in range(NT):
                            ins = nc.vector.scalar_tensor_tensor(x[:, t, cs], x[:, t, cs], rs[:, t:t + 1],
                                                                 lnp[:, 1, cs], ALU.mult, ALU.add)
                        ins.then_inc(sem("ln_affine"), 1)
                    return
                for n in range(4):
                    cs = slice(n * NCOL, (n + 1) * NCOL)
                    for t in range(NT):
                        ins = nc.vector.tensor_scalar(x[:, t, cs], x[:, t, cs], mv[:, t, 0:1], rs[:, t:t + 1],
                                                      ALU.subtract, ALU.mult)
                    ins.then_inc(sem("ln_chunk"), 1)
                for v in range(8):
                    u_lo(U_LN[s] + v, slice(2 * v, 2 * v + 2), v % 2)

            def ln_affine(s, n):
                if n == 0:
                    dve.wait_ge(sem("ln_in"), 32 * (s + 1))
                dve.wait_ge(sem("ln_chunk"), 4 * s + 4)
                dve.wait_ge(t_full, T_LN[s] + 2 * n + 2)
                cs = slice(n * NCOL, (n + 1) * NCOL)
                for t in range(NT):
                    ins = nc.vector.tensor_tensor(x[:, t, cs], x[:, t, cs], lnp[:, 0, cs], ALU.mult)
                link(ins)
                for t in range(NT):
                    ins = nc.vector.tensor_tensor(x[:, t, cs], x[:, t, cs], lnp[:, 1, cs], ALU.add)
                ins.then_inc(sem("ln_affine"), 1)

            def hidden(layer, name, c0, i, nf=2):
                q = H_LAYER * layer + H0[name] + c0 + 2 * i
                f = (0 if name == "up_a" else FT_A) + 2 * c0 + 4 * i
                col = C_CONV + layer * 4 * FT + f
                dve.wait_ge(h_bias, q + 1)
                for tap, lag, s in ((1, 1, h_tap), (0, 2, h_conv)):
                    for k in range(nf):
                        ins = nc.vector.scalar_tensor_tensor(
                            gc[:, k, lag:S], T[1][:, k * S:(k + 1) * S - lag],
                            cols[:, bass.ds(col + tap * FT + k, 1)], gc[:, k, lag:S], ALU.mult, ALU.add)
                    ins.then_inc(s, 1)
                    if tap:
                        dve.wait_ge(h_tap, q + 1)
                dve.wait_ge(h_gelu, q + 1)
                nc.vector.tensor_tensor(h32[:, 0:nf, :], T[0][:, 0:nf * S].rearrange("p (k s) -> p k s", k=nf),
                                        gc[:, 0:nf, :], ALU.mult).then_inc(h_mul, 1)
                dve.wait_ge(h_hi, q + 1)
                at = bass.ds(2 * c0 + 4 * i, nf)
                nc.vector.tensor_tensor(hlo[:, at, :], h32[:, 0:nf, :], hhi[:, at, :].bitcast(f32), ALU.subtract
                                        ).then_inc(h_lo, 1)

            def mlp(layer):
                for name in ("up_a", "up_b"):
                    key = (layer, name)
                    last = PH[key]["chunks"] - 1
                    prev = lambda c0, i: hidden(layer, name, c0 - 1, i)
                    steps(key, 0, 1, norm=2 * layer if name == "up_a" else None)
                    steps(key, 1, 9, mid=prev)
                    if name == "up_b":
                        steps(key, 9, 11, mid=prev)
                        hidden(layer, name, last - 1, 0)
                        lo_unit(PH[key], last, 0, 2, UNIT)
                        lo_unit(PH[key], last, 0, 3, UNIT)
                    else:
                        steps(key, last, last + 1, mid=prev)
                    hidden(layer, name, last, 0, 1 if name == "up_b" else 2)
                    down = (layer, "down" + name[2:])
                    steps(down, 0, 4, tail=y_out(down, name == "up_a", name == "up_b"),
                          more=not (layer == DEPTH - 1 and name == "up_b"))

            nc.vector.memset(t1[:, 0:1], 0.0).then_inc(w_lo, RAW_SLOTS)
            nc.vector.memset(t1[:, 1:2], 0.0).then_inc(a_step, A0)
            nc.vector.memset(var[:, 0:1], 0.0).then_inc(a_out, 1)
            nc.vector.memset(var[:, 1:2], 0.0).then_inc(u_ready, 2)
            nc.vector.memset(sd[:, 0:1], 0.0).then_inc(t_free, 2)
            nc.vector.memset(sd[:, 1:2], 0.0).then_inc(acc_free, 2)
            nc.vector.memset(rs[:, 0:1], 0.0).then_inc(h_mul, 1)
            def start_acc(b):
                return acc_start if b % 2 else ada_acc

            dve.wait_ge(sem("silu_c"), 1)
            ada_rows(dve, nc.vector, ada_acc, 0, 0, KT)
            dve.wait_ge(sem("rows_T"), 1)
            nc.vector.tensor_copy(cols[:, 0:2 * 96 + 4 * FT], bank[0][:, 0:2 * 96 + 4 * FT]).then_inc(sem("cols_in"), 1)
            nc.vector.tensor_copy(cols[:, 2 * 96 + 4 * FT:n_cols], bank[1][:, 0:n_cols - 2 * 96 - 4 * FT]
                                  ).then_inc(sem("cols_in"), 1)
            dve.wait_ge(sem("cols_in"), 2)
            for b in range(1, 10):
                if b < 8:
                    ada_rows(dve, nc.vector, start_acc(b), b, 0, KT)
                if b <= 8:
                    ada_evac((0, (b - 1) % 2, (b - 1) // 2, b - 1))
                if b >= 3 and b % 2:
                    for v in (b - 3, b - 2):
                        u_lo(v, slice(2 * v, 2 * v + 2), v % 2)
                    for v in (b - 3, b - 2):
                        lo_unit(PH[0, "in"], 0, 0, v, UNIT)
            lo_unit(PH[0, "in"], 2, 0, 0, UNIT)
            lo_unit(PH[0, "in"], 2, 0, 1, UNIT)
            steps((0, "in"), 2, 4)
            steps((0, "in"), 4, 8)

            dve.wait_ge(sem("lr_hi"), 1)
            nc.vector.tensor_tensor(w_lrl[:, :, :], w_lr[:, :, :], w_lrh[:, :, :].bitcast(f32), ALU.subtract
                                    ).then_inc(sem("lr_lo"), 1)
            ada_rows(dve, nc.vector, ada_acc, GLA_FIRST[3], 0, KT)
            mix_rows(0, 8)
            dve.wait_ge(sem("lr"), 1)
            nc.vector.tensor_copy(lr[:, :, :], bank[7][:, 0:NT * GRANK].rearrange("p (t r) -> p t r", t=NT)
                                  ).then_inc(sem("lr_out"), 1)
            ada_evac(GLA_FIRST)
            mix_rows(0, 8)
            dve.wait_ge(sem("lr_T"), 1)
            nc.vector.tensor_copy(lrT[:, :], bank[7][0:GRANK, 0:S]).then_inc(sem("lr_T_out"), 1)
            mix_rows(0, 6)

            def mix_lo(v):
                u_lo(U_MIX + v, slice(2 * v, 2 * v + 2), v % 2)
            mix_lo(0)
            mix_lo(1)
            mix_rows(0, 6)
            dve.wait_ge(sem("gate_pre"), 1)
            dve.wait_ge(sem("gla_in"), 32)
            for t in range(NT):
                ins = nc.vector.tensor_tensor(loga[:, t, :], bank[6 + t][:, :], b_g[:, :], ALU.add)
            ins.then_inc(sem("gate_pre_out"), 1)
            mix_rows(0, 4)
            mix_lo(2)
            mix_lo(3)
            dve.wait_ge(t_full, T_MIX + 4)
            mix_rows(0, 8)
            dve.wait_ge(sem("gate_pre_out"), 1)
            dve.wait_ge(sem("ls"), 3)
            nc.vector.scalar_tensor_tensor(loga[:, :, :].rearrange("p t c -> p (t c)"),
                                           loga[:, :, :].rearrange("p t c -> p (t c)"), 0.0,
                                           kdec[:, :, :].rearrange("p t c -> p (t c)"), ALU.min, ALU.subtract
                                           ).then_inc(sem("log_a"), 1)
            nc.vector.memset(scT[:, :, :, :], 0.0).then_inc(sem("sc_zero"), 1)
            mix_rows(0, 12)
            dve.wait_ge(sem("exp_suf"), 2)
            nc.vector.tensor_tensor(kdec[:, :, :], kdec[:, :, :], z[:, :, OFF_K:OFF_V], ALU.mult).then_inc(sem("kdec"), 1)
            mix_rows(0, 4)
            dve.wait_ge(sem("qk_T_out"), 1)
            dve.wait_ge(sem("exp_b"), 4)
            for j in range(2):
                hs = slice(2 * j, 2 * j + 2)
                e_b = bank[2 + j].rearrange("p (h s) -> p h s", h=2)
                nc.vector.tensor_copy(decay[:, hs, :], e_b[:, :, CH - 1::CH])
                nc.vector.tensor_tensor(qdT[:, hs, :], qdT[:, hs, :], e_b, ALU.mult)
                ins = nc.vector.tensor_tensor(kiT[:, hs, :], kiT[:, hs, :], bank[j].rearrange("p (h s) -> p h s", h=2),
                                              ALU.mult)
            ins.then_inc(sem("qk_dec"), 1)
            mix_rows(0, 8)
            dve.wait_ge(sem("qk_dec"), 1)
            dve.wait_ge(sem("scores"), 1)
            dve.wait_ge(sem("sc_zero"), 1)
            for t in range(NT):
                for h in range(GH):
                    ins = nc.vector.copy_predicated(scT[:, t, h, :], sum_inc.bitcast(i32),
                                                    bank[6 + t][:, h * P:(h + 1) * P])
            ins.then_inc(sem("scores_out"), 1)
            mix_rows(0, 10)
            dve.wait_ge(sem("outer"), 1)
            for j in range(2):
                ins = nc.vector.tensor_copy(state[:, 0, 2 * j:2 * j + 2, :],
                                            bank[j].rearrange("p (h v) -> p h v", h=2))
            link(ins)
            for c in (1, 2):
                for h in range(GH):
                    to = state[:, 1, h, :] if c == 1 else state3[:, h, :]
                    ins = nc.vector.scalar_tensor_tensor(to, state[:, c - 1, h, :], decay[:, h, c:c + 1],
                                                         bank[2 * c + h // 2][:, (h % 2) * GDV:(h % 2 + 1) * GDV],
                                                         ALU.mult, ALU.add)
                if c == 1:
                    link(ins)
            ins.then_inc(sem("states"), 1)
            mix_rows(0, 10)
            dve.wait_ge(sem("gla_o"), 1)
            for q in range(8):
                t, h = divmod(q, GH)
                ins = nc.vector.bn_stats(gbn[:, q, :], bank[4 + 2 * t + h // 2][:, (h % 2) * GDV:(h % 2 + 1) * GDV])
            link(ins)
            for q in range(8):
                ins = nc.vector.bn_aggr(gmv[:, q, :], gbn[:, q, :])
            link(ins)
            nc.vector.tensor_scalar(gvar, gmv[:, :, 1], EPS, None, ALU.add).then_inc(sem("gla_var"), 1)
            dve.wait_ge(sem("gla_var"), 1)
            rstd(gvar, gsd, grs, gt, "gla_var", "gla_sd", 1)
            dve.wait_ge(sem("silu_r"), 2)
            for q in range(8):
                t, h = divmod(q, GH)
                ins = nc.vector.scalar_tensor_tensor(
                    z[:, t, OFF_Q + h * GDV:OFF_Q + (h + 1) * GDV], bank[4 + 2 * t + h // 2][:, (h % 2) * GDV:(h % 2 + 1) * GDV],
                    gmv[:, q, 0:1], z[:, t, OFF_R + h * GDV:OFF_R + (h + 1) * GDV], ALU.subtract, ALU.mult)
            link(ins)
            for h in range(GH):
                for t in range(NT):
                    o = z[:, t, OFF_Q + h * GDV:OFF_Q + (h + 1) * GDV]
                    ins = nc.vector.tensor_scalar(o, o, grs[:, t * GH + h:t * GH + h + 1], None, ALU.mult)
                ins.then_inc(sem("y_b"), 1)
            dve.wait_ge(sem("y_b"), 4)
            for v in range(4, 8):
                mix_rows(0, 3)
                mix_lo(v)
            ada_evac_mix(0)
            steps((0, "out"), 0, 4, tail=y_out((0, "out"), True, True))
            layer_norm(0, False)
            mlp(0)
            layer_norm(1, False)
            steps((1, "qkv"), 0, 4, norm=1)
            steps((1, "qkv"), 4, 8)
            steps((1, "qkv"), 8, 12)
            for s in range(1, AH + 3):
                if s <= AH:
                    h = s - 1
                    dve.wait_ge(sem("att_s"), h + 1)
                    sb = bank[6 + h % 2]
                    nc.vector.reduce_max(nmax[:, h % 2, 0:1], sb[:, 0:P], AX.X, negate=True)
                    nc.vector.reduce_max(nmax[:, h % 2, 1:2], sb[:, P:3 * P], AX.X, negate=True
                                         ).then_inc(sem("att_max"), 1)
                if 2 <= s <= AH + 1:
                    h = s - 2
                    dve.wait_ge(sem("att_pT"), h + 1)
                    nc.vector.tensor_copy(probT[:, h % 2, :], bank[h % 2][:, 0:3 * P]).then_inc(sem("att_pT_out"), 1)
                if s <= AH:
                    h = s - 1
                    mix_rows(1, 1)
                    dve.wait_ge(sem("att_exp"), h + 1)
                    nc.vector.reciprocal(rinv[:, h % 2, :], rsum[:, h % 2, :]).then_inc(sem("att_rinv"), 1)
                    mix_rows(1, len(MIX[1]) * KT // AH - 1)
                if s == AH + 1:
                    ada_evac_mix(1)
                if s >= 3:
                    h = s - 3
                    dve.wait_ge(u_hi_done, U_ATT + h + 1)
                    nc.vector.tensor_tensor(ulo[:, h, :], bank[2 + h % 2][:, 0:S], uhi[:, h, :].bitcast(f32),
                                            ALU.subtract).then_inc(u_ready, 1)
            steps((1, "o"), 0, 4, tail=y_out((1, "o"), True, True))
            layer_norm(2, False)
            mlp(1)
            layer_norm(3, True)

        @block.tensor
        def _(pe):
            def unit(ph, c0, i, j, parts, u_of, first, last, banks, after=None, late=None):
                u, un = unit_no(ph, c0, i, j)
                pe.wait_ge(w_hi, un + 1)
                if after is not None:
                    pe.wait_ge(u_ready, after)
                h, l = u_of
                width = UNIT // (8 if len(parts) == 8 else 4)
                slot = u % HL_SLOTS
                for n, (k, kt) in enumerate(parts):
                    if late is not None and kt == late[0]:
                        pe.wait_ge(h_lo, late[1])
                    w = whi[:, slot, k * width:(k + 1) * width]
                    for t in range(NT):
                        nc.tensor.matmul(banks[t][:, 0:width], h[:, kt, t * P:(t + 1) * P], w,
                                         start=first and n == 0, stop=False)
                        ins = nc.tensor.matmul(banks[t][:, 0:width], l[:, kt, t * P:(t + 1) * P], w,
                                               start=False, stop=False)
                ins.then_inc(wh_used, 1)
                pe.wait_ge(w_lo, un + (RAW_SLOTS + 1))
                for n, (k, kt) in enumerate(parts):
                    w = wlo[:, slot, k * width:(k + 1) * width]
                    for t in range(NT):
                        ins = nc.tensor.matmul(banks[t][:, 0:width], h[:, kt, t * P:(t + 1) * P], w,
                                               start=False, stop=last and n == len(parts) - 1)
                ins.then_inc(w_used, 1)

            def ada_sum_mix(layer):
                m = MIX_FIRST[layer]
                pe.wait_ge(a_step, (m + len(MIX[layer])) * KT + A0)
                pe.wait_ge(a_out, m + 1)
                to = ada_p if layer == 0 else T[0]
                for n, acc in enumerate(mix_accs[layer]):
                    for q in range(4):
                        ins = nc.tensor.matmul(to[:, 4 * n + q:4 * n + q + 1], acc[:, q * P:(q + 1) * P],
                                               ones[:, 0:1], start=True, stop=True)
                ins.then_inc(a_sum, len(MIX[layer]))

            def ada_sum(blk, acc=ada_acc):
                layer, part, n, m = blk
                pe.wait_ge(a_step, m * KT + (A0 + KT))
                pe.wait_ge(a_out, m + 1)
                if part in (2, 5):
                    ins = nc.tensor.matmul(ada_p[:, :], ones, acc[:, :], start=True, stop=True)
                else:
                    for q in range(4):
                        ins = nc.tensor.matmul(ada_p[:, q:q + 1], acc[:, q * P:(q + 1) * P], ones[:, 0:1],
                                               start=True, stop=True)
                ins.then_inc(a_sum, 1)

            def chunks(key, lo, hi, u_of=(uhi, ulo), u_from=None, mid=None, late=None, before=None):
                ph = PH[key]
                start = [sum(ph["kts"][:j]) for j in range(ph["n"])]

                def body(c0, i):
                    small = key[1] == "up_b" and c0 == 11
                    n = 2 if small else ph["n"]
                    pe.wait_ge(acc_free, ph["chunk"] + c0 + 2 * i + 1)
                    banks = bank[2 * (c0 % 2):2 * (c0 % 2) + 2]
                    for j in range(n):
                        if before and j in before and c0 == lo and i == 0:
                            before[j]()
                        k0, kn = (8 * j, 8) if small else (start[j], ph["kts"][j])
                        unit(ph, c0, i, j, [(k, k0 + k) for k in range(kn)], u_of, j == 0, j == n - 1, banks,
                             None if u_from is None else u_from + (k0 + kn) // 2, late)
                        if j == 0 and mid:
                            mid(c0, i)
                    beside = ada_of(key, lo, c0, i)
                    if beside and beside[1]:
                        ada_sum(beside[0])
                if hi - lo == 1:
                    body(lo, 0)
                elif before:
                    for c in range(lo, hi):
                        body(lo + (c - lo) % 2, (c - lo) // 2)
                else:
                    pairs(pe, lo, hi, body)

            def hidden_T(layer, name, c0, i, nf=2):
                q = H_LAYER * layer + H0[name] + c0 + 2 * i
                pe.wait_ge(acc_free, PH[layer, name]["chunk"] + c0 + 2 * i + 3)
                pe.wait_ge(h_mul, q + 1)
                for s in range(2):
                    for k in range(nf):
                        for t in range(NT):
                            ins = nc.tensor.transpose(T[s][:, k * S + t * P:k * S + (t + 1) * P],
                                                      g_tok[:, t, (s * nf + k) * P:(s * nf + k + 1) * P], ident)
                ins.then_inc(h_T, 1)

            def mlp(layer, u_from):
                for name in ("up_a", "up_b"):
                    key = (layer, name)
                    last = PH[key]["chunks"] - 1
                    prev = lambda c0, i: hidden_T(layer, name, c0 - 1, i)
                    chunks(key, 0, 1, u_from=u_from,
                           before={1: lambda: ln_T(2 * layer, range(4, 8))} if name == "up_a" else None)
                    chunks(key, 1, 9, mid=prev)
                    if name == "up_b":
                        chunks(key, 9, 11, mid=prev)
                    chunks(key, last, last + 1, mid=prev)
                    hidden_T(layer, name, last, 0, 1 if name == "up_b" else 2)
                    done = H_LAYER * layer + H0[name] + last + 1
                    pe.wait_ge(h_lo, done - 1)
                    kt = 2 * last
                    chunks((layer, "down" + name[2:]), 0, 4, u_of=(hhi, hlo), late=(kt, done))
                    u_from = None

            def channels_T(src, base, v):
                pe.wait_ge(t_free, base + v + 1)
                for k in range(2):
                    for t in range(NT):
                        ins = nc.tensor.transpose(T[v % 2][:, k * S + t * P:k * S + (t + 1) * P], src(t, 2 * v + k), ident)
                ins.then_inc(t_full, 1)

            sizes = [96] * 2 + [FT] * 8 + [8, 8, 64, 64, KT]
            pe.wait_ge(sem("const_in"), 16)
            pe.wait_ge(sem("c_in"), 16)
            nc.tensor.transpose(bank[2][:, 0:KT], rows[0:KT, ROW_SRC - 1, :], ident[0:KT, 0:KT]
                                ).then_inc(sem("c_T"), 1)
            pe.wait_ge(sem("rows_in"), 16 * ROW_DMAS)
            at = 0
            for i, size in enumerate(sizes[:-1]):
                if i == 6:
                    at = 0
                to = bank[0 if i < 6 else 1]
                ins = nc.tensor.transpose(to[:, at:at + size], rows[0:size, i, :], ident[0:size, 0:size])
                at += size
            ins.then_inc(sem("rows_T"), 1)
            ada_sum((0, 0, 0, 0))
            pe.wait_ge(sem("x_in"), 16)
            for v in range(8):
                channels_T(lambda t, k: x[:, t, k * P:(k + 1) * P], T_X, v)
            pe.wait_ge(sem("cols_in"), 2)
            for b in range(1, 10):
                if b < 8:
                    ada_sum((0, b % 2, b // 2, b), acc_start if b % 2 else ada_acc)
                if b >= 3 and b % 2:
                    g = (b - 3) // 2
                    for c in range(2):
                        unit(PH[0, "in"], 0, 0, 2 * g + c, [(k, 4 * g + k) for k in range(4)], (uhi, ulo), g == 0,
                             g == 3, bank[2 * c:2 * c + 2], 2 + U_FIRST + 2 * g + 2)
            chunks((0, "in"), 2, 4)
            chunks((0, "in"), 4, 8)

            pe.wait_ge(sem("lr_lo"), 1)
            for t in range(NT):
                for kt in range(KT):
                    uh, ul = uhi[:, kt, t * P:(t + 1) * P], ulo[:, kt, t * P:(t + 1) * P]
                    to = bank[7][:, t * GRANK:(t + 1) * GRANK]
                    nc.tensor.matmul(to, uh, w_lrh[:, kt, :], start=kt == 0, stop=False)
                    nc.tensor.matmul(to, uh, w_lrl[:, kt, :], start=False, stop=False)
                    ins = nc.tensor.matmul(to, ul, w_lrh[:, kt, :], start=False, stop=kt == KT - 1)
            ins.then_inc(sem("lr"), 1)
            ada_sum(GLA_FIRST)
            pe.wait_ge(acc_free, 2 + 8)
            pe.wait_ge(sem("pool_in"), 16 * 5)

            def pool_mean(g):
                for k in range(2):
                    col = (2 * g + k) * P
                    nc.tensor.matmul(bank[g][:, k * S:(k + 1) * S], z[:, 0, col:col + P], band[:, g, 0:S],
                                     start=True, stop=False)
                    ins = nc.tensor.matmul(bank[g][:, k * S + P:(k + 1) * S], z[:, 1, col:col + P], band[:, g, S:S + P],
                                           start=False, stop=True)
                ins.then_inc(sem("pool_T"), 1)

            def pool_map(g):
                pe.wait_ge(t_free, T_MIX + g + 1)
                pe.wait_ge(sem("pool_T_out"), g + 1)
                for d in range(2):
                    for k in range(2):
                        ins = nc.tensor.matmul(T[g % 2][:, d * S:(d + 1) * S], w_pool[:, g, k, d * P:(d + 1) * P],
                                               dT[:, g % 2, k, :], start=k == 0, stop=k == 1)
                ins.then_inc(t_full, 1)
            pool_mean(0)
            pool_mean(1)
            pool_mean(2)
            pool_mean(3)
            pe.wait_ge(sem("lr_out"), 1)
            for t in range(NT):
                ins = nc.tensor.transpose(bank[7][0:GRANK, t * P:(t + 1) * P], lr[:, t, :], ident)
            ins.then_inc(sem("lr_T"), 1)
            pool_map(0)
            pe.wait_ge(sem("lr_T_out"), 1)
            pe.wait_ge(sem("gla_in"), 32)
            pe.wait_ge(a_out, MIX_FIRST[0] + 1)
            for t in range(NT):
                ins = nc.tensor.matmul(bank[6 + t][:, :], lrT[:, t * P:(t + 1) * P], w_g[:, :], start=True, stop=True)
            ins.then_inc(sem("gate_pre"), 1)
            for g in range(1, 4):
                pool_map(g)
            for j, off in ((0, OFF_Q), (2, OFF_K)):
                for h in range(GH):
                    for t in range(NT):
                        ins = nc.tensor.transpose(bank[j + h // 2][:, (h % 2) * S + t * P:(h % 2) * S + (t + 1) * P],
                                                  z[:, t, off + h * GDK:off + (h + 1) * GDK], ident)
            ins.then_inc(sem("qk_T"), 1)
            pe.wait_ge(sem("log_a"), 1)
            pe.wait_ge(sem("qk_T_out"), 1)
            for t in range(NT):
                nc.tensor.matmul(bank[t][:, :], sum_suf, loga[:, t, :], start=True, stop=True)
            for h in range(GH):
                for t in range(NT):
                    ins = nc.tensor.matmul(bank[2 + h // 2][:, (h % 2) * S + t * P:(h % 2) * S + (t + 1) * P],
                                           loga[:, t, h * GDK:(h + 1) * GDK], sum_inc, start=True, stop=True)
            ins.then_inc(sem("cum"), 1)
            pe.wait_ge(sem("qk_dec"), 1)
            for t in range(NT):
                for h in range(GH):
                    ins = nc.tensor.matmul(bank[6 + t][:, h * P:(h + 1) * P], kiT[:, h, t * P:(t + 1) * P],
                                           qdT[:, h, t * P:(t + 1) * P], start=True, stop=True)
            ins.then_inc(sem("scores"), 1)
            pe.wait_ge(sem("kdec"), 1)
            pe.wait_ge(t_free, 2 + T_MIX + 4)
            for c in range(3):
                t, r = c // 2, slice(c % 2 * CH, (c % 2 + 1) * CH)
                for h in range(GH):
                    ins = nc.tensor.matmul(bank[2 * c + h // 2][:, (h % 2) * GDV:(h % 2 + 1) * GDV],
                                           kdec[r, t, h * GDK:(h + 1) * GDK],
                                           z[r, t, OFF_V + h * GDV:OFF_V + (h + 1) * GDV], start=True, stop=True)
            ins.then_inc(sem("outer"), 1)
            pe.wait_ge(sem("scores_out"), 1)
            pe.wait_ge(sem("states"), 1)
            for t in range(NT):
                for h in range(GH):
                    to = bank[4 + 2 * t + h // 2][:, (h % 2) * GDV:(h % 2 + 1) * GDV]
                    ins = nc.tensor.matmul(to, scT[:, t, h, :], z[:, t, OFF_V + h * GDV:OFF_V + (h + 1) * GDV],
                                           start=True, stop=False, skip_group_check=True)
                    for c in (2 * t, 2 * t + 1):
                        if c:
                            st = state[:, c - 1, h, :] if c < 3 else state3[:, h, :]
                            r = slice(c % 2 * CH, (c % 2 + 1) * CH)
                            ins = nc.tensor.matmul(to[r, :], qdT[:, h, c * CH:(c + 1) * CH], st, start=False,
                                                   stop=True, skip_group_check=True)
            ins.then_inc(sem("gla_o"), 1)
            def y_b_T():
                for v in range(4, 8):
                    pe.wait_ge(sem("y_b"), v - 3)
                    channels_T(lambda t, k: z[:, t, OFF_Q + (k - 8) * P:OFF_Q + (k - 7) * P], T_MIX, v)
                ada_sum_mix(0)
            chunks((0, "out"), 0, 4, u_from=2 + U_MIX, before={2: y_b_T})

            def ln_T(s, pieces):
                for v in pieces:
                    pe.wait_ge(sem("ln_chunk"), 4 * s + v // 2 + 1)
                    channels_T(lambda t, k: x[:, t, k * P:(k + 1) * P], T_LN[s], v)
            ln_T(0, range(4))
            mlp(0, 2 + U_LN[0])
            ln_T(1, range(4))
            chunks((1, "qkv"), 0, 4, u_from=2 + U_LN[1], before={1: lambda: ln_T(1, range(4, 8))})
            chunks((1, "qkv"), 4, 8)
            chunks((1, "qkv"), 8, 12)

            C_QKV = PH[1, "qkv"]["chunk"] + 12
            pe.wait_ge(acc_free, 2 + C_QKV)
            pe.wait_ge(t_free, 2 + T_LN[1] + 8)
            pe.wait_ge(a_out, MIX_FIRST[1] + 1)
            pe.wait_ge(sem("toep_in"), 16)
            for s in range(AH + 3):
                if s < AH:
                    if s >= 2:
                        pe.wait_ge(sem("att_qk"), s - 1)
                    for j in range(2):
                        for t in range(NT):
                            ins = nc.tensor.transpose(T[s % 2][:, j * S + t * P:j * S + (t + 1) * P],
                                                      qkv[:, t, j * D + s * AD:j * D + (s + 1) * AD], ident)
                    ins.then_inc(sem("att_T"), 1)
                if 1 <= s <= AH:
                    h = s - 1
                    pe.wait_ge(sem("att_qk"), h + 1)
                    if h >= 2:
                        pe.wait_ge(sem("att_exp"), h - 1)
                    sb, q, k = bank[6 + h % 2], qkT[:, h % 2, 0:S], qkT[:, h % 2, S:2 * S]
                    nc.tensor.matmul(sb[:, 0:P], q[:, 0:P], k[:, 0:P], start=True, stop=False)
                    nc.tensor.matmul(sb[:, 0:P], toep[:, h, 0:P], rev, start=False, stop=False)
                    nc.tensor.matmul(sb[:, 0:P], mask_q, mask_k, start=False, stop=True)
                    nc.tensor.matmul(sb[:, P:3 * P], q[:, P:S], k[:, 0:S], start=True, stop=False)
                    nc.tensor.matmul(sb[:, P:2 * P], toep[:, h, P:S], rev, start=False, stop=False)
                    nc.tensor.matmul(sb[:, 2 * P:3 * P], toep[:, h, 0:P], rev, start=False, stop=False)
                    nc.tensor.matmul(sb[:, 2 * P:3 * P], mask_q, mask_k, start=False, stop=True
                                     ).then_inc(sem("att_s"), 1)
                if 2 <= s <= AH + 1:
                    h = s - 2
                    pe.wait_ge(sem("att_p"), h + 1)
                    if h >= 2:
                        pe.wait_ge(sem("att_pT_out"), h - 1)
                    for j in range(3):
                        ins = nc.tensor.transpose(bank[h % 2][:, j * P:(j + 1) * P], prob[:, h % 2, j * P:(j + 1) * P], ident)
                    ins.then_inc(sem("att_pT"), 1)
                if s == AH + 1:
                    ada_sum_mix(1)
                if s >= 3:
                    h = s - 3
                    pe.wait_ge(sem("att_pT_out"), h + 1)
                    if h >= 2:
                        pe.wait_ge(u_ready, 2 + U_ATT + h - 1)
                    v0 = 2 * D + h * AD
                    nc.tensor.matmul(bank[2 + h % 2][:, 0:S], qkv[:, 0, v0:v0 + AD], probT[:, h % 2, 0:S],
                                     start=True, stop=False)
                    nc.tensor.matmul(bank[2 + h % 2][:, P:S], qkv[:, 1, v0:v0 + AD], probT[:, h % 2, 2 * P:3 * P],
                                     start=False, stop=True).then_inc(sem("att_o"), 1)
            pe.wait_ge(u_ready, 2 + U_ATT + AH)
            chunks((1, "o"), 0, 4)
            ln_T(2, range(4))
            mlp(1, 2 + U_LN[2])


_INS = ["x", "c", "w_ada", "b_ada", "ln_g", "ln_b", "w_in_ab", "w_gate_lr", "b_gate", "gla_norm_g", "w_pool",
        "pool_scale", "w_out_ab", "w_qkv", "rel_bias", "w_o", "w_up", "conv_w", "conv_b", "w_down"]


def constant_tables():
    import numpy as np
    j, i = np.arange(P)[:, None], np.arange(P)[None, :]
    same = j // CH == i // CH
    consts = np.zeros((P, CONST_COLS), np.float32)
    consts[:, 0:P] = j == i
    consts[:, P:2 * P] = j == P - 1 - i
    consts[:, 2 * P:3 * P] = (same & (j <= i)) / GTAU
    consts[:, 3 * P:4 * P] = (same & (j > i)) / GTAU
    consts[:, 4 * P:5 * P] = 1.0
    consts[0, 5 * P:5 * P + CH] = 1.0
    consts[0, 6 * P + CH:7 * P] = NEG
    band = np.zeros((P, 4, BAND), np.float32)
    src, dst = np.arange(S)[:, None], np.arange(S)[None, :]
    for g, w in enumerate(WINDOWS):
        m = ((src <= dst) & (src > dst - w)) / np.minimum(dst + 1, w) - (src == dst)
        band[:, g, 0:S] = m[0:P]
        band[:, g, S:] = m[P:, P:]
    return {"consts": consts, "band": band}


def kernel(**inputs):
    import numpy as np
    import concourse.bacc as bacc
    from concourse.bass_utils import run_bass_kernel_spmd as run

    nc = bacc.Bacc("TRN2", target_bir_lowering=False, num_devices=1, dynamic_dma_scratch_size=1024)
    arrays, args = {}, {}
    for name, a in [(n, inputs[n]) for n in _INS] + list(constant_tables().items()):
        a = np.ascontiguousarray(a)
        arrays[f"in_{name}"] = a
        args[name] = nc.dram_tensor(f"in_{name}", a.shape, mybir.dt.from_np(a.dtype), kind="ExternalInput").ap()
    out = nc.dram_tensor("out_x", (1, S, D), mybir.dt.float32, kind="ExternalOutput").ap()
    build(nc, args, out)
    r = run(nc, [arrays], core_ids=[0])
    return r.results[0]["out_x"]
```
